# Optimizing a Trainium2 kernel written in Bass

```python
import math
import jax, jax.numpy as jnp
from jax import lax
import numpy as np

D_MODEL = 1024
BATCH = 1
SEQ = 256
DEPTH = 2

GRID_W = 64
CTX_LEN = 256
EPS = 1e-6
N_MOD = 9
DN_HEADS = 4
DN_HEAD_DIM = 128
DN_WIDTH = DN_HEADS * DN_HEAD_DIM
CONV_WIDTH = 3
DN_CHUNK = 64
DIFF_HEADS = 4
DIFF_QK_DIM = 64
DIFF_V_DIM = 2 * DIFF_QK_DIM
DIFF_WIDTH = DIFF_HEADS * DIFF_V_DIM
Q_BLOCK = 128
ROPE_BASE = 10000.0
RET_HEADS = 8
RET_KEY_DIM = D_MODEL // RET_HEADS
RET_VALUE_DIM = 2 * RET_KEY_DIM
RET_V_WIDTH = RET_HEADS * RET_VALUE_DIM
RET_CHUNK = 64
D_FF = 2816
N_AB_LAYERS = (DEPTH + 1) // 2
N_RET_LAYERS = DEPTH // 2
AB_SIZES = [DN_WIDTH] * 4 + [2 * DN_HEADS] * 2 + [DIFF_WIDTH] * 3
AB_IN = sum(AB_SIZES)
RET_SIZES = [RET_HEADS * RET_KEY_DIM] * 2 + [RET_V_WIDTH] * 2
RET_IN = sum(RET_SIZES)

kernel_name = "hybrid_deltanet_diffattn_retention_macaron_dit"

F32 = jnp.float32

def rms_norm(x, w=None):
    xf = x.astype(F32)
    y = xf * lax.rsqrt(jnp.mean(xf * xf, axis=-1, keepdims=True) + EPS)
    if w is not None:
        y = y * w.astype(F32)
    return y.astype(x.dtype)

def l2norm(t):
    return t * lax.rsqrt(jnp.sum(t * t, axis=-1, keepdims=True) + EPS)

def split_cols(p, sizes):
    return jnp.split(p, [int(s) for s in np.cumsum(sizes)[:-1]], axis=-1)

def to_heads(t, n):
    B, L, _ = t.shape
    return t.reshape(B, L, n, -1).transpose(0, 2, 1, 3)

def ada_in(x, g, m, s):
    return rms_norm(x, g) * (1 + m[:, 3 * s + 1][:, None, :]) + m[:, 3 * s][:, None, :]

def ada_gate(m, s):
    return m[:, 3 * s + 2][:, None, :]

def swiglu(h, w_in, w_out):
    g, u = jnp.split(h @ w_in, 2, axis=-1)
    return (jax.nn.silu(g) * u) @ w_out

def rotate_half(x):
    x1, x2 = jnp.split(x, 2, axis=-1)
    return jnp.concatenate([-x2, x1], axis=-1)

def rope(x, ang):
    cos = jnp.concatenate([jnp.cos(ang)] * 2, axis=-1)
    sin = jnp.concatenate([jnp.sin(ang)] * 2, axis=-1)
    return x * cos + rotate_half(x) * sin

def axial_angles(L):
    rows = L // GRID_W
    r, cidx = jnp.meshgrid(jnp.arange(rows), jnp.arange(GRID_W), indexing='ij')
    axis_dim = DIFF_QK_DIM // 2
    inv = ROPE_BASE ** (-jnp.arange(0, axis_dim, 2, dtype=F32) / axis_dim)
    return (r.reshape(-1).astype(F32)[:, None] * inv, cidx.reshape(-1).astype(F32)[:, None] * inv)

def axial_rope(x, ang_r, ang_c):
    xr, xc = jnp.split(x, 2, axis=-1)
    return jnp.concatenate([rope(xr, ang_r), rope(xc, ang_c)], axis=-1)

def short_conv(u, w):
    k = w.shape[0]
    return lax.conv_general_dilated(u, w.astype(u.dtype)[:, None, :], window_strides=(1,),
                                    padding=[(k // 2, k // 2)],
                                    dimension_numbers=('NWC', 'WIO', 'NWC'),
                                    feature_group_count=u.shape[-1])

def two_pass(fn, ctx_seqs, lat_seqs, S0):
    outs_c, outs_l = [], []
    for d in range(2):
        f = (lambda t: jnp.flip(t, 2)) if d == 1 else (lambda t: t)
        oc, S = fn(d, [f(t) for t in ctx_seqs], S0)
        ol, _ = fn(d, [f(t) for t in lat_seqs], S)
        outs_c.append(f(oc))
        outs_l.append(f(ol))
    return outs_c[0] + outs_c[1], outs_l[0] + outs_l[1]

def gated_delta_chunked(q, k, v, log_a, beta, S0):
    B, H, L, _ = q.shape
    dv = v.shape[-1]
    C = DN_CHUNK
    n = L // C
    q, k, v = (t.reshape(B, H, n, C, t.shape[-1]) for t in (q, k, v))
    log_a, beta = (t.reshape(B, H, n, C) for t in (log_a, beta))
    g = jnp.cumsum(log_a, axis=-1)
    tril = jnp.tril(jnp.ones((C, C), bool))
    strict = jnp.tril(jnp.ones((C, C), bool), -1)
    gamma = jnp.exp(jnp.where(tril, g[..., :, None] - g[..., None, :], -jnp.inf))
    kb = k * beta[..., None]
    lower = jnp.where(strict, jnp.einsum('bhnid,bhnjd->bhnij', kb, k) * gamma, 0.0)
    tmat = lower + jnp.eye(C, dtype=lower.dtype)
    solve = lambda rhs: lax.linalg.triangular_solve(tmat, rhs, left_side=True, lower=True,
                                                    unit_diagonal=True)
    u = solve(v * beta[..., None])
    w = solve(kb * jnp.exp(g)[..., None])
    qk = jnp.einsum('bhnid,bhnjd->bhnij', q, k) * gamma

    def step(S, inp):
        q_i, k_i, u_i, w_i, g_i, qk_i = inp
        v_new = u_i - jnp.einsum('bhcd,bhde->bhce', w_i, S)
        o = (jnp.einsum('bhcd,bhde->bhce', q_i * jnp.exp(g_i)[..., None], S)
             + jnp.einsum('bhij,bhje->bhie', qk_i, v_new))
        g_last = g_i[..., -1:]
        S = (S * jnp.exp(g_last)[..., None]
             + jnp.einsum('bhcd,bhce->bhde', k_i * jnp.exp(g_last - g_i)[..., None], v_new))
        return S, o

    xs = tuple(jnp.moveaxis(t, 2, 0) for t in (q, k, u, w, g, qk))
    S, o = lax.scan(step, S0, xs)
    return jnp.moveaxis(o, 0, 2).reshape(B, H, L, dv), S

def retention_chunked(q, k, v, log_gamma, S0):
    B, H, L, _ = q.shape
    dv = v.shape[-1]
    C = RET_CHUNK
    n = L // C
    q, k, v = (t.reshape(B, H, n, C, t.shape[-1]) for t in (q, k, v))
    pos = jnp.arange(C, dtype=F32)
    lg = log_gamma[:, None]
    tril = jnp.tril(jnp.ones((C, C), bool))
    dec = jnp.exp(jnp.where(tril, (pos[:, None] - pos[None, :]) * lg[:, :, None], -jnp.inf))
    o_inner = jnp.einsum('bhnij,bhnje->bhnie',
                         jnp.einsum('bhnid,bhnjd->bhnij', q, k) * dec[:, None], v)
    q_dec = jnp.exp(lg * (pos + 1))[:, :, None]
    k_dec = jnp.exp(lg * (C - 1 - pos))[:, :, None]
    c_dec = jnp.exp(log_gamma * C)[:, None, None]

    def step(S, inp):
        q_i, k_i, v_i, o_i = inp
        o = o_i + jnp.einsum('bhcd,bhde->bhce', q_i, S) * q_dec
        S = S * c_dec + jnp.einsum('bhcd,bhce->bhde', k_i * k_dec, v_i)
        return S, o

    xs = tuple(jnp.moveaxis(t, 2, 0) for t in (q, k, v, o_inner))
    S, o = lax.scan(step, S0, xs)
    return jnp.moveaxis(o, 0, 2).reshape(B, H, L, dv), S

def diff_attend(q, k, v, lam_full):
    s = jnp.einsum('bhmqd,bhmkd->bhmqk', q, k) * DIFF_QK_DIM ** -0.5
    p = jax.nn.softmax(s, axis=-1)
    return jnp.einsum('bhqk,bhkd->bhqd', p[:, :, 0] - lam_full * p[:, :, 1], v)

def ab_mixer(hc, hl, w_in, conv_w, A_log, dt_bias, dn_norm_w, lam, subln_w, w_out,
             layer_idx, with_ctx_out):
    pc = split_cols(hc @ w_in, AB_SIZES)
    pl = split_cols(hl @ w_in, AB_SIZES)
    B, L, _ = hl.shape
    A_log = A_log.astype(F32)
    dt_bias = dt_bias.astype(F32)

    def dn_seqs(p):
        q, k, v, _, a, b = p[:6]
        qkv = jax.nn.silu(short_conv(jnp.concatenate([q, k, v], axis=-1), conv_w)).astype(F32)
        q, k, v = (to_heads(t, DN_HEADS) for t in jnp.split(qkv, 3, axis=-1))
        q = l2norm(q) * DN_HEAD_DIM ** -0.5
        k = l2norm(k)
        Bs, Ls, _ = a.shape
        a = a.astype(F32).reshape(Bs, Ls, 2, DN_HEADS)
        b = b.astype(F32).reshape(Bs, Ls, 2, DN_HEADS)
        log_a = (-jnp.exp(A_log) * jax.nn.softplus(a + dt_bias)).transpose(0, 3, 1, 2)
        beta = jax.nn.sigmoid(b).transpose(0, 3, 1, 2)
        return [q, k, v, log_a, beta]

    S0 = jnp.zeros((B, DN_HEADS, DN_HEAD_DIM, DN_HEAD_DIM), F32)
    dn_fn = lambda d, s, S: gated_delta_chunked(s[0], s[1], s[2], s[3][..., d], s[4][..., d], S)
    dn_c, dn_l = two_pass(dn_fn, dn_seqs(pc), dn_seqs(pl), S0)

    def dn_merge(o, z):
        Bs, H, Ls, dv = o.shape
        y = rms_norm(o.transpose(0, 2, 1, 3), dn_norm_w) * jax.nn.silu(z.astype(F32)).reshape(Bs, Ls, H, dv)
        return y.reshape(Bs, Ls, H * dv)

    lambda_init = 0.8 - 0.6 * math.exp(-0.3 * layer_idx)
    lamf = lam.astype(F32)
    lam_full = jnp.exp(jnp.sum(lamf[0] * lamf[1])) - jnp.exp(jnp.sum(lamf[2] * lamf[3])) + lambda_init

    def diff_qkv(p):
        q, k, v = p[6:]
        Bs, Ls, _ = q.shape
        q, k = (t.astype(F32).reshape(Bs, Ls, DIFF_HEADS, 2, DIFF_QK_DIM).transpose(0, 2, 3, 1, 4)
                for t in (q, k))
        return q, k, to_heads(v, DIFF_HEADS).astype(F32)

    def diff_merge(o):
        Bs, H, Ls, dv = o.shape
        return (rms_norm(o, subln_w) * (1 - lambda_init)).transpose(0, 2, 1, 3).reshape(Bs, Ls, H * dv)

    qc, kc, vc = diff_qkv(pc)
    ql, kl, vl = diff_qkv(pl)
    ang_r, ang_c = axial_angles(L)
    ql, kl = axial_rope(ql, ang_r, ang_c), axial_rope(kl, ang_r, ang_c)
    k_all = jnp.concatenate([kc, kl], axis=3)
    v_all = jnp.concatenate([vc, vl], axis=2)
    nb = L // Q_BLOCK
    qb = jnp.moveaxis(ql.reshape(B, DIFF_HEADS, 2, nb, Q_BLOCK, DIFF_QK_DIM), 3, 0)
    ol = lax.map(lambda qi: diff_attend(qi, k_all, v_all, lam_full), qb)
    ol = jnp.moveaxis(ol, 0, 2).reshape(B, DIFF_HEADS, L, DIFF_V_DIM)

    y_l = jnp.concatenate([dn_merge(dn_l, pl[3]), diff_merge(ol)], axis=-1).astype(hl.dtype) @ w_out
    if not with_ctx_out:
        return None, y_l
    oc = diff_attend(qc, kc, vc, lam_full)
    y_c = jnp.concatenate([dn_merge(dn_c, pc[3]), diff_merge(oc)], axis=-1).astype(hc.dtype) @ w_out
    return y_c, y_l

def ret_mixer(hc, hl, w_in, decay_logit, w_out, with_ctx_out):
    def stream(h, rotate):
        q, k, v, g = split_cols(h @ w_in, RET_SIZES)
        q, k, v = (to_heads(t, RET_HEADS).astype(F32) for t in (q, k, v))
        if rotate:
            inv = ROPE_BASE ** (-jnp.linspace(0.0, 1.0, RET_KEY_DIM // 2, dtype=F32))
            ang = jnp.arange(h.shape[1], dtype=F32)[:, None] * inv
            q, k = rope(q, ang), rope(k, ang)
        return [q, k * RET_KEY_DIM ** -0.5, v], g

    sc, gc = stream(hc, False)
    sl, gl = stream(hl, True)
    log_gamma = jax.nn.log_sigmoid(decay_logit.astype(F32))
    S0 = jnp.zeros((hl.shape[0], RET_HEADS, RET_KEY_DIM, RET_VALUE_DIM), F32)
    ret_fn = lambda d, s, S: retention_chunked(s[0], s[1], s[2], log_gamma[d], S)
    oc, ol = two_pass(ret_fn, sc, sl, S0)

    def merge(o, g, dtype):
        Bs, H, Ls, dv = o.shape
        y = rms_norm(o.transpose(0, 2, 1, 3)).reshape(Bs, Ls, H * dv) * jax.nn.silu(g.astype(F32))
        return y.astype(dtype) @ w_out

    y_l = merge(ol, gl, hl.dtype)
    if not with_ctx_out:
        return None, y_l
    return merge(oc, gc, hc.dtype), y_l

def setup_inputs(seed: int = 0) -> dict:
    key = jax.random.key(seed)
    ks = jax.random.split(key, 24)
    nrm = lambda k, shape, s: jax.random.normal(k, shape, F32) * s
    x = nrm(ks[0], (BATCH, SEQ, D_MODEL), 1.0)
    c = nrm(ks[1], (BATCH, D_MODEL), 1.0)
    ctx = nrm(ks[2], (BATCH, CTX_LEN, D_MODEL), 1.0)
    c_ctx = nrm(ks[3], (D_MODEL,), 1.0)
    ada_w = nrm(ks[4], (DEPTH, D_MODEL, N_MOD * D_MODEL), D_MODEL ** -0.5)
    ada_b = nrm(ks[5], (DEPTH, N_MOD * D_MODEL), 0.01)
    norm_w = 1.0 + nrm(ks[6], (DEPTH, 3, D_MODEL), 0.02)
    final_norm_w = 1.0 + nrm(ks[7], (D_MODEL,), 0.02)
    ffn_w_in = nrm(ks[8], (DEPTH, 2, D_MODEL, 2 * D_FF), D_MODEL ** -0.5)
    ffn_w_out = nrm(ks[9], (DEPTH, 2, D_FF, D_MODEL), D_FF ** -0.5)
    ab_w_in = nrm(ks[10], (N_AB_LAYERS, D_MODEL, AB_IN), D_MODEL ** -0.5)
    ab_conv_w = nrm(ks[11], (N_AB_LAYERS, CONV_WIDTH, 3 * DN_WIDTH), CONV_WIDTH ** -0.5)
    dn_A_log = jnp.log(jax.random.uniform(ks[12], (N_AB_LAYERS, 2, DN_HEADS), F32, 1.0, 16.0))
    dt = jnp.exp(jax.random.uniform(ks[13], (N_AB_LAYERS, 2, DN_HEADS), F32,
                                    math.log(1e-3), math.log(1e-1)))
    dn_dt_bias = dt + jnp.log(-jnp.expm1(-dt))
    dn_norm_w = 1.0 + nrm(ks[14], (N_AB_LAYERS, DN_HEAD_DIM), 0.02)
    diff_lambda = nrm(ks[15], (N_AB_LAYERS, 4, DIFF_QK_DIM), 0.1)
    diff_subln_w = 1.0 + nrm(ks[16], (N_AB_LAYERS, DIFF_V_DIM), 0.02)
    ab_w_out = nrm(ks[17], (N_AB_LAYERS, DN_WIDTH + DIFF_WIDTH, D_MODEL), (DN_WIDTH + DIFF_WIDTH) ** -0.5)
    ret_w_in = nrm(ks[18], (N_RET_LAYERS, D_MODEL, RET_IN), D_MODEL ** -0.5)
    base_logit = jnp.asarray(np.log(2.0 ** (5.0 + np.arange(RET_HEADS)) - 1.0).astype(np.float32))
    ret_decay_logit = base_logit + nrm(ks[19], (N_RET_LAYERS, 2, RET_HEADS), 0.1)
    ret_w_out = nrm(ks[20], (N_RET_LAYERS, RET_V_WIDTH, D_MODEL), RET_V_WIDTH ** -0.5)
    return {"x": x, "c": c, "ctx": ctx, "c_ctx": c_ctx, "ada_w": ada_w, "ada_b": ada_b,
            "norm_w": norm_w, "final_norm_w": final_norm_w, "ffn_w_in": ffn_w_in,
            "ffn_w_out": ffn_w_out, "ab_w_in": ab_w_in, "ab_conv_w": ab_conv_w,
            "dn_A_log": dn_A_log, "dn_dt_bias": dn_dt_bias, "dn_norm_w": dn_norm_w,
            "diff_lambda": diff_lambda, "diff_subln_w": diff_subln_w, "ab_w_out": ab_w_out,
            "ret_w_in": ret_w_in, "ret_decay_logit": ret_decay_logit, "ret_w_out": ret_w_out}

def reference(x, c, ctx, c_ctx, ada_w, ada_b, norm_w, final_norm_w, ffn_w_in, ffn_w_out,
              ab_w_in, ab_conv_w, dn_A_log, dn_dt_bias, dn_norm_w, diff_lambda, diff_subln_w,
              ab_w_out, ret_w_in, ret_decay_logit, ret_w_out):
    xc = ctx
    s_lat = jax.nn.silu(c)
    s_ctx = jax.nn.silu(c_ctx)[None]
    for l in range(DEPTH):
        last = l == DEPTH - 1
        m_lat = (s_lat @ ada_w[l] + ada_b[l]).reshape(-1, N_MOD, D_MODEL)
        m_ctx = (s_ctx @ ada_w[l] + ada_b[l]).reshape(1, N_MOD, D_MODEL)
        x = x + 0.5 * ada_gate(m_lat, 0) * swiglu(ada_in(x, norm_w[l, 0], m_lat, 0), ffn_w_in[l, 0], ffn_w_out[l, 0])
        xc = xc + 0.5 * ada_gate(m_ctx, 0) * swiglu(ada_in(xc, norm_w[l, 0], m_ctx, 0), ffn_w_in[l, 0], ffn_w_out[l, 0])
        hl = ada_in(x, norm_w[l, 1], m_lat, 1)
        hc = ada_in(xc, norm_w[l, 1], m_ctx, 1)
        i = l // 2
        if l % 2 == 0:
            yc, yl = ab_mixer(hc, hl, ab_w_in[i], ab_conv_w[i], dn_A_log[i], dn_dt_bias[i],
                              dn_norm_w[i], diff_lambda[i], diff_subln_w[i], ab_w_out[i],
                              l, not last)
        else:
            yc, yl = ret_mixer(hc, hl, ret_w_in[i], ret_decay_logit[i], ret_w_out[i], not last)
        x = x + ada_gate(m_lat, 1) * yl
        x = x + 0.5 * ada_gate(m_lat, 2) * swiglu(ada_in(x, norm_w[l, 2], m_lat, 2), ffn_w_in[l, 1], ffn_w_out[l, 1])
        if not last:
            xc = xc + ada_gate(m_ctx, 1) * yc
            xc = xc + 0.5 * ada_gate(m_ctx, 2) * swiglu(ada_in(xc, norm_w[l, 2], m_ctx, 2), ffn_w_in[l, 1], ffn_w_out[l, 1])
    return rms_norm(x, final_norm_w)


_drawn_inputs = setup_inputs


def setup_inputs(seed=0):
    import zlib

    import numpy as np

    out = dict(_drawn_inputs(seed))
    spreads = {}
    factors = {}
    for name, (base, spread) in spreads.items():
        noise = np.random.default_rng([zlib.crc32(name.encode()), seed]).standard_normal(out[name].shape)
        drawn = base * np.exp(spread * noise) if base else spread * noise
        out[name] = __import__('jax').numpy.asarray(drawn.astype(out[name].dtype))
    for name, factor in factors.items():
        out[name] = (out[name] * factor).astype(out[name].dtype)
    return out
```

```python
import math

import numpy as np

import concourse.bass as bass
from concourse import mybir

F32 = mybir.dt.float32
F32R = mybir.dt.float32r
BF16 = mybir.dt.bfloat16
ALU = mybir.AluOpType
ACT = mybir.ActivationFunctionType
AX = mybir.AxisListType

P = 128
D = 1024
KD = D // P
SEQ = 256
T = 2 * SEQ
NT = T // P
FF = 2816
NF = FF // P
FA, FB = 12, 10
DNH, DFH, RH = 4, 4, 8
EPS = 1e-6
LAMBDA_INIT = 0.8 - 0.6 * math.exp(0.0)
NADA = 2 * 9 * KD
CTX, LAT = slice(0, SEQ), slice(SEQ, T)
NEG = -1.0e30
LEVELS = 7

C_ID, C_ONE, C_TRIF, C_TRIB, C_CUTF, C_CUTB, C_ROTD, C_ROTR = range(8)
C_COSD, C_SIND = 8 * P, 8 * P + SEQ
NCONST = 8 * P + 2 * SEQ


def constants():
    i = np.arange(P)
    j, n = i[:, None], i[None, :]
    blocks = [np.eye(P), np.ones((P, P)), j <= n, j >= n,
              np.where(j <= n, 0.0, NEG), np.where(j >= n, 0.0, NEG)]

    def rotation(size):
        r = np.zeros((P, P))
        h = size // 2
        for o in range(P):
            if o % size < h:
                r[o + h, o] = -1.0
            else:
                r[o - h, o] = 1.0
        return r

    blocks += [rotation(32), rotation(P)]
    f32 = np.float32
    axis = 32
    inv = f32(10000.0) ** (-np.arange(0, axis, 2, dtype=f32) / f32(axis))
    tok = np.arange(SEQ)
    row, col = (tok // 64).astype(f32), (tok % 64).astype(f32)
    ang = np.zeros((P, SEQ), f32)
    for p in range(P):
        q = p % 64
        ang[p] = (row if q < 32 else col) * inv[q % 16]
    const = np.concatenate([np.asarray(b, f32) for b in blocks] + [np.cos(ang), np.sin(ang)], axis=1)
    levels = np.zeros((2, LEVELS, P, P), f32)
    for s in range(LEVELS):
        b = 1 << s
        m = ((n // (2 * b)) == (j // (2 * b))) & ((n // b) % 2 == 1) & ((j // b) % 2 == 0)
        levels[0, s], levels[1, s] = m, m.T
    levels = np.ascontiguousarray(levels.transpose(2, 0, 1, 3).reshape(P, 2 * LEVELS * P))
    ii = np.arange(SEQ)[None, :].astype(f32)
    jj = np.arange(SEQ)[:, None].astype(f32)
    tables = [np.abs(ii - jj), (jj <= ii), (jj >= ii), SEQ + ii - jj, SEQ - ii + jj]
    ret = [np.asarray(t, f32).reshape(2, P, SEQ).transpose(1, 0, 2).reshape(P, 2 * SEQ) for t in tables]
    invr = f32(10000.0) ** (-np.linspace(0.0, 1.0, 64, dtype=f32))
    angr = np.concatenate([invr, invr])[:, None] * tok[None, :].astype(f32)
    ret = np.concatenate(ret + [np.cos(angr), np.sin(angr)], axis=1).astype(f32)
    return const.astype(f32), levels, ret


class Tally:

    def __init__(self, sem):
        self.sem, self.n, self.i, self.k = sem, 0, 0, 0

    def inc(self, instruction, by=1):
        instruction.then_inc(self.sem, by)
        self.n += by

    def now(self):
        return self.n + self.i * self.k

    def enter(self, i, k):
        self.i, self.k, self.at = i, k, self.n

    def wait_by(self, eng):
        eng.wait_ge(self.sem, self.now())

    def leave(self, rounds):
        assert self.n - self.at == self.k, (self.n, self.at, self.k)
        self.n = self.at + rounds * self.k
        self.i = self.k = 0


def stages(names):
    return {name: n + 1 for n, name in enumerate(names)}


def build(nc, a):
    sems = {}

    def sem(name):
        if name not in sems:
            sems[name] = nc.alloc_semaphore(name)
        return sems[name]

    base = (nc.sbuf_base + 31) // 32 * 32
    end = nc.sbuf_usable_end
    cursor = [base]

    def put(name, shape, dt=F32, at=None):
        size = int(np.prod(shape[1:])) * (2 if dt == BF16 else 4)
        if at is None:
            at = cursor[0]
            cursor[0] += (size + 31) // 32 * 32
            assert cursor[0] <= end, (name, cursor[0], end)
        return nc.alloc_sbuf_tensor_at(name, shape, dt, offset=at), at

    x, _ = put("x", [P, KD, T])
    h_hi, at_h = put("h_hi", [P, KD, T], F32R)
    h_lo, _ = put("h_lo", [P, KD, T], F32R)
    w_raw = [put(f"w_raw{i}", [P, 2048])[0] for i in range(2)]
    w_hi, w_lo = [None, None], [None, None]
    w_hi[0], at_ring = put("w_hi0", [P, 2048], F32R)
    w_lo[0], _ = put("w_lo0", [P, 2048], F32R)
    w_hi[1], _ = put("w_hi1", [P, 2048], F32R)
    w_lo[1], _ = put("w_lo1", [P, 2048], F32R)
    ada_w, at_ada = put("ada_w", [P, 2, D])
    silu_c, _ = put("silu_c", [P, 2, D])
    ada_product, _ = put("ada_product", [P, D], BF16)
    at_r = cursor[0]
    cursor[0] += 72 * 1024
    sil, at_sil = put("sil", [P, 2, T])
    prod, at_prod = put("prod", [P, 2, T])
    const, _ = put("const", [P, NCONST])
    mcol, _ = put("mcol", [P, 2, NADA])
    mbias, _ = put("mbias", [P, NADA])
    norm_g, _ = put("norm_g", [P, 7, KD])
    mod, _ = put("mod", [P, 6, 3, 2, KD])
    mod_tmp, _ = put("mod_tmp", [P, 2, KD])
    conv_w, _ = put("conv_w", [P, 12, 3])
    vecs, _ = put("vecs", [P, 8])
    gate_in, _ = put("gate_in", [P, 2, 32])
    small, _ = put("small", [P, 512])
    hid_hi, _ = put("hid_hi", [P, FA, T], F32R, at=at_r)
    hid_lo, _ = put("hid_lo", [P, FA, T], F32R, at=at_r + FA * T * 4)
    ada0, _ = put("ada0", [P, KD, D], at=at_r)
    c_cols = small[:, 440:440 + 2 * KD]
    KB = 1024
    dn, _ = put("dn", [P, 4, DNH, T], at=at_r)
    df, _ = put("df", [P, 3 * DFH, T], at=at_r + 32 * KB)
    df_v, _ = put("df_v", [P, NT, DFH, P], at=at_r + 56 * KB)
    df_o, _ = put("df_o", [P, NT, DFH, P], at=at_r + 64 * KB)
    k_tok, _ = put("k_tok", [P, NT, DNH, P], at=at_h)
    v_tok, _ = put("v_tok", [P, NT, DNH, P], at=at_h + 8 * KB)
    dn_sq, _ = put("dn_sq", [P, 2, DNH, T], at=at_h + 16 * KB)
    gram_t, delta_t, sys_t, cut_t, inv_n, inv_t, xbuf, v_new, state, k_stage = ([None, None] for _ in range(10))
    spots = [at_r + 32 * KB + 2 * KB * i for i in range(12)] + [at_h + 16 * KB + 2 * KB * i for i in range(8)]
    for d in range(2):
        for buf, name in ((delta_t, "decay_t"), (gram_t, "qk_t"), (sys_t, "sys_t"), (cut_t, "cut_t"),
                          (inv_n, "inv"), (inv_t, "inv_t"), (xbuf, "xbuf"), (v_new, "v_new"),
                          (state, "state"), (k_stage, "k_stage")):
            buf[d], _ = put(f"{name}{d}", [P, DNH, P], at=spots.pop(0))
    levels, _ = put("levels", [P, 2 * LEVELS * P], at=at_ring)
    dn_o, _ = put("dn_o", [P, NT, DNH, P], at=at_ring + 8 * KB)
    y_f, _ = put("y_f", [P, 8, T], at=at_r)
    merge_sq, _ = put("merge_sq", [P, 8, P], at=at_ring + 16 * KB)
    merge_o, _ = put("merge_o", [P, 8, P], at=at_ring + 20 * KB)
    rq, _ = put("rq", [P, RH, SEQ], at=at_r)
    rk, _ = put("rk", [P, RH, T], at=at_r + 8 * KB)
    rv, _ = put("rv", [P, NT, 2 * D], at=at_r + 24 * KB)
    rg, _ = put("rg", [P, 16, SEQ], at=at_r + 56 * KB)
    ry_hi, _ = put("ry_hi", [P, 16, SEQ], F32R, at=at_r + 56 * KB)
    ry_lo, _ = put("ry_lo", [P, 16, SEQ], F32R, at=at_r + 8 * KB)
    rc, _ = put("rc", [P, 12 * SEQ], at=at_ada)
    r_decay = [put(f"r_decay{i}", [P, 4 * SEQ], at=at_h + 4 * KB * i)[0] for i in range(2)]
    r_back = [put(f"r_back{i}", [P, 4 * SEQ], at=at_h + (8 + 4 * i) * KB)[0] for i in range(2)]
    r_probs = [put(f"r_probs{i}", [P, 4 * SEQ], at=at_h + (16 + 4 * i) * KB)[0] for i in range(2)]
    r_kst = [put(f"r_kst{i}", [P, T], at=at_h + (24 + 2 * i) * KB)[0] for i in range(2)]
    r_square, _ = put("r_square", [P, 2 * SEQ], at=at_h + 28 * KB)

    ps = nc.alloc_psum_tensor("ps", [P, 8, 512], F32)
    NRM = 4

    def c_(i):
        return const[:, i * P:(i + 1) * P]

    ident, ones = c_(C_ID), c_(C_ONE)

    def over(ap, n):
        return ap.unsqueeze(1).to_broadcast([P, n, ap.shape[1]])

    def spread(ap, n):
        return ap.unsqueeze(2).to_broadcast([P, ap.shape[1], n])

    runs = []

    def run(name, n, elems, source):
        s0 = sum(r[2] for r in runs)
        runs.append((name, s0, n, elems, source))

    def ffn_runs(j):
        def up(f0):
            return lambda r: a["w_up"][j, bass.ds(f0 + r, 1)].rearrange("a p n -> (a p) n")

        def down(f0, nf):
            return lambda r: a["w_down"][j, bass.ds(r, 1), :, f0 * P:(f0 + nf) * P].rearrange("a p n -> (a p) n")

        run(f"up{j}a", FA, 2048, up(0))
        run(f"down{j}a", KD, FA * P, down(0, FA))
        run(f"up{j}b", FB, 2048, up(FA))
        run(f"down{j}b", KD, FB * P, down(FA, FB))

    def tiles(key, t0):
        return lambda r: a[key][bass.ds(t0 + r, 1)].rearrange("a p n -> (a p) n")

    ffn_runs(0)
    run("diff", 6, 2048, tiles("w_ab", 0))
    run("conv", 6, 2048, tiles("w_ab", 6))
    run("z", 2, 2048, tiles("w_ab", 12))
    run("ab", 1, 128, lambda r: a["w_ab16"])
    run("about", KD, D, tiles("w_ab_out", 0))
    ffn_runs(1)
    ffn_runs(2)
    run("retq", 4, 2048, tiles("w_ret", 0))
    run("retk", 4, 2048, tiles("w_ret", 4))
    run("retv", 8, 2048, tiles("w_ret", 8))
    run("retg", 8, 2048, tiles("w_ret", 16))
    run("retout", KD, 2048, tiles("w_ret_out", 0))
    ffn_runs(3)
    R = {r[0]: r for r in runs}
    STEPS = sum(r[2] for r in runs)
    ELEMS = [r[3] for r in runs for _ in range(r[2])]

    def walk(eng, name, body, tallies=(), skip=0):
        _, s0, n, _, _ = R[name]
        looped = (n - 2 - skip) // 2
        for r in range(skip):
            body(s0 + r, (s0 + r) % 2, r, ELEMS[s0 + r + 2])
        if looped >= 2:
            with eng.Fori(0, looped) as i:
                for t, k in tallies:
                    t.enter(i, k)
                for b in range(2):
                    r = skip + 2 * i + b
                    body(s0 + r, (s0 + skip + b) % 2, r, ELEMS[s0 + skip + b])
                for t, k in tallies:
                    t.leave(looped)
            first = skip + 2 * looped
        else:
            first = skip
        for r in range(first, n):
            s = s0 + r
            body(s, s % 2, r, ELEMS[s + 2] if s + 2 < STEPS else 0)

    raw_ready = [sem(f"raw_ready{i}") for i in range(2)]
    hi_ready = sem("hi_ready")
    lo_ready = sem("lo_ready")
    step_done = sem("step_done")
    acc_free = sem("acc_free")
    silu_done = sem("silu_done")
    hidden_hi = sem("hidden_hi")
    hidden_lo = sem("hidden_lo")
    sq_ready = sem("sq_ready")
    ssq_done = sem("ssq_done")
    root_done = sem("root_done")
    diag_done = sem("diag_done")
    rstd_done = sem("rstd_done")
    mod_ready = sem("mod_ready")
    normed = sem("normed")
    shifted = sem("shifted")
    h_hi_done = sem("h_hi_done")
    h_lo_done = sem("h_lo_done")
    ada_ready = [sem(f"ada_ready{i}") for i in range(2)]
    ada_dot = sem("ada_dot")
    loaded = sem("loaded")
    c_silu = sem("c_silu")

    norms = ["n00", "n01", "n02", "n10", "n11", "n12", "fin"]
    chunks_before = {n: KD * i for i, n in enumerate(norms)}
    ups_before = {}
    count = 0
    for j in range(4):
        for part, nf in (("a", FA), ("b", FB)):
            ups_before[f"up{j}{part}"] = count
            count += nf

    RESIDENT = 9
    ADA_SHIFT = KD
    ADA_START = 2 * KD
    c_loaded, x_loaded = sem("c_loaded"), sem("x_loaded")
    ada0_ready, ada0_done = [sem(f"ada0_ready{k}") for k in range(KD)], sem("ada0_done")

    def sp_program(sp):
        sp.dma_start(c_cols, a["c_cols"]).then_inc(c_loaded, 16)
        sp.dma_start(silu_c[:, 0, :], a["c_ctx"].partition_broadcast(P)).then_inc(c_loaded, 16)
        sp.dma_start(silu_c[:, 1, :], a["c"][0, :].partition_broadcast(P)).then_inc(c_loaded, 16)
        sp.dma_start(x[:], a["xT"]).then_inc(x_loaded, 16)
        sp.dma_start(const[:], a["const"]).then_inc(x_loaded, 16)
        for k in range(KD):
            sp.dma_start(ada0[:, k, :], a["ada0"][k]).then_inc(ada0_ready[k], 16)
        for dst, key in ((mbias[:], "mbias"), (norm_g[:], "norm_g"), (conv_w[:], "conv_w"),
                         (vecs[:, 0:1], "dn_norm"), (vecs[:, 1:2], "subln")):
            sp.dma_start(dst, a[key]).then_inc(loaded, 16)
        sp.dma_start(gate_in[:, 0, :], a["a_log"][0, :].partition_broadcast(P)).then_inc(loaded, 16)
        sp.dma_start(gate_in[:, 1, :], a["dt_bias"][0, :].partition_broadcast(P)).then_inc(loaded, 16)
        sp.dma_start(small[:, 0:16], a["ret_decay"][0, :].partition_broadcast(P)).then_inc(loaded, 16)
        sp.dma_start(small[:, 64:320], a["lam"][0, :].partition_broadcast(P)).then_inc(loaded, 16)

        for name, s0, n, elems, source in runs:
            def load(s, slot, r, wait=True):
                if wait:
                    sp.wait_ge(lo_ready, s - 1)
                src = source(r)
                sp.dma_start(w_raw[slot][:, 0:elems], src).then_inc(raw_ready[slot], 16)

            first = 0
            if s0 == 0:
                load(0, 0, 0, wait=False)
                load(1, 1, 1, wait=False)
                first = 2
            m = (n - first) // 2
            if m >= 2:
                with sp.Fori(0, m) as i:
                    for b in range(2):
                        load(s0 + first + 2 * i + b, (s0 + first + b) % 2, first + 2 * i + b)
                first += 2 * m
            for r in range(first, n):
                load(s0 + r, (s0 + r) % 2, r)
        sp.wait_ge(sem("out_ready"), 1)
        sp.dma_start(a["out"], x[:, :, LAT]).then_inc(sem("out_stored"), 16)
        sp.wait_ge(sem("out_stored"), 16)

    ADA_BEFORE_DN = ADA_START + 60 + 2

    def pool_program(pool):
        def tile(t, slot, wait=True):
            if wait:
                pool.wait_ge(ada_dot, 2 * t - 2)
            index = t if isinstance(t, int) and t < ADA_SHIFT else t - ADA_START + ADA_SHIFT
            pool.dma_start(ada_w[:, slot, :], a["ada"][bass.ds(index, 1)].rearrange("a p n -> (a p) n")) \
                .then_inc(ada_ready[slot], 16)

        for t in range(ADA_SHIFT):
            tile(t, t % 2, wait=t >= 2)
        for t in range(2):
            pool.wait_ge(ada_dot, 2 * (ADA_SHIFT - 1 + t))
            tile(ADA_START + t, t, wait=False)
        with pool.Fori(0, (ADA_BEFORE_DN - ADA_START - 2) // 2) as i:
            for b in range(2):
                tile(ADA_START + 2 + 2 * i + b, b)
        pool_deltanet(pool)
        with pool.Fori(0, (NADA - ADA_BEFORE_DN) // 2) as i:
            for b in range(2):
                tile(ADA_BEFORE_DN + 2 * i + b, b)
        pool_retention(pool)

    order_a = Tally(sem("scalar_order"))

    def split_hi(act, s, slot, elems, deferred=False):
        act.wait_ge(raw_ready[slot], 8 * (s - slot) + 16)
        if not (isinstance(s, int) and s < 2):
            act.wait_ge(step_done, s - 1)
        act.activation(w_hi[slot][:, 0:elems], w_raw[slot][:, 0:elems], ACT.Copy).then_inc(hi_ready, 1)

    def act_up(act, name, cols):
        u0 = ups_before[name]
        n = cols.stop - cols.start

        def body(s, slot, r, ahead):
            act.wait_ge(step_done, s + 1)
            act.activation(sil[:, slot, 0:n], ps[:, 2 * slot, cols], ACT.Silu).then_inc(silu_done, 1)
            if ahead:
                split_hi(act, s + 2, slot, ahead)
            act.wait_ge(acc_free, s + 3)
            act.activation(hid_hi[:, bass.ds(r, 1), cols].rearrange("p a n -> p (a n)"), prod[:, slot, 0:n],
                           ACT.Copy).then_inc(hidden_hi, 1)
        walk(act, name, body)

    def act_plain(act, name):
        def body(s, slot, r, ahead):
            if ahead:
                split_hi(act, s + 2, slot, ahead)
        walk(act, name, body)

    def act_square(act, norm, r, slot, cols):
        n = cols.stop - cols.start
        if not (isinstance(r, int) and chunks_before[norm] + r < 2):
            act.wait_ge(ssq_done, chunks_before[norm] + r - 1)
        act.activation(prod[:, slot, 0:n], x[:, bass.ds(r, 1), cols].rearrange("p a n -> p (a n)"),
                       ACT.Square).then_inc(sq_ready, 1)

    warm_root, _ = put("warm_root", [P, 1])
    warmed = sem("warmed")

    def act_down_norm(act, name, norm, cols):
        s0 = R[name][1]

        def body(s, slot, r, ahead):
            if ahead:
                split_hi(act, s + 2, slot, ahead)
            if isinstance(r, int) and r == KD - 1:
                act.activation(warm_root[:], vecs[:, 2:3], ACT.Sqrt).then_inc(warmed, 1)
            act.wait_ge(acc_free, s + 3)
            act_square(act, norm, r, slot, cols)
        walk(act, name, body)

    def act_root(act, norm, t0, scale):
        k = norms.index(norm)
        act.wait_ge(ssq_done, chunks_before[norm] + KD)
        act.activation(small[:, 320 + 16 * k + t0:320 + 16 * k + NT], ps[:, NRM, t0:NT], ACT.Sqrt, bias=vecs[:, 2:3],
                       scale=scale).then_inc(root_done, 1)

    def act_modulate(act, norm):
        k, base_c = norms.index(norm), chunks_before[norm]

        def one(c, b):
            act.wait_ge(normed, base_c + c + 1)
            if not (isinstance(c, int) and base_c + c < 2):
                act.wait_ge(h_lo_done, base_c + c - 1)
            for st, cols in live(norm):
                last = act.activation(sil[:, b, cols], prod[:, b, cols], ACT.Identity,
                                      bias=mod[:, k, 1, st, bass.ds(c, 1)], scale=mod[:, k, 0, st, bass.ds(c, 1)])
            last.then_inc(shifted, 1)
            act.wait_ge(shifted, base_c + c + 1)
            cols = streams_of(norm)
            act.activation(h_hi[:, bass.ds(c, 1), cols].rearrange("p a n -> p (a n)"), sil[:, b, cols],
                           ACT.Copy).then_inc(h_hi_done, 1)
        one(0, 0)
        one(1, 1)
        with act.Fori(0, (KD - 2) // 2) as i:
            for b in range(2):
                one(2 * i + 2 + b, b)

    def streams_of(norm):
        return slice(live(norm)[0][1].start, T)

    def live(norm):
        return ((1, LAT),) if norm in ("n12", "fin") else ((0, CTX), (1, LAT))

    ALL = slice(0, T)

    def scalar_program(act):
        act.wait_ge(c_loaded, 48)
        act.activation(c_cols, c_cols, ACT.Silu).then_inc(c_silu, 1)
        act.activation(silu_c[:], silu_c[:], ACT.Silu).then_inc(c_silu, 1)
        act.wait_ge(sem("eps_set"), 1)
        act.wait_ge(x_loaded, 32)
        for r in range(KD):
            act_square(act, "n00", r, r % 2, ALL)
        act_root(act, "n00", 0, 1.0 / D)
        act.wait_ge(loaded, 16 * RESIDENT)
        split_hi(act, 0, 0, ELEMS[0])
        split_hi(act, 1, 1, ELEMS[1])
        act_modulate(act, "n00")
        act_up(act, "up0a", ALL)
        act_plain(act, "down0a")
        act_up(act, "up0b", ALL)
        act_down_norm(act, "down0b", "n01", ALL)
        act_root(act, "n01", 0, 1.0 / D)
        act_modulate(act, "n01")
        act_ab(act)
        act_down_norm(act, "about", "n02", ALL)
        act_root(act, "n02", 0, 1.0 / D)
        act_modulate(act, "n02")
        act_up(act, "up1a", ALL)
        act_plain(act, "down1a")
        act_up(act, "up1b", ALL)
        act_down_norm(act, "down1b", "n10", ALL)
        act_root(act, "n10", 0, 1.0 / D)
        act_modulate(act, "n10")
        act_up(act, "up2a", ALL)
        act_plain(act, "down2a")
        act_up(act, "up2b", ALL)
        act_down_norm(act, "down2b", "n11", ALL)
        act_root(act, "n11", 0, 1.0 / D)
        act_modulate(act, "n11")
        act_ret(act)
        act_down_norm(act, "retout", "n12", LAT)
        act_root(act, "n12", 2, 1.0 / D)
        act_modulate(act, "n12")
        act_up(act, "up3a", LAT)
        act_plain(act, "down3a")
        act_up(act, "up3b", LAT)
        act_down_norm(act, "down3b", "fin", LAT)
        act_root(act, "fin", 2, 1.0 / D)

    order_v = Tally(sem("vector_order"))

    def split_lo(dve, s, slot, elems):
        dve.wait_ge(hi_ready, s + 1)
        dve.tensor_tensor(w_lo[slot][:, 0:elems], w_raw[slot][:, 0:elems], w_hi[slot][:, 0:elems].bitcast(F32),
                          ALU.subtract).then_inc(lo_ready, 1)

    def ada_tile(dve, t, slot):
        dve.wait_ge(ada_ready[slot], 8 * ((t if isinstance(t, int) and t < ADA_SHIFT else t - ADA_START + ADA_SHIFT) - slot) + 16)
        for st in range(2):
            if not (isinstance(t, int) and t == 0 and st == 0):
                dve.wait_ge(ada_dot, 2 * t + st)
            dve.scalar_tensor_tensor(out=ada_product[:], in0=ada_w[:, slot, :], scalar=1.0, in1=silu_c[:, st, :],
                                     op0=ALU.mult, op1=ALU.mult, accum_out=mcol[:, st, bass.ds(t, 1)]) \
               .then_inc(ada_dot, 1)

    ada_next = [0]

    def dve_up(dve, name, cols, ada):
        u0, t0 = ups_before[name], ada_next[0]
        n = cols.stop - cols.start

        def body(s, slot, r, ahead):
            dve.wait_ge(silu_done, u0 + r + 1)
            if not (isinstance(r, int) and u0 + r < 2):
                dve.wait_ge(hidden_lo, u0 + r - 1)
            dve.tensor_tensor(prod[:, slot, 0:n], sil[:, slot, 0:n], ps[:, 2 * slot + 1, cols], ALU.mult) \
               .then_inc(acc_free, 1)
            if ahead:
                split_lo(dve, s + 2, slot, ahead)
            dve.wait_ge(hidden_hi, u0 + r + 1)
            dve.tensor_tensor(hid_lo[:, bass.ds(r, 1), cols].rearrange("p a n -> p (a n)"), prod[:, slot, 0:n],
                              hid_hi[:, bass.ds(r, 1), cols].rearrange("p a n -> p (a n)").bitcast(F32),
                              ALU.subtract).then_inc(hidden_lo, 1)
            for q in range(ada):
                ada_tile(dve, t0 + ada * r + q, (t0 + q) % 2)
        walk(dve, name, body, skip=2)
        ada_next[0] += ada * R[name][2]

    def dve_down(dve, name, norm_gate, streams, ada):
        k, t0 = norms.index(norm_gate), ada_next[0]

        def body(s, slot, r, ahead):
            dve.wait_ge(step_done, s + 1)
            for st, cols in streams:
                xc = x[:, bass.ds(r, 1), cols].rearrange("p a n -> p (a n)")
                last = dve.scalar_tensor_tensor(out=xc, in0=ps[:, 2 * slot, cols],
                                                scalar=mod[:, k, 2, st, bass.ds(r, 1)], in1=xc,
                                                op0=ALU.mult, op1=ALU.add)
            last.then_inc(acc_free, 1)
            if ahead:
                split_lo(dve, s + 2, slot, ahead)
            if ada:
                ada_tile(dve, t0 + r, (t0 + slot + R[name][1]) % 2)
        walk(dve, name, body)
        ada_next[0] += R[name][2] if ada else 0

    def dve_mod(dve, norm):
        k = norms.index(norm)
        t = 3 * KD * k

        def bias(m):
            return over(mbias[:, t + m * KD:t + (m + 1) * KD], 2)

        dve.wait_ge(ada_dot, 2 * (t + 3 * KD)) if norm != "n00" else None
        order_v.inc(dve.tensor_tensor(mod_tmp[:], mcol[:, :, t + KD:t + 2 * KD], bias(1), ALU.add))
        order_v.wait_by(dve)
        order_v.inc(dve.scalar_tensor_tensor(out=mod[:, k, 0], in0=mod_tmp[:], scalar=1.0,
                                             in1=over(norm_g[:, k, :], 2), op0=ALU.add, op1=ALU.mult))
        dve.tensor_tensor(mod[:, k, 1], mcol[:, :, t:t + KD], bias(0), ALU.add).then_inc(mod_ready, 1)
        order_v.wait_by(dve)

    def dve_gate(dve, norm):
        k = norms.index(norm)
        t = 3 * KD * k + 2 * KD
        dve.wait_ge(ada_dot, 2 * (t + KD))
        order_v.inc(dve.tensor_tensor(mod_tmp[:], mcol[:, :, t:t + KD], over(mbias[:, t:t + KD], 2), ALU.add))
        order_v.wait_by(dve)
        order_v.inc(dve.tensor_scalar(mod[:, k, 2], mod_tmp[:], 1.0 if k % 3 == 1 else 0.5, None, ALU.mult))
        order_v.wait_by(dve)

    def dve_rstd(dve, norm, t0):
        k = norms.index(norm)
        root = small[:, 320 + 16 * k:320 + 16 * k + NT]
        inv = small[:, 328 + 16 * k:328 + 16 * k + NT]
        dve.wait_ge(root_done, k + 1)
        dve.wait_ge(acc_free, 2)
        order_v.inc(dve.reciprocal(inv[:, t0:NT], root[:, t0:NT]))
        order_v.wait_by(dve)
        for t in range(t0, NT):
            last = dve.tensor_scalar(sil[:, 0, t * P:(t + 1) * P], ident, inv[:, t:t + 1], None, ALU.mult)
        last.then_inc(diag_done, 1)

    def dve_modulate(dve, norm):
        base_c, cols = chunks_before[norm], streams_of(norm)
        dve.wait_ge(rstd_done, norms.index(norm) + 1)
        dve.wait_ge(mod_ready, norms.index(norm) + 1)

        def flat(ap, c):
            return ap[:, bass.ds(c, 1), cols].rearrange("p a n -> p (a n)")

        def normalise(c, b):
            if not (isinstance(c, int) and base_c + c < 2):
                dve.wait_ge(shifted, base_c + c - 1)
            dve.tensor_tensor(prod[:, b, cols], flat(x, c), ps[:, NRM, cols], ALU.mult).then_inc(normed, 1)

        def lo_part(c, b):
            dve.wait_ge(h_hi_done, base_c + c + 1)
            dve.tensor_tensor(flat(h_lo, c), sil[:, b, cols], flat(h_hi, c).bitcast(F32), ALU.subtract) \
               .then_inc(h_lo_done, 1)

        normalise(0, 0)
        normalise(1, 1)
        with dve.Fori(0, (KD - 2) // 2) as i:
            for b in range(2):
                lo_part(2 * i + b, b)
                normalise(2 * i + 2 + b, b)
        lo_part(KD - 2, 0)
        lo_part(KD - 1, 1)
        dve.wait_ge(h_lo_done, base_c + KD)

    BOTH = ((0, CTX), (1, LAT))
    ONLY = ((1, LAT),)

    def vector_program(dve):
        dve.memset(vecs[:, 2:3], EPS).then_inc(sem("eps_set"), 1)
        for slot in range(2):
            dve.memset(sil[:, slot], 0.0).then_inc(acc_free, 1)
        dve.wait_ge(c_silu, 2)
        for t in range(ADA_SHIFT):
            ada_tile(dve, t, t % 2)
        dve.wait_ge(x_loaded, 32)
        dve_rstd(dve, "n00", 0)
        split_lo(dve, 0, 0, ELEMS[0])
        split_lo(dve, 1, 1, ELEMS[1])
        dve.wait_ge(loaded, 16 * RESIDENT)
        order_v.inc(dve.tensor_scalar(vecs[:, 1:2], vecs[:, 1:2], 1.0 - LAMBDA_INIT, None, ALU.mult))
        dve.wait_ge(ada0_done, 1)
        dve.tensor_copy(mcol[:, :, ADA_SHIFT:ADA_START],
                        ps[:, 5, 0:2 * KD].rearrange("p (n s) -> p s n", s=2)).then_inc(ada_dot, 2 * KD)
        ada_next[0] = ADA_START
        dve.wait_ge(ada_dot, 2 * ADA_START)
        dve_mod(dve, "n00")
        dve_modulate(dve, "n00")
        dve_up(dve, "up0a", ALL, 2)
        dve_gate(dve, "n00")
        dve_down(dve, "down0a", "n00", BOTH, 1)
        dve_up(dve, "up0b", ALL, 2)
        dve_down(dve, "down0b", "n00", BOTH, 1)
        dve_mod(dve, "n01")
        dve_rstd(dve, "n01", 0)
        dve_modulate(dve, "n01")
        dve_ab(dve)
        dve_gate(dve, "n01")
        dve_down(dve, "about", "n01", BOTH, 1)
        dve_mod(dve, "n02")
        dve_rstd(dve, "n02", 0)
        dve_modulate(dve, "n02")
        dve_gate(dve, "n02")
        dve_up(dve, "up1a", ALL, 2)
        dve_down(dve, "down1a", "n02", BOTH, 1)
        dve_up(dve, "up1b", ALL, 2)
        dve_down(dve, "down1b", "n02", BOTH, 1)
        dve_mod(dve, "n10")
        dve_rstd(dve, "n10", 0)
        dve_modulate(dve, "n10")
        dve_gate(dve, "n10")
        dve_up(dve, "up2a", ALL, 0)
        dve_down(dve, "down2a", "n10", BOTH, 0)
        dve_up(dve, "up2b", ALL, 0)
        dve_down(dve, "down2b", "n10", BOTH, 0)
        dve_mod(dve, "n11")
        dve_rstd(dve, "n11", 0)
        dve_modulate(dve, "n11")
        dve_ret(dve)
        dve_gate(dve, "n11")
        dve_down(dve, "retout", "n11", ONLY, 0)
        dve_mod(dve, "n12")
        dve_rstd(dve, "n12", 2)
        dve_modulate(dve, "n12")
        dve_gate(dve, "n12")
        dve_up(dve, "up3a", LAT, 0)
        dve_down(dve, "down3a", "n12", ONLY, 0)
        dve_up(dve, "up3b", LAT, 0)
        dve_down(dve, "down3b", "n12", ONLY, 0)
        dve_rstd(dve, "fin", 2)
        dve.wait_ge(rstd_done, len(norms))
        for c in range(KD):
            last = dve.scalar_tensor_tensor(out=x[:, c, LAT], in0=x[:, c, LAT], scalar=norm_g[:, 6, c:c + 1],
                                            in1=ps[:, NRM, LAT], op0=ALU.mult, op1=ALU.mult)
        last.then_inc(sem("out_ready"), 1)

    def products(pe, out, slot, off, nk, rhs_hi, rhs_lo, first=True, last=True):
        for k in range(nk):
            hi = w_hi[slot][:, off + k * P:off + (k + 1) * P]
            lo = w_lo[slot][:, off + k * P:off + (k + 1) * P]
            pe.matmul(out, lo, rhs_hi(k), start=first and k == 0, stop=False)
            pe.matmul(out, hi, rhs_lo(k), start=False, stop=False)
            mm = pe.matmul(out, hi, rhs_hi(k), start=False, stop=last and k == nk - 1)
        return mm

    def pe_ready(pe, s):
        pe.wait_ge(lo_ready, s + 1)
        pe.wait_ge(acc_free, s + 1)

    def pair_products(pe, s, slot, cols, norm=None):
        pe_ready(pe, s)
        for k in range(KD if norm else 0):
            pe.wait_ge(h_lo_done, chunks_before[norm] + k + 1)
            for u in range(2):
                mm = products(pe, ps[:, 2 * slot + u, cols], slot, u * D + k * P, 1, lambda _: h_hi[:, k, cols],
                              lambda _: h_lo[:, k, cols], k == 0, k == KD - 1)
        for u in range(0 if norm else 2):
            mm = products(pe, ps[:, 2 * slot + u, cols], slot, u * D, KD,
                          lambda k: h_hi[:, k, cols], lambda k: h_lo[:, k, cols])
        mm.then_inc(step_done, 1)

    def pe_pairs(pe, name, cols, norm=None):
        def body(s, slot, r, ahead):
            pair_products(pe, s, slot, cols, norm if isinstance(r, int) and r == 0 else None)
        walk(pe, name, body, skip=2)

    def pe_ssq(pe, norm, r, slot, t0):
        pe.wait_ge(sq_ready, chunks_before[norm] + r + 1)
        off = t0 * P
        for t in range(t0, NT):
            mm = pe.matmul(ps[:, NRM, t:t + 1], prod[:, slot, t * P - off:(t + 1) * P - off], ones[:, 0:1],
                           start=isinstance(r, int) and r == 0 and t == t0,
                           stop=isinstance(r, int) and r == KD - 1, skip_group_check=True)
        mm.then_inc(ssq_done, 1)

    def pe_down(pe, name, nk, hi, lo, cols, norm=None, up=None, t0=0, ready=None):
        s0 = R[name][1]

        def body(s, slot, r, ahead):
            pe_ready(pe, s)
            if up and isinstance(r, int) and r == 0:
                pe.wait_ge(hidden_lo, up - 1)
            off = s
            for k in range(nk):
                if up and isinstance(r, int) and r == 0 and k == nk - 1:
                    pe.wait_ge(hidden_lo, up)
                if ready and isinstance(r, int) and r == 0:
                    ready(k)
                whi = w_hi[slot][:, k * P:(k + 1) * P]
                wlo = w_lo[slot][:, k * P:(k + 1) * P]
                pe.matmul(ps[:, 2 * slot, cols], wlo, hi(k), start=k == 0, stop=False)
                pe.matmul(ps[:, 2 * slot, cols], whi, lo(k), start=False, stop=False)
                mm = pe.matmul(ps[:, 2 * slot, cols], whi, hi(k), start=False, stop=k == nk - 1)
            mm.then_inc(step_done, 1)
            if norm and not (isinstance(r, int) and r == 0):
                pe_ssq(pe, norm, r - 1, 1 - slot, t0)
        walk(pe, name, body, skip=2)
        if norm:
            pe_ssq(pe, norm, KD - 1, (s0 + KD - 1) % 2, t0)

    def pe_rstd(pe, norm, t0):
        pe.wait_ge(diag_done, norms.index(norm) + 1)
        pe.matmul(ps[:, NRM, t0 * P:T], ones, sil[:, 0, t0 * P:T], start=True, stop=True).then_inc(rstd_done, 1)

    def pe_ffn(pe, j, cols, of, norm, t0):
        for part, nf in (("a", FA), ("b", FB)):
            name = f"up{j}{part}"
            pe_pairs(pe, name, cols, norm=of if part == "a" else None)
            pe_down(pe, f"down{j}{part}", nf, lambda k: hid_hi[:, k, cols], lambda k: hid_lo[:, k, cols], cols,
                    norm=norm if part == "b" else None, up=ups_before[name] + nf, t0=t0)

    def tensor_program(pe):
        pe.wait_ge(x_loaded, 32)
        for r in range(KD):
            pe_ssq(pe, "n00", r, r % 2, 0)
        pe.wait_ge(c_silu, 1)
        for k in range(KD):
            pe.wait_ge(ada0_ready[k], 16)
            for n in range(KD):
                mm = pe.matmul(ps[:, 5, 2 * n:2 * n + 2], ada0[:, k, n * P:(n + 1) * P],
                               c_cols[:, 2 * k:2 * k + 2], start=k == 0 and n == 0, stop=k == KD - 1,
                               skip_group_check=True)
        mm.then_inc(ada0_done, 1)
        pe_rstd(pe, "n00", 0)
        pe_ffn(pe, 0, ALL, "n00", "n01", 0)
        pe_rstd(pe, "n01", 0)
        pe_ab(pe)
        pe_down(pe, "about", KD, lambda k: h_hi[:, k, :], lambda k: h_lo[:, k, :], ALL, norm="n02")
        pe_rstd(pe, "n02", 0)
        pe_ffn(pe, 1, ALL, "n02", "n10", 0)
        pe_rstd(pe, "n10", 0)
        pe_ffn(pe, 2, ALL, "n10", "n11", 0)
        pe_rstd(pe, "n11", 0)
        pe_ret(pe)
        pe_down(pe, "retout", 16, lambda k: ry_hi[:, k, :], lambda k: ry_lo[:, k, :], LAT, norm="n12", t0=2,
                ready=lambda k: pe.wait_ge(r_lo, k // 2 + 1))
        pe_rstd(pe, "n12", 2)
        pe_ffn(pe, 3, LAT, "n12", "fin", 2)
        pe_rstd(pe, "fin", 2)

    dnf = dn[:].rearrange("p a h t -> p (a h) t")
    S_AB = R["ab"][1]
    gates, _ = put("gates", [P, 12, 32])
    ab_tok, G_Y, G_ABS, G_EXP, G_S, G_S2, G_POLY, G_OUT = (gates[:, n, :] for n in range(8))
    log_decay, beta, g_tmp = gates[:, 8, :], gates[:, 9, :], gates[:, 10, :]
    ab_raw, _ = put("ab_raw", [P, NT, 16])
    qk_inv, _ = put("qk_inv", [P, 2, NT, 4], at=at_ring + 26 * KB)
    qk_root, _ = put("qk_root", [P, 2, NT, 4], at=at_ring + 27 * KB)
    dsm, _ = put("dsm", [P, 2, 6, 4])
    la_stage, _ = put("la_stage", [P, 2, 4])
    attn_s, _ = put("attn_s", [P, 16])
    merge_s, _ = put("merge_s", [P, NT, 24], at=at_ring + 24 * KB)

    abs_ready, exp_ready = sem("abs_ready"), sem("exp_ready")

    def dve_softplus(dve, y, out, n, use):
        ab, ex, s, s2, p = (g[:, 0:n] for g in (G_ABS, G_EXP, G_S, G_S2, G_POLY))
        order_v.inc(dve.tensor_scalar(ab, y, -1.0, None, ALU.mult))
        order_v.wait_by(dve)
        dve.tensor_tensor(ab, ab, y, ALU.max).then_inc(abs_ready, 1)
        dve.wait_ge(exp_ready, use)
        order_v.inc(dve.tensor_scalar(s, ex, 2.0, None, ALU.add))
        order_v.wait_by(dve)
        order_v.inc(dve.reciprocal(s2, s))
        order_v.wait_by(dve)
        order_v.inc(dve.tensor_tensor(s, ex, s2, ALU.mult))
        order_v.wait_by(dve)
        order_v.inc(dve.tensor_tensor(s2, s, s, ALU.mult))
        order_v.wait_by(dve)
        order_v.inc(dve.tensor_scalar(p, s2, 1.0 / 17.0, None, ALU.mult))
        for term in range(7, 0, -1):
            order_v.wait_by(dve)
            order_v.inc(dve.scalar_tensor_tensor(out=p, in0=p, scalar=1.0 / (2 * term + 1), in1=s2,
                                                 op0=ALU.add, op1=ALU.mult))
        order_v.wait_by(dve)
        order_v.inc(dve.scalar_tensor_tensor(out=p, in0=p, scalar=1.0, in1=s, op0=ALU.add, op1=ALU.mult))
        order_v.inc(dve.tensor_scalar(ab, y, 0.0, None, ALU.max))
        order_v.wait_by(dve)
        order_v.inc(dve.scalar_tensor_tensor(out=out, in0=p, scalar=2.0, in1=ab, op0=ALU.mult, op1=ALU.add))
        order_v.wait_by(dve)

    def act_softplus(act, n, use):
        act.wait_ge(abs_ready, use)
        act.activation(G_EXP[:, 0:n], G_ABS[:, 0:n], ACT.Exp, scale=-1.0).then_inc(exp_ready, 1)

    rot_done, rope_done = sem("rot_done"), sem("rope_done")
    dv_turned, dv_done = sem("dv_turned"), sem("dv_done")
    lam_sum, lam_exp = sem("lam_sum"), sem("lam_exp")
    scores_done, max_done, probs_done = sem("scores_done"), sem("max_done"), sem("probs_done")
    mixed_done, turned_done, pt_done = sem("mixed_done"), sem("turned_done"), sem("pt_done")
    pv_done, attn_out = sem("pv_done"), sem("attn_out")
    ATTN = [(h, qt, SEQ if qt < 2 else T) for h in range(DFH) for qt in range(NT)]
    S_DIFF_END = R["conv"][1]

    def pe_diff(pe):
        pe.wait_ge(acc_free, S_DIFF_END + 2)
        for j in range(4):
            if j >= 2:
                pe.wait_ge(rope_done, j - 1)
            pe.matmul(ps[:, 5 + j % 2, :], c_(C_ROTD), df[:, 2 * j:2 * j + 2, LAT], start=True, stop=True) \
              .then_inc(rot_done, 1)
        for t in range(NT):
            bank = (4, 7)[t % 2]
            if t >= 2:
                pe.wait_ge(dv_done, t - 1)
            for h in range(DFH):
                mm = pe.transpose(ps[:, bank, h * P:(h + 1) * P], df[:, 8 + h, t * P:(t + 1) * P], ident)
            mm.then_inc(dv_turned, 1)
        pe.wait_ge(rope_done, 4)
        pe.wait_ge(dv_done, NT)
        for n, (h, qt, nk) in enumerate(ATTN):
            if n >= 2:
                pe.wait_ge(probs_done, n - 1)
            for m in range(2):
                rows = slice(64 * m, 64 * m + 64)
                mm = pe.matmul(ps[:, 2 * (n % 2) + m, 0:nk], df[rows, h, qt * P:(qt + 1) * P], df[rows, 4 + h, 0:nk],
                               start=True, stop=True)
            mm.then_inc(scores_done, 1)
            if n >= 1:
                pe_attend(pe, n - 1)
        pe_attend(pe, len(ATTN) - 1)
        pe.wait_ge(attn_out, len(ATTN))

    def pe_attend(pe, n):
        h, qt, nk = ATTN[n]
        pe.wait_ge(mixed_done, n + 1)
        if n >= 2:
            pe.wait_ge(pt_done, n - 1)
        for kt in range(nk // P):
            mm = pe.transpose(ps[:, 5 + n % 2, kt * P:(kt + 1) * P], prod[:, 0, kt * P:(kt + 1) * P], ident)
        mm.then_inc(turned_done, 1)
        pe.wait_ge(pt_done, n + 1)
        if n >= 2:
            pe.wait_ge(attn_out, n - 1)
        for kt in range(nk // P):
            mm = pe.matmul(ps[:, (4, 7)[n % 2], 0:P], prod[:, 1, kt * P:(kt + 1) * P], df_v[:, kt, h, :],
                           start=kt == 0, stop=kt == nk // P - 1)
        mm.then_inc(pv_done, 1)

    def act_diff(act):
        for t in range(NT):
            act.wait_ge(dv_turned, t + 1)
            act.activation(df_v[:, t].rearrange("p h d -> p (h d)"), ps[:, (4, 7)[t % 2], :], ACT.Copy) \
               .then_inc(dv_done, 1)
        act.wait_ge(lam_sum, 1)
        act.activation(attn_s[:, 2:4], attn_s[:, 0:2], ACT.Exp).then_inc(lam_exp, 1)
        for n in range(len(ATTN) + 1):
            if n < len(ATTN):
                nk = ATTN[n][2]
                act.wait_ge(max_done, n + 1)
                if n >= 1:
                    act.wait_ge(mixed_done, n)
                for m in range(2):
                    last = act.activation(sil[:, m, 0:nk], ps[:, 2 * (n % 2) + m, 0:nk], ACT.Exp,
                                          bias=attn_s[:, 6 + m:7 + m], scale=0.125, accum_out=attn_s[:, 8 + m:9 + m])
                last.then_inc(probs_done, 1)
            if n >= 1:
                h, qt, nk = ATTN[n - 1]
                act.wait_ge(turned_done, n)
                if n >= 2:
                    act.wait_ge(pv_done, n - 1)
                act.activation(prod[:, 1, 0:nk], ps[:, 5 + (n - 1) % 2, 0:nk], ACT.Copy).then_inc(pt_done, 1)
                act.wait_ge(pv_done, n)
                act.activation(df_o[:, qt, h, :], ps[:, (4, 7)[(n - 1) % 2], 0:P], ACT.Copy).then_inc(attn_out, 1)

    def dve_diff(dve):
        for j in range(4):
            lat = df[:, 2 * j:2 * j + 2, LAT]
            dve.wait_ge(rot_done, j + 1)
            if j:
                dve.wait_ge(rope_done, j)
            p2 = prod[:, j % 2, :].rearrange("p (a t) -> p a t", a=2)
            rot = ps[:, 5 + j % 2, :].rearrange("p (a t) -> p a t", a=2)
            dve.tensor_tensor(p2, rot, over(const[:, C_SIND:C_SIND + SEQ], 2), ALU.mult)
            order_v.inc(dve.tensor_tensor(lat, lat, over(const[:, C_COSD:C_COSD + SEQ], 2), ALU.mult))
            order_v.wait_by(dve)
            dve.tensor_tensor(lat, lat, p2, ALU.add).then_inc(rope_done, 1)
        dve.wait_ge(rope_done, 4)
        lam = small[:, 64:320]
        for m in range(2):
            last = dve.tensor_tensor(sil[:, 0, m * 64:(m + 1) * 64],
                                     lam[:, m * 128:m * 128 + 64], lam[:, m * 128 + 64:m * 128 + 128], ALU.mult)
        order_v.inc(last)
        order_v.wait_by(dve)
        dve.tensor_reduce(attn_s[:, 0:2], sil[:, 0, 0:128].rearrange("p (m d) -> p m d", m=2), AX.X, ALU.add) \
           .then_inc(lam_sum, 1)
        dve.wait_ge(lam_exp, 1)
        order_v.inc(dve.tensor_tensor(attn_s[:, 4:5], attn_s[:, 3:4], attn_s[:, 2:3], ALU.subtract))
        order_v.wait_by(dve)
        order_v.inc(dve.tensor_scalar(attn_s[:, 5:6], attn_s[:, 4:5], LAMBDA_INIT, None, ALU.subtract))
        order_v.wait_by(dve)
        for n in range(len(ATTN) + 1):
            if n < len(ATTN):
                nk = ATTN[n][2]
                dve.wait_ge(scores_done, n + 1)
                order_v.inc(dve.tensor_reduce(attn_s[:, 12:14], ps[:, 2 * (n % 2):2 * (n % 2) + 2, 0:nk], AX.X, ALU.max))
                order_v.wait_by(dve)
                if n >= 1:
                    dve.wait_ge(probs_done, n)
                dve.tensor_scalar(attn_s[:, 6:8], attn_s[:, 12:14], -0.125, None, ALU.mult).then_inc(max_done, 1)
                if n >= 1:
                    dve.wait_ge(turned_done, n)
                dve.wait_ge(probs_done, n + 1)
                order_v.inc(dve.reciprocal(attn_s[:, 10:12], attn_s[:, 8:10]))
                order_v.wait_by(dve)
                order_v.inc(dve.tensor_tensor(attn_s[:, 14:15], attn_s[:, 11:12], attn_s[:, 5:6], ALU.mult))
                order_v.inc(dve.tensor_scalar(prod[:, 0, 0:nk], sil[:, 0, 0:nk], attn_s[:, 10:11], None, ALU.mult))
                order_v.wait_by(dve)
                dve.scalar_tensor_tensor(out=prod[:, 0, 0:nk], in0=sil[:, 1, 0:nk], scalar=attn_s[:, 14:15],
                                         in1=prod[:, 0, 0:nk], op0=ALU.mult, op1=ALU.add).then_inc(mixed_done, 1)

    conv_center, conv_out = sem("conv_center"), sem("conv_out")
    gate_exp, gates_ready = sem("gate_exp"), sem("gates_ready")
    qk_squared, qk_summed, qk_rooted = sem("qk_squared"), sem("qk_summed"), sem("qk_rooted")
    qk_inverse = sem("qk_inverse")
    kv_turned, k_tok_done, v_tok_done = sem("kv_turned"), sem("k_tok_done"), sem("v_tok_done")
    k_back, k_feat_done = sem("k_back"), sem("k_feat_done")
    levels_ready = sem("levels_ready")

    def act_conv(act):
        def body(s, slot, r, ahead):
            act.wait_ge(step_done, s + 1)
            if not (isinstance(r, int) and r == 0):
                act.wait_ge(conv_out, r)
            for u in range(2):
                act.activation(prod[:, u, :], ps[:, 2 * slot + u, :], ACT.Copy,
                               scale=conv_w[:, bass.ds(2 * r + u, 1), 1:2].rearrange("p a b -> p (a b)")) \
                   .then_inc(conv_center, 1)
            if ahead:
                split_hi(act, s + 2, slot, ahead)
            act.wait_ge(acc_free, s + 3)
            act.activation(dnf[:, bass.ds(2 * r, 2), :], prod[:], ACT.Silu).then_inc(conv_out, 1)
        walk(act, "conv", body, skip=2)

        def z_body(s, slot, r, ahead):
            if r == 0:
                split_hi(act, s + 2, slot, ahead)
            act.wait_ge(acc_free, s + 3)
            act.activation(dnf[:, 12 + 2 * r:14 + 2 * r, :], prod[:], ACT.Silu).then_inc(conv_out, 1)
        walk(act, "z", z_body)

    def dve_conv(dve):
        def body(s, slot, r, ahead):
            dve.wait_ge(conv_center, 2 * r + 2)
            for side, (dst, src, tap) in enumerate(((slice(1, SEQ), slice(0, SEQ - 1), 0), (slice(0, SEQ - 1), slice(1, SEQ), 2))):
                for u in range(2):
                    out = prod[:, u, :].rearrange("p (a t) -> p a t", a=2)[:, :, dst]
                    tap_w = conv_w[:, bass.ds(2 * r + u, 1), tap:tap + 1].rearrange("p a b -> p (a b)")
                    last = dve.scalar_tensor_tensor(
                        out=out, in0=ps[:, 2 * slot + u, :].rearrange("p (a t) -> p a t", a=2)[:, :, src],
                        scalar=tap_w, in1=out, op0=ALU.mult, op1=ALU.add)
                if side == 0:
                    order_v.inc(last)
                    order_v.wait_by(dve)
            last.then_inc(acc_free, 1)
            if ahead:
                split_lo(dve, s + 2, slot, ahead)
        walk(dve, "conv", body, tallies=((order_v, 2),))

        def z_body(s, slot, r, ahead):
            dve.wait_ge(step_done, s + 1)
            dve.wait_ge(conv_out, 6 + r)
            dve.tensor_copy(prod[:], ps[:, 2 * slot:2 * slot + 2, :]).then_inc(acc_free, 1)
            if r == 0:
                split_lo(dve, s + 2, slot, ahead)
        walk(dve, "z", z_body)

    def pe_ab16(pe):
        s, slot = S_AB, S_AB % 2
        pe_ready(pe, s)
        for t in range(NT):
            tt = slice(t * P, (t + 1) * P)
            for k in range(KD):
                kk = slice(16 * k, 16 * k + 16)
                out = ps[:, 2 * slot, 16 * t:16 * t + 16]
                pe.matmul(out, h_lo[:, k, tt], w_hi[slot][:, kk], start=t == 0 and k == 0, stop=False,
                          skip_group_check=True)
                pe.matmul(out, h_hi[:, k, tt], w_lo[slot][:, kk], start=False, stop=False, skip_group_check=True)
                mm = pe.matmul(out, h_hi[:, k, tt], w_hi[slot][:, kk], start=False, stop=k == KD - 1,
                               skip_group_check=True)
        mm.then_inc(step_done, 1)

    def dve_gates(dve):
        dve.wait_ge(step_done, S_AB + 1)
        dve.tensor_copy(ab_raw[:].rearrange("p t n -> p (t n)"), ps[:, 2 * (S_AB % 2), 0:64]).then_inc(acc_free, 1)
        dve.wait_ge(acc_free, S_AB + 3)
        y = G_Y.rearrange("p (t n) -> p t n", t=NT)
        order_v.inc(dve.tensor_tensor(y, ab_raw[:, :, 0:8], gate_in[:, 1, :].rearrange("p (t n) -> p t n", t=NT), ALU.add))
        order_v.wait_by(dve)
        dve_softplus(dve, G_Y, G_OUT, 32, 1)
        dve.wait_ge(gate_exp, 1)
        dve.scalar_tensor_tensor(out=log_decay, in0=G_OUT, scalar=-1.0, in1=ab_tok, op0=ALU.mult, op1=ALU.mult)
        order_v.inc(dve.tensor_scalar(g_tmp, g_tmp, 1.0, None, ALU.add))
        order_v.wait_by(dve)
        dve.reciprocal(beta, g_tmp).then_inc(gates_ready, 1)
        dve.wait_ge(qk_rooted, 1)
        dve.reciprocal(qk_inv[:], qk_root[:]).then_inc(qk_inverse, 1)
        dve.wait_ge(qk_inverse, 1)
        order_v.inc(dve.tensor_scalar(qk_inv[:, 0], qk_inv[:, 0], P ** -0.5, None, ALU.mult))
        order_v.wait_by(dve)
        for d in range(2):
            dve.memset(state[d][:], 0.0).then_inc(sem("state_zero"), 1)
        for t in range(NT):
            dve.wait_ge(kv_turned, t + 1)
            dve.tensor_tensor(k_tok[:, t], ps[:, t % 2, :].rearrange("p (h d) -> p h d", h=4),
                              spread(qk_inv[:, 1, t, :], P), ALU.mult).then_inc(k_tok_done, 1)

    def act_gates(act):
        act.wait_ge(step_done, S_AB + 1)
        act.dma_start(levels[:], a["levels"]).then_inc(levels_ready, 16)
        act_softplus(act, 32, 1)
        act.wait_ge(acc_free, S_AB + 3)
        act.activation(ab_tok, gate_in[:, 0, :], ACT.Exp)
        act.activation(g_tmp.rearrange("p (t n) -> p t n", t=NT), ab_raw[:, :, 8:16], ACT.Exp, scale=-1.0) \
           .then_inc(gate_exp, 1)
        act.wait_ge(conv_out, 8)
        act.activation(dn_sq[:], dn[:, 0:2], ACT.Square).then_inc(qk_squared, 1)
        act.wait_ge(qk_summed, 1)
        act.activation(qk_root[:].rearrange("p w t h -> p (w t h)"), ps[:, NRM, 0:32], ACT.Sqrt,
                       bias=vecs[:, 2:3]).then_inc(qk_rooted, 1)
        for t in range(NT):
            act.wait_ge(kv_turned, t + 1)
            act.activation(v_tok[:, t].rearrange("p h d -> p (h d)"), ps[:, 2 + t % 2, :], ACT.Copy) \
               .then_inc(v_tok_done, 1)
            act.wait_ge(k_back, t + 1)
            act.activation(dn[:, 1, :, t * P:(t + 1) * P], ps[:, 5 + t % 2, :].rearrange("p (h d) -> p h d", h=4),
                           ACT.Copy).then_inc(k_feat_done, 1)

    def pe_gates(pe):
        pe.wait_ge(qk_squared, 1)
        for w in range(2):
            for t in range(NT):
                for h in range(DNH):
                    col = 16 * w + 4 * t + h
                    mm = pe.matmul(ps[:, NRM, col:col + 1], dn_sq[:, w, h, t * P:(t + 1) * P], ones[:, 0:1],
                                   start=col == 0, stop=True, skip_group_check=True)
        mm.then_inc(qk_summed, 1)
        pe.wait_ge(acc_free, S_AB + 3)
        for t in range(NT):
            tt = slice(t * P, (t + 1) * P)
            if t >= 2:
                pe.wait_ge(k_tok_done, t - 1)
                pe.wait_ge(v_tok_done, t - 1)
            for h in range(DNH):
                pe.transpose(ps[:, t % 2, h * P:(h + 1) * P], dn[:, 1, h, tt], ident)
            for h in range(DNH):
                mm = pe.transpose(ps[:, 2 + t % 2, h * P:(h + 1) * P], dn[:, 2, h, tt], ident)
            mm.then_inc(kv_turned, 1)
            pe.wait_ge(k_tok_done, t + 1)
            if t >= 2:
                pe.wait_ge(k_feat_done, t - 1)
            for h in range(DNH):
                mm = pe.transpose(ps[:, 5 + t % 2, h * P:(h + 1) * P], k_tok[:, t, h, :], ident)
            mm.then_inc(k_back, 1)

    inverse = [f"{n}{l}" for l in range(1, LEVELS) for n in ("X", "TU")]
    PE_ST = stages(["G", "KK", "QK", "X0"] + inverse + ["W", "V", "O", "S"])
    ACT_ST = stages(["GC", "EG", "EL", "EC", "DEC", "DC"] + [f"X{l}" for l in range(1, LEVELS)] + ["WN"])
    DVE_ST = stages(["CUT", "DSUB", "SYS", "QKM", "M0", "T0", "U0", "M1"]
                    + [f"{n}{l + 1 if n == 'M' else l}" for l in range(1, LEVELS - 1) for n in ("M", "T", "U")]
                    + ["KEG", "QE", "KDEC", "U6", "VN", "OUT", "ST"])
    dn_pe = [sem(f"dn_products{d}") for d in range(2)]
    dn_act = [sem(f"dn_scalar{d}") for d in range(2)]
    dn_dve = [sem(f"dn_vector{d}") for d in range(2)]
    staged = [sem(f"dn_staged{d}") for d in range(2)]
    CUTS, TRIS = (C_CUTF, C_CUTB), (C_TRIF, C_TRIB)
    LAST = (P - 1, 0)

    def need(eng, which, table, d, it, stage):
        eng.wait_ge(which[d], it * len(table) + table[stage])

    def chunk(d, stream, b):
        return 2 * stream + (b if d == 0 else 1 - b)

    def heads(buf):
        return buf[:].rearrange("p h d -> p (h d)")

    def joined(ap, l, side):
        return ap.rearrange("p (n s b) -> p n s b", s=2, b=1 << l)[:, :, side, :]

    def bank(n, d):
        return ps[:, 2 * n + d, :]

    def bank4(n, d):
        return bank(n, d).rearrange("p (h d) -> p h d", h=4)

    def pool_deltanet(pool):
        pool.wait_ge(k_feat_done, NT)
        pool.wait_ge(gates_ready, 1)
        for stream in range(2):
            for b in range(2):
                it = 2 * stream + b
                for d in range(2):
                    tt = chunk(d, stream, b)
                    if it:
                        pool.wait_ge(dn_dve[d], it * len(DVE_ST))
                    pool.tensor_copy(k_stage[d][:], dn[:, 1, :, bass.ds(tt * P, P)]).then_inc(staged[d], 1)
                    pool.tensor_copy(la_stage[:, d, :], log_decay[:, bass.ds(tt * 8 + 4 * d, 4)]).then_inc(staged[d], 1)

    def pe_deltanet(pe):
        pe.wait_ge(qk_inverse, 1)
        pe.wait_ge(k_feat_done, NT)
        pe.wait_ge(sem("state_zero"), 2)
        with pe.Fori(0, 2) as stream:
            for b in range(2):
                it = 2 * stream + b
                for d in range(2):
                    pe.wait_ge(staged[d], 2 * it + 2)
                    for h in range(DNH):
                        pe.matmul(bank(0, d)[:, h * P:(h + 1) * P], la_stage[:, d, h:h + 1].to_broadcast([P, P]),
                                  c_(TRIS[d]), start=True, stop=True)
                    pe.matmul(bank(1, d)[:, 0:4], c_(TRIS[d]), la_stage[:, d, :], start=True, stop=True) \
                      .then_inc(dn_pe[d], 1)
                for d in range(2):
                    for h in range(DNH):
                        mm = pe.matmul(bank(2, d)[:, h * P:(h + 1) * P], k_stage[d][:, h, :], k_stage[d][:, h, :],
                                       start=True, stop=True)
                    mm.then_inc(dn_pe[d], 1)
                    for h in range(DNH):
                        mm = pe.matmul(bank(3, d)[:, h * P:(h + 1) * P], k_stage[d][:, h, :],
                                       dn[:, 0, h, bass.ds(chunk(d, stream, b) * P, P)], start=True, stop=True)
                    mm.then_inc(dn_pe[d], 1)
                for l in range(LEVELS):
                    for d in range(2):
                        need(pe, dn_dve, DVE_ST, d, it, "M0" if l == 0 else "M1" if l == 1 else f"U{l - 1}")
                        for h in range(DNH):
                            mm = pe.matmul(bank(0, d)[:, h * P:(h + 1) * P], cut_t[d][:, h, :],
                                           ident if l == 0 else inv_n[d][:, h, :], start=True, stop=True)
                        mm.then_inc(dn_pe[d], 1)
                    for d in range(2):
                        if l == 0:
                            continue
                        need(pe, dn_act, ACT_ST, d, it, f"X{l}")
                        for h in range(DNH):
                            if l < LEVELS - 1:
                                pe.matmul(joined(bank4(1, d)[:, h], l, d), inv_t[d][:, h, :],
                                          joined(xbuf[d][:, h], l, d), start=True, stop=True)
                            mm = pe.matmul(joined(bank4(2, d)[:, h], l, 1 - d), xbuf[d][:, h, :],
                                           joined(inv_t[d][:, h], l, 1 - d), start=True, stop=True)
                        mm.then_inc(dn_pe[d], 1)
                for d in range(2):
                    need(pe, dn_dve, DVE_ST, d, it, "U6")
                    for h in range(DNH):
                        mm = pe.matmul(bank(0, d)[:, h * P:(h + 1) * P], inv_n[d][:, h, :], inv_t[d][:, h, :],
                                       start=True, stop=True)
                    mm.then_inc(dn_pe[d], 1)
                for d in range(2):
                    tt = chunk(d, stream, b)
                    need(pe, dn_act, ACT_ST, d, it, "WN")
                    for h in range(DNH):
                        out = bank(1, d)[:, h * P:(h + 1) * P]
                        pe.matmul(out, inv_t[d][:, h, :], v_tok[:, bass.ds(tt, 1), h, :].rearrange("p a d -> p (a d)"),
                                  start=True, stop=False)
                        mm = pe.matmul(out, xbuf[d][:, h, :], state[d][:, h, :], start=False, stop=True)
                    mm.then_inc(dn_pe[d], 1)
                for d in range(2):
                    need(pe, dn_dve, DVE_ST, d, it, "VN")
                    for h in range(DNH):
                        out = bank(2, d)[:, h * P:(h + 1) * P]
                        pe.matmul(out, cut_t[d][:, h, :], state[d][:, h, :], start=True, stop=False)
                        mm = pe.matmul(out, gram_t[d][:, h, :], v_new[d][:, h, :], start=False, stop=True)
                    mm.then_inc(dn_pe[d], 1)
                    for h in range(DNH):
                        mm = pe.matmul(bank(3, d)[:, h * P:(h + 1) * P], sys_t[d][:, h, :], v_new[d][:, h, :],
                                       start=True, stop=True)
                    mm.then_inc(dn_pe[d], 1)

    def act_deltanet(act):
        with act.Fori(0, 2) as stream:
            for b in range(2):
                it = 2 * stream + b
                for d in range(2):
                    s = dsm[:, d]
                    need(act, dn_pe, PE_ST, d, it, "G")
                    act.activation(s[:, 0], bank(1, d)[:, 0:4], ACT.Copy).then_inc(dn_act[d], 1)
                    act.activation(heads(v_new[d]), bank(0, d), ACT.Exp).then_inc(dn_act[d], 1)
                    act.activation(s[:, 4], bank4(0, d)[:, :, LAST[d]], ACT.Exp).then_inc(dn_act[d], 1)
                    need(act, dn_act, ACT_ST, d, it, "GC")
                    act.activation(s[:, 1], s[:, 0], ACT.Exp).then_inc(dn_act[d], 1)
                for d in range(2):
                    s = dsm[:, d]
                    need(act, dn_dve, DVE_ST, d, it, "CUT")
                    act.activation(heads(delta_t[d]), heads(delta_t[d]), ACT.Exp).then_inc(dn_act[d], 1)
                    need(act, dn_dve, DVE_ST, d, it, "DSUB")
                    act.activation(s[:, 3], s[:, 2], ACT.Exp).then_inc(dn_act[d], 1)
                for l in range(1, LEVELS):
                    for d in range(2):
                        need(act, dn_pe, PE_ST, d, it, f"X{l}")
                        act.activation(heads(xbuf[d]), bank(0, d), ACT.Copy).then_inc(dn_act[d], 1)
                for d in range(2):
                    need(act, dn_pe, PE_ST, d, it, "W")
                    act.activation(heads(xbuf[d]), bank(0, d), ACT.Copy, scale=-1.0).then_inc(dn_act[d], 1)

    def dve_deltanet(dve):
        dve.wait_ge(levels_ready, 16)
        with dve.Fori(0, 2) as stream:
            for b in range(2):
                it = 2 * stream + b

                def beta_of(d, h):
                    return beta[:, bass.ds(chunk(d, stream, b) * 8 + 4 * d + h, 1)]

                for d in range(2):
                    s = dsm[:, d]
                    need(dve, dn_act, ACT_ST, d, it, "EL")
                    for h in range(DNH):
                        last = dve.scalar_tensor_tensor(out=delta_t[d][:, h, :], in0=bank4(0, d)[:, h, :],
                                                        scalar=s[:, 0, h:h + 1], in1=c_(CUTS[d]),
                                                        op0=ALU.subtract, op1=ALU.min)
                    last.then_inc(dn_dve[d], 1)
                    dve.tensor_tensor(s[:, 2], bank4(0, d)[:, :, LAST[d]], s[:, 0], ALU.subtract).then_inc(dn_dve[d], 1)
                for d in range(2):
                    need(dve, dn_act, ACT_ST, d, it, "DEC")
                    need(dve, dn_pe, PE_ST, d, it, "QK")
                    for h in range(DNH):
                        last = dve.scalar_tensor_tensor(out=sys_t[d][:, h, :], in0=bank4(2, d)[:, h, :],
                                                        scalar=beta_of(d, h), in1=delta_t[d][:, h, :],
                                                        op0=ALU.mult, op1=ALU.mult)
                    last.then_inc(dn_dve[d], 1)
                    dve.tensor_tensor(heads(gram_t[d]), bank(3, d), heads(delta_t[d]), ALU.mult).then_inc(dn_dve[d], 1)
                    need(dve, dn_dve, DVE_ST, d, it, "SYS")
                    dve_mask(dve, d, 0)
                for d in range(2):
                    need(dve, dn_pe, PE_ST, d, it, "X0")
                    dve.tensor_tensor(inv_n[d][:], over(ident, 4), bank4(0, d), ALU.subtract).then_inc(dn_dve[d], 1)
                    dve.tensor_tensor(inv_t[d][:], over(ident, 4), cut_t[d][:], ALU.subtract).then_inc(dn_dve[d], 1)
                    need(dve, dn_dve, DVE_ST, d, it, "U0")
                    dve_mask(dve, d, 1)
                for l in range(1, LEVELS - 1):
                    for d in range(2):
                        need(dve, dn_pe, PE_ST, d, it, f"X{l}")
                        dve_mask(dve, d, l + 1)
                    for d in range(2):
                        need(dve, dn_pe, PE_ST, d, it, f"TU{l}")
                        n, t = joined(heads(inv_n[d]), l, d), joined(heads(inv_t[d]), l, 1 - d)
                        dve.tensor_tensor(n, n, joined(bank(1, d), l, d), ALU.subtract).then_inc(dn_dve[d], 1)
                        dve.tensor_tensor(t, t, joined(bank(2, d), l, 1 - d), ALU.subtract).then_inc(dn_dve[d], 1)
                for d in range(2):
                    s, tt = dsm[:, d], chunk(d, stream, b)
                    kt = k_tok[:, bass.ds(tt, 1)].rearrange("p a h d -> p (a h) d")
                    need(dve, dn_pe, PE_ST, d, it, "X6")
                    need(dve, dn_act, ACT_ST, d, it, "DC")
                    dve.tensor_tensor(inv_n[d][:], kt, spread(s[:, 1], P), ALU.mult).then_inc(dn_dve[d], 1)
                    dve.tensor_tensor(cut_t[d][:], dn[:, 0, :, bass.ds(tt * P, P)], v_new[d][:], ALU.mult) \
                       .then_inc(dn_dve[d], 1)
                    dve.tensor_tensor(sys_t[d][:], kt, spread(s[:, 3], P), ALU.mult).then_inc(dn_dve[d], 1)
                    need(dve, dn_pe, PE_ST, d, it, "TU6")
                    t = joined(heads(inv_t[d]), LEVELS - 1, 1 - d)
                    dve.tensor_tensor(t, t, joined(bank(2, d), LEVELS - 1, 1 - d), ALU.subtract).then_inc(dn_dve[d], 1)
                for d in range(2):
                    tt = chunk(d, stream, b)
                    need(dve, dn_pe, PE_ST, d, it, "V")
                    dve.tensor_tensor(v_new[d][:], bank4(1, d), spread(beta[:, bass.ds(tt * 8 + 4 * d, 4)], P),
                                      ALU.mult).then_inc(dn_dve[d], 1)
                for d in range(2):
                    tt = chunk(d, stream, b)
                    o = dn_o[:, bass.ds(tt, 1)].rearrange("p a h d -> p (a h) d")
                    need(dve, dn_pe, PE_ST, d, it, "O")
                    if b == 0:
                        dve.tensor_copy(o, bank4(2, d)).then_inc(dn_dve[d], 1)
                    else:
                        need(dve, dn_dve, DVE_ST, 1 - d, it - 1, "OUT")
                        dve.tensor_tensor(o, o, bank4(2, d), ALU.add).then_inc(dn_dve[d], 1)
                    need(dve, dn_pe, PE_ST, d, it, "S")
                    for h in range(DNH):
                        last = dve.scalar_tensor_tensor(out=state[d][:, h, :], in0=state[d][:, h, :],
                                                        scalar=dsm[:, d, 4, h:h + 1], in1=bank4(3, d)[:, h, :],
                                                        op0=ALU.mult, op1=ALU.add)
                    last.then_inc(dn_dve[d], 1)

    def dve_mask(dve, d, l):
        m = levels[:, (d * LEVELS + l) * P:(d * LEVELS + l + 1) * P]
        dve.tensor_tensor(cut_t[d][:], sys_t[d][:], over(m, 4), ALU.mult).then_inc(dn_dve[d], 1)

    merged, merge_squared, merge_rooted = sem("merged"), sem("merge_squared"), sem("merge_rooted")
    merge_scaled, merge_turned = sem("merge_scaled"), sem("merge_turned")
    merge_dn, merge_df, y_hi_done, y_lo_done = sem("merge_dn"), sem("merge_df"), sem("y_hi_done"), sem("y_lo_done")
    merge_sum = sem("merge_sum")

    def act_merge(act):
        for t in range(NT):
            ms = merge_s[:, t]
            act.wait_ge(merged, t + 1)
            act.activation(merge_sq[:], merge_o[:], ACT.Square).then_inc(merge_squared, 1)
            act.wait_ge(merge_sum, t + 1)
            act.activation(ms[:, 8:16], ms[:, 0:8], ACT.Sqrt, bias=vecs[:, 2:3], scale=1.0 / P) \
               .then_inc(merge_rooted, 1)
            act.wait_ge(merge_turned, t + 1)
            act.activation(y_f[:, 4:8, t * P:(t + 1) * P],
                           ps[:, 2 * (t % 2) + 1, :].rearrange("p (h d) -> p h d", h=4), ACT.Copy,
                           scale=vecs[:, 1:2]).then_inc(merge_df, 1)
        act.wait_ge(merge_df, NT)
        act.wait_ge(merge_dn, NT)
        for c in range(KD):
            act.activation(h_hi[:, c, :], y_f[:, c, :], ACT.Copy).then_inc(y_hi_done, 1)

    def dve_merge(dve):
        for d in range(2):
            dve.wait_ge(dn_dve[d], 4 * len(DVE_ST))
        for t in range(NT):
            ms = merge_s[:, t]
            if t:
                dve.wait_ge(merge_turned, t)
            dve.tensor_tensor(merge_o[:, 0:4], dn_o[:, t], spread(qk_inv[:, 0, t, :], P), ALU.mult)
            dve.tensor_copy(merge_o[:, 4:8], df_o[:, t]).then_inc(merged, 1)
            dve.wait_ge(merge_squared, t + 1)
            dve.tensor_reduce(ms[:, 0:8], merge_sq[:], AX.X, ALU.add).then_inc(merge_sum, 1)
            dve.wait_ge(merge_rooted, t + 1)
            order_v.inc(dve.reciprocal(ms[:, 16:24], ms[:, 8:16]))
            order_v.wait_by(dve)
            dve.tensor_tensor(merge_o[:], merge_o[:], spread(ms[:, 16:24], P), ALU.mult).then_inc(merge_scaled, 1)
            dve.wait_ge(merge_turned, t + 1)
            dve.scalar_tensor_tensor(out=y_f[:, 0:4, t * P:(t + 1) * P],
                                     in0=ps[:, 2 * (t % 2), :].rearrange("p (h d) -> p h d", h=4),
                                     scalar=vecs[:, 0:1], in1=dn[:, 3, :, t * P:(t + 1) * P],
                                     op0=ALU.mult, op1=ALU.mult).then_inc(merge_dn, 1)
        dve.wait_ge(merge_dn, NT)
        for c in range(KD):
            dve.wait_ge(y_hi_done, c + 1)
            dve.tensor_tensor(h_lo[:, c, :], y_f[:, c, :], h_hi[:, c, :].bitcast(F32), ALU.subtract) \
               .then_inc(y_lo_done, 1)

    def pe_merge(pe):
        for t in range(NT):
            pe.wait_ge(merge_scaled, t + 1)
            if t >= 2:
                pe.wait_ge(merge_dn, t - 1)
                pe.wait_ge(merge_df, t - 1)
            for h in range(8):
                mm = pe.transpose(ps[:, 2 * (t % 2) + h // 4, (h % 4) * P:(h % 4 + 1) * P], merge_o[:, h, :], ident)
            mm.then_inc(merge_turned, 1)
        pe.wait_ge(y_lo_done, KD)
        pe.wait_ge(merge_df, NT)

    def pe_ab(pe):
        pe_pairs(pe, "diff", ALL, norm="n01")
        pe_diff(pe)
        pe_pairs(pe, "conv", ALL)
        pe_pairs(pe, "z", ALL)
        pe_ab16(pe)
        pe_gates(pe)
        pe_deltanet(pe)
        pe_merge(pe)

    def act_ab(act):
        act_plain(act, "diff")
        act_diff(act)
        act_conv(act)
        act_gates(act)
        act_deltanet(act)
        act_merge(act)
        act.wait_ge(merge_dn, NT)
        for s in (S_AB + 1, S_AB + 2):
            split_hi(act, s, s % 2, ELEMS[s])

    def dve_ab(dve):
        def body(s, slot, r, ahead):
            dve.wait_ge(step_done, s + 1)
            dve.tensor_copy(df[:, bass.ds(2 * r, 2), :], ps[:, 2 * slot:2 * slot + 2, :]).then_inc(acc_free, 1)
            if ahead:
                split_lo(dve, s + 2, slot, ahead)
        walk(dve, "diff", body)
        dve_diff(dve)
        dve_conv(dve)
        dve_gates(dve)
        dve_deltanet(dve)
        dve_merge(dve)
        for s in (S_AB + 1, S_AB + 2):
            split_lo(dve, s, s % 2, ELEMS[s])

    rcopied, rrot, rroped = sem("ret_copied"), sem("ret_rotated"), sem("ret_roped")
    v_turned, v_placed = sem("ret_v_turned"), sem("ret_v_placed")
    g_placed = sem("ret_g_placed")
    tables_ready, decays_ready = sem("tables_ready"), sem("decays_ready")
    lg, _ = put("lg", [P, 32])
    rs, _ = put("rs", [P, 2, 6])
    r_staged, r_exps, r_decayed = sem("ret_staged"), sem("ret_exps"), sem("ret_decayed")
    r_scores, r_weighed, r_mixed = sem("ret_scores"), sem("ret_weighed"), sem("ret_mixed")
    r_squared, r_rooted, r_inverse, r_scaled = (sem(f"ret_{n}") for n in ("squared", "rooted", "inverse", "scaled"))
    r_turned, r_gated, r_hi, r_lo = (sem(f"ret_{n}") for n in ("turned", "gated", "hi", "lo"))
    r_halves = sem("ret_halves")
    LEAD, LAG = 1, 2

    def head_slots(eng, body):
        def straight(h):
            body(h, h % 2, lambda g: 0 <= h + g < RH)
        for h in range(-LEAD, LAG):
            straight(h)
        with eng.Fori(0, (RH - LEAD - LAG) // 2) as i:
            for b in range(2):
                body(2 * i + LAG + b, b, lambda g: True)
        for h in range(LAG + (RH - LEAD - LAG) // 2 * 2, RH + LAG):
            straight(h)

    sil2 = [sil[:, i, :].rearrange("p (a t) -> p a t", a=2) for i in range(2)]
    prod2 = [prod[:, i, :].rearrange("p (a t) -> p a t", a=2) for i in range(2)]
    S_RQ, S_RV, S_RG = R["retq"][1], R["retv"][1], R["retg"][1]
    COS_R, SIN_R = rc[:, 10 * SEQ:11 * SEQ], rc[:, 11 * SEQ:12 * SEQ]

    def pool_retention(pool):
        pool.wait_ge(ada_dot, 2 * NADA)
        pool.dma_start(rc[:], a["ret_tables"]).then_inc(tables_ready, 16)
        pool.wait_ge(rroped, 8)
        pool.wait_ge(step_done, S_RG + 8)
        with pool.Fori(0, RH // 2) as i:
            for b in range(2):
                pool.tensor_copy(r_kst[b][:], rk[:, bass.ds(2 * i + b, 1), :].rearrange("p a t -> p (a t)")) \
                    .then_inc(r_staged, 1)
            pool.wait_ge(r_scores, 2 * i + 2)

    def pe_rotate(pe, s, slot, r):
        pe.wait_ge(acc_free, s + 3)
        pe.matmul(ps[:, 5 + slot, :], c_(C_ROTR), sil[:, slot, :], start=True, stop=True).then_inc(rrot, 1)

    def pe_ret(pe):
        def lagged(name, cols, follow):
            s0, n = R[name][1], R[name][2]

            def body(s, slot, r, ahead):
                pair_products(pe, s, slot, cols, "n11" if name == "retq" and isinstance(r, int) and r == 0 else None)
                if not (isinstance(r, int) and r == 0):
                    follow(s - 1, 1 - slot, r - 1)
            walk(pe, name, body, skip=2)
            follow(s0 + n - 1, (s0 + n - 1) % 2, n - 1)

        lagged("retq", LAT, lambda s, slot, r: pe_rotate(pe, s, slot, r))
        lagged("retk", ALL, lambda s, slot, r: pe_rotate(pe, s, slot, r))

        def turn_v(s, slot, r):
            pe.wait_ge(acc_free, s + 3)
            if not (isinstance(r, int) and r == 0):
                pe.wait_ge(v_placed, r)
            else:
                pe.wait_ge(rroped, 8)
            for u in range(2):
                for t in range(NT):
                    mm = pe.transpose(ps[:, 5 + t // 2, (t % 2) * 256 + u * P:(t % 2) * 256 + (u + 1) * P],
                                      sil[:, u, t * P:(t + 1) * P], ident)
            mm.then_inc(v_turned, 1)
        lagged("retv", ALL, turn_v)
        pe_pairs(pe, "retg", LAT)
        pe.wait_ge(acc_free, S_RG + 8 + 2)

        def body(h, b, has):
            if has(1):
                pe.wait_ge(r_staged, h + 2)
                if has(-1):
                    pe.wait_ge(r_weighed, h)
                for kt in range(NT):
                    mm = pe.matmul(ps[:, 2 * (1 - b) + kt // 2, (kt % 2) * 256:(kt % 2 + 1) * 256],
                                   r_kst[1 - b][:, kt * P:(kt + 1) * P],
                                   rq[:, bass.ds(h + 1, 1), :].rearrange("p a t -> p (a t)"), start=True, stop=True)
                mm.then_inc(r_scores, 1)
            if has(0):
                pe.wait_ge(r_weighed, h + 1)
                if has(-2):
                    pe.wait_ge(r_scaled, h - 1)
                for qt in range(2):
                    for kt in range(NT):
                        mm = pe.matmul(ps[:, 4 + b, qt * 256:(qt + 1) * 256],
                                       r_probs[b][:, kt * 256 + qt * P:kt * 256 + (qt + 1) * P],
                                       rv[:, kt, bass.ds(h * 256, 256)], start=kt == 0, stop=kt == NT - 1)
                mm.then_inc(r_mixed, 1)
            if has(-1):
                pe.wait_ge(r_scaled, h)
                for f in range(2):
                    for qt in range(2):
                        mm = pe.transpose(ps[:, 7 - b, f * 256 + qt * P:f * 256 + (qt + 1) * P],
                                          prod[:, 1 - b, qt * 256 + f * P:qt * 256 + (f + 1) * P], ident)
                mm.then_inc(r_turned, 1)
        head_slots(pe, body)

    def act_ret(act):
        act_plain(act, "retq")
        act_plain(act, "retk")

        def v_body(s, slot, r, ahead):
            if ahead:
                split_hi(act, s + 2, slot, ahead)
            if not (isinstance(r, int) and r == 0):
                place_v(r - 1)

        def place_v(r):
            act.wait_ge(v_turned, r + 1)
            act.activation(rv[:, :, bass.ds(r * 256, 256)],
                           ps[:, 5:7, :].rearrange("p b (t n) -> p (b t) n", t=2), ACT.Copy).then_inc(v_placed, 1)
        walk(act, "retv", v_body, skip=2)
        place_v(7)

        def g_body(s, slot, r, ahead):
            if ahead:
                split_hi(act, s + 2, slot, ahead)
            act.wait_ge(acc_free, s + 3)
            act.activation(rg[:, bass.ds(2 * r, 2), :], sil2[0 if slot == S_RG % 2 else 1], ACT.Silu) \
               .then_inc(g_placed, 1)
        walk(act, "retg", g_body)
        act_softplus(act, 16, 2)
        act.wait_ge(decays_ready, 1)
        act.wait_ge(tables_ready, 16)

        def body(h, b, has):
            if has(1):
                if has(-1):
                    act.wait_ge(r_weighed, h)
                lf, lb = lg[:, bass.ds(h + 1, 1)], lg[:, bass.ds(9 + h, 1)]
                dec, back = r_decay[1 - b], r_back[1 - b]
                act.activation(dec[:, 512:1024], rc[:, 0:512], ACT.Exp, scale=lf)
                act.activation(back[:, 512:1024], rc[:, 0:512], ACT.Exp, scale=lb).then_inc(r_exps, 1)
                act.activation(dec[:, 0:512], rc[:, 1536:2048], ACT.Exp, scale=lf)
                act.activation(back[:, 0:512], rc[:, 2048:2560], ACT.Exp, scale=lb).then_inc(r_exps, 1)
            if has(-2):
                act.wait_ge(r_gated, h - 1)
                act.activation(ry_hi[:, bass.ds(2 * h - 4, 2), :], sil2[b], ACT.Copy).then_inc(r_hi, 1)
            if has(0):
                act.wait_ge(r_mixed, h + 1)
                if has(-1):
                    act.wait_ge(r_squared, h)
                if has(-2):
                    act.wait_ge(r_inverse, h - 1)
                for qt in range(2):
                    last = act.activation(r_square[:, qt * 256:(qt + 1) * 256], ps[:, 4 + b, qt * 256:(qt + 1) * 256],
                                          ACT.Square, accum_out=rs[:, b, qt:qt + 1])
                last.then_inc(r_squared, 1)
                act.wait_ge(r_squared, h + 1)
                act.activation(rs[:, b, 2:4], rs[:, b, 0:2], ACT.Sqrt, bias=vecs[:, 2:3], scale=1.0 / 256) \
                   .then_inc(r_rooted, 1)
        head_slots(act, body)

    def dve_ret(dve):
        def rope(r, slot, out, total):
            dve.wait_ge(rrot, total + r + 1)
            dve.tensor_tensor(prod2[slot], ps[:, 5 + slot, :].rearrange("p (a t) -> p a t", a=2), over(SIN_R, 2), ALU.mult)
            order_v.inc(dve.tensor_tensor(out, sil2[slot], over(COS_R, 2), ALU.mult))
            order_v.wait_by(dve)
            dve.tensor_tensor(out, out, prod2[slot], ALU.add).then_inc(rroped, 1)

        def q_out(r):
            return rq[:, bass.ds(2 * r, 2), :]

        def k_out(r):
            return rk[:, bass.ds(2 * r, 2), LAT]

        dve.wait_ge(tables_ready, 16)
        for name, out, total in (("retq", q_out, 0), ("retk", k_out, 4)):
            s0, n = R[name][1], R[name][2]

            def body(s, slot, r, ahead):
                dve.wait_ge(step_done, s + 1)
                if name == "retk":
                    dve.tensor_copy(rk[:, bass.ds(2 * r, 2), CTX], ps[:, 2 * slot:2 * slot + 2, CTX])
                dve.tensor_copy(sil2[slot], ps[:, 2 * slot:2 * slot + 2, LAT]).then_inc(acc_free, 1)
                if ahead:
                    split_lo(dve, s + 2, slot, ahead)
                if r >= 1:
                    rope(r - 1, 1 - slot, out(r - 1), total)
            for r in range(n):
                s = s0 + r
                body(s, s % 2, r, ELEMS[s + 2])
            rope(n - 1, (s0 + n - 1) % 2, out(n - 1), total)

        def v_body(s, slot, r, ahead):
            dve.wait_ge(step_done, s + 1)
            if not (isinstance(r, int) and r == 0):
                dve.wait_ge(v_turned, r)
            else:
                dve.wait_ge(rroped, 8)
            dve.tensor_copy(sil[:], ps[:, 2 * slot:2 * slot + 2, :]).then_inc(acc_free, 1)
            if ahead:
                split_lo(dve, s + 2, slot, ahead)
        walk(dve, "retv", v_body, skip=2)

        def g_body(s, slot, r, ahead):
            dve.wait_ge(step_done, s + 1)
            if isinstance(r, int) and r == 0:
                dve.wait_ge(v_turned, 8)
            if not (isinstance(r, int) and r < 2):
                dve.wait_ge(g_placed, r - 1)
            dve.tensor_copy(sil2[0 if slot == S_RG % 2 else 1], ps[:, 2 * slot:2 * slot + 2, LAT]).then_inc(acc_free, 1)
            if ahead:
                split_lo(dve, s + 2, slot, ahead)
        walk(dve, "retg", g_body, skip=2)
        order_v.inc(dve.tensor_scalar(G_Y[:, 0:16], small[:, 0:16], -1.0, None, ALU.mult))
        order_v.wait_by(dve)
        dve_softplus(dve, G_Y[:, 0:16], lg[:, 16:32], 16, 2)
        dve.tensor_scalar(lg[:, 0:16], lg[:, 16:32], -1.0, None, ALU.mult).then_inc(decays_ready, 1)

        def body(h, b, has):
            if has(-1):
                r = rs[:, 1 - b]
                dve.wait_ge(r_rooted, h)
                dve.reciprocal(r[:, 4:6], r[:, 2:4]).then_inc(r_inverse, 1)
                dve.wait_ge(r_inverse, h)
                for qt in range(2):
                    last = dve.tensor_scalar(prod[:, 1 - b, qt * 256:(qt + 1) * 256],
                                             ps[:, 5 - b, qt * 256:(qt + 1) * 256], r[:, 4 + qt:5 + qt], None, ALU.mult)
                last.then_inc(r_scaled, 1)
            if has(-2):
                dve.wait_ge(r_turned, h - 1)
                dve.tensor_tensor(sil2[b], ps[:, 6 + b, :].rearrange("p (a t) -> p a t", a=2),
                                  rg[:, bass.ds(2 * h - 4, 2), :], ALU.mult).then_inc(r_gated, 1)
            if has(1):
                dec, back = r_decay[1 - b], r_back[1 - b]
                dve.wait_ge(r_exps, 2 * h + 3)
                dve.tensor_tensor(dec[:, 512:1024], dec[:, 512:1024], rc[:, 512:1024], ALU.mult)
                dve.tensor_tensor(back[:, 512:1024], back[:, 512:1024], rc[:, 1024:1536], ALU.mult) \
                   .then_inc(r_halves, 1)
                dve.wait_ge(r_exps, 2 * h + 4)
                dve.wait_ge(r_halves, h + 2)
                dve.tensor_tensor(dec[:], dec[:], back[:], ALU.add).then_inc(r_decayed, 1)
                dve.wait_ge(r_decayed, h + 2)
                dve.wait_ge(r_scores, h + 2)
                if has(-1):
                    dve.wait_ge(r_mixed, h)
                dve.scalar_tensor_tensor(out=r_probs[1 - b][:],
                                         in0=ps[:, 2 - 2 * b:4 - 2 * b, :].rearrange("p b t -> p (b t)"),
                                         scalar=P ** -0.5, in1=dec[:], op0=ALU.mult, op1=ALU.mult) \
                   .then_inc(r_weighed, 1)
            if has(-2):
                dve.wait_ge(r_hi, h - 1)
                dve.tensor_tensor(ry_lo[:, bass.ds(2 * h - 4, 2), :], sil2[b],
                                  ry_hi[:, bass.ds(2 * h - 4, 2), :].bitcast(F32), ALU.subtract).then_inc(r_lo, 1)
        head_slots(dve, body)

    with nc.Block() as block:
        @block.sync
        def _(sp):
            sp_program(sp)

        @block.gpsimd
        def _(pool):
            pool_program(pool)

        @block.scalar
        def _(act):
            scalar_program(act)

        @block.vector
        def _(dve):
            vector_program(dve)

        @block.tensor
        def _(pe):
            tensor_program(pe)


def lay_out(x, c, ctx, c_ctx, ada_w, ada_b, norm_w, final_norm_w, ffn_w_in, ffn_w_out, ab_w_in, ab_conv_w,
            dn_A_log, dn_dt_bias, dn_norm_w, diff_lambda, diff_subln_w, ab_w_out, ret_w_in, ret_decay_logit,
            ret_w_out):
    def columns(w, n):
        k = w.shape[0] // P
        return w.reshape(k, P, n, P).transpose(2, 1, 0, 3).reshape(n, P, k * P)

    def pairs(w, n):
        return columns(w, n).reshape(n // 2, 2, P, -1).transpose(0, 2, 1, 3).reshape(n // 2, P, -1)

    const, levels, ret = constants()
    tokens = np.concatenate([ctx[0], x[0]], axis=0)
    w = ab_w_in[0]
    return {
        "xT": tokens.T.reshape(KD, P, T).transpose(1, 0, 2),
        "c": c, "c_ctx": c_ctx,
        "ada": np.delete(ada_w.transpose(0, 2, 1).reshape(NADA, P, D), slice(KD, 2 * KD), axis=0),
        "ada0": ada_w[0, :, D:2 * D].reshape(KD, P, D),
        "c_cols": np.stack([c_ctx.reshape(KD, P), c.reshape(KD, P)], axis=-1).transpose(1, 0, 2).reshape(P, 2 * KD),
        "mbias": ada_b.reshape(NADA, P).T,
        "norm_g": np.concatenate([norm_w.reshape(6, D), final_norm_w[None]]).reshape(7, KD, P).transpose(2, 0, 1),
        "w_up": ffn_w_in.reshape(4, KD, P, 2, NF, P).transpose(0, 4, 2, 3, 1, 5).reshape(4, NF, P, 2 * D),
        "w_down": ffn_w_out.reshape(4, NF, P, KD, P).transpose(0, 3, 2, 1, 4).reshape(4, KD, P, FF),
        "w_ab": np.concatenate([pairs(w[:, 2064:3600], 12), pairs(w[:, 0:2048], 16)]),
        "w_ab16": w[:, 2048:2064].reshape(KD, P, 16).transpose(1, 0, 2).reshape(P, KD * 16),
        "w_ab_out": columns(ab_w_out[0], KD),
        "w_ret": pairs(ret_w_in[0], 48),
        "w_ret_out": columns(ret_w_out[0], KD),
        "conv_w": ab_conv_w[0].reshape(3, 12, P).transpose(2, 1, 0),
        "dn_norm": dn_norm_w.reshape(P, 1), "subln": diff_subln_w.reshape(P, 1),
        "a_log": np.tile(dn_A_log.reshape(1, 8), (1, NT)), "dt_bias": np.tile(dn_dt_bias.reshape(1, 8), (1, NT)),
        "ret_decay": ret_decay_logit.reshape(1, 16), "lam": diff_lambda.reshape(1, 256),
        "const": const, "levels": levels, "ret_tables": ret,
    }


def kernel(**inputs):
    from concourse import bacc
    from concourse.bass_utils import run_bass_kernel_spmd

    arrays = {k: np.ascontiguousarray(v) for k, v in lay_out(**{k: np.asarray(v) for k, v in inputs.items()}).items()}
    nc = bacc.Bacc("TRN2", target_bir_lowering=False, num_devices=1)
    aps = {}
    for name, v in arrays.items():
        aps[name] = nc.dram_tensor(f"in_{name}", v.shape, mybir.dt.from_np(v.dtype), kind="ExternalInput").ap()
    aps["out"] = nc.dram_tensor("out_y", (P, KD, SEQ), F32, kind="ExternalOutput").ap()
    build(nc, aps)
    r = run_bass_kernel_spmd(nc, [{f"in_{k}": v for k, v in arrays.items()}], core_ids=[0])
    got = r.results[0]["out_y"]
    return got.transpose(2, 1, 0).reshape(1, SEQ, D)
```

```python
import math

import numpy as np

import concourse.bass as bass
from concourse import mybir

F32 = mybir.dt.float32
F32R = mybir.dt.float32r
BF16 = mybir.dt.bfloat16
ALU = mybir.AluOpType
ACT = mybir.ActivationFunctionType
AX = mybir.AxisListType

P = 128
D = 1024
KD = D // P
SEQ = 256
T = 2 * SEQ
NT = T // P
FF = 2816
NF = FF // P
FA, FB = 12, 10
DNH, DFH, RH = 4, 4, 8
EPS = 1e-6
LAMBDA_INIT = 0.8 - 0.6 * math.exp(0.0)
NADA = 2 * 9 * KD
CTX, LAT = slice(0, SEQ), slice(SEQ, T)
NEG = -1.0e30
LEVELS = 7

C_ID, C_ONE, C_TRIF, C_TRIB, C_CUTF, C_CUTB, C_ROTD, C_ROTR = range(8)
C_COSD, C_SIND = 8 * P, 8 * P + SEQ
NCONST = 8 * P + 2 * SEQ


def constants():
    i = np.arange(P)
    j, n = i[:, None], i[None, :]
    blocks = [np.eye(P), np.ones((P, P)), j <= n, j >= n,
              np.where(j <= n, 0.0, NEG), np.where(j >= n, 0.0, NEG)]

    def rotation(size):
        r = np.zeros((P, P))
        h = size // 2
        for o in range(P):
            if o % size < h:
                r[o + h, o] = -1.0
            else:
                r[o - h, o] = 1.0
        return r

    blocks += [rotation(32), rotation(P)]
    f32 = np.float32
    axis = 32
    inv = f32(10000.0) ** (-np.arange(0, axis, 2, dtype=f32) / f32(axis))
    tok = np.arange(SEQ)
    row, col = (tok // 64).astype(f32), (tok % 64).astype(f32)
    ang = np.zeros((P, SEQ), f32)
    for p in range(P):
        q = p % 64
        ang[p] = (row if q < 32 else col) * inv[q % 16]
    const = np.concatenate([np.asarray(b, f32) for b in blocks] + [np.cos(ang), np.sin(ang)], axis=1)
    levels = np.zeros((2, LEVELS, P, P), f32)
    for s in range(LEVELS):
        b = 1 << s
        m = ((n // (2 * b)) == (j // (2 * b))) & ((n // b) % 2 == 1) & ((j // b) % 2 == 0)
        levels[0, s], levels[1, s] = m, m.T
    levels = np.ascontiguousarray(levels.transpose(2, 0, 1, 3).reshape(P, 2 * LEVELS * P))
    ii = np.arange(SEQ)[None, :].astype(f32)
    jj = np.arange(SEQ)[:, None].astype(f32)
    tables = [np.abs(ii - jj), (jj <= ii), (jj >= ii), SEQ + ii - jj, SEQ - ii + jj]
    ret = [np.asarray(t, f32).reshape(2, P, SEQ).transpose(1, 0, 2).reshape(P, 2 * SEQ) for t in tables]
    invr = f32(10000.0) ** (-np.linspace(0.0, 1.0, 64, dtype=f32))
    angr = np.concatenate([invr, invr])[:, None] * tok[None, :].astype(f32)
    ret = np.concatenate(ret + [np.cos(angr), np.sin(angr)], axis=1).astype(f32)
    return const.astype(f32), levels, ret


class Tally:

    def __init__(self, sem):
        self.sem, self.n, self.i, self.k = sem, 0, 0, 0

    def inc(self, instruction, by=1):
        instruction.then_inc(self.sem, by)
        self.n += by

    def now(self):
        return self.n + self.i * self.k

    def enter(self, i, k):
        self.i, self.k, self.at = i, k, self.n

    def wait_by(self, eng):
        eng.wait_ge(self.sem, self.now())

    def leave(self, rounds):
        assert self.n - self.at == self.k, (self.n, self.at, self.k)
        self.n = self.at + rounds * self.k
        self.i = self.k = 0


def stages(names):
    return {name: n + 1 for n, name in enumerate(names)}


def build(nc, a):
    sems = {}

    def sem(name):
        if name not in sems:
            sems[name] = nc.alloc_semaphore(name)
        return sems[name]

    base = (nc.sbuf_base + 31) // 32 * 32
    end = nc.sbuf_usable_end
    cursor = [base]

    def put(name, shape, dt=F32, at=None):
        size = int(np.prod(shape[1:])) * (2 if dt == BF16 else 4)
        if at is None:
            at = cursor[0]
            cursor[0] += (size + 31) // 32 * 32
            assert cursor[0] <= end, (name, cursor[0], end)
        return nc.alloc_sbuf_tensor_at(name, shape, dt, offset=at), at

    x, _ = put("x", [P, KD, T])
    h_hi, at_h = put("h_hi", [P, KD, T], F32R)
    h_lo, _ = put("h_lo", [P, KD, T], F32R)
    w_raw = [put(f"w_raw{i}", [P, 2048])[0] for i in range(2)]
    w_hi, w_lo = [None, None], [None, None]
    w_hi[0], at_ring = put("w_hi0", [P, 2048], F32R)
    w_lo[0], _ = put("w_lo0", [P, 2048], F32R)
    w_hi[1], _ = put("w_hi1", [P, 2048], F32R)
    w_lo[1], _ = put("w_lo1", [P, 2048], F32R)
    ada_w, at_ada = put("ada_w", [P, 2, D])
    silu_c, _ = put("silu_c", [P, 2, D])
    ada_product, _ = put("ada_product", [P, D], BF16)
    at_r = cursor[0]
    cursor[0] += 72 * 1024
    sil, at_sil = put("sil", [P, 2, T])
    prod, at_prod = put("prod", [P, 2, T])
    const, _ = put("const", [P, NCONST])
    mcol, _ = put("mcol", [P, 2, NADA])
    mbias, _ = put("mbias", [P, NADA])
    norm_g, _ = put("norm_g", [P, 7, KD])
    mod, _ = put("mod", [P, 6, 3, 2, KD])
    mod_tmp, _ = put("mod_tmp", [P, 2, KD])
    conv_w, _ = put("conv_w", [P, 12, 3])
    vecs, _ = put("vecs", [P, 8])
    gate_in, _ = put("gate_in", [P, 2, 32])
    small, _ = put("small", [P, 512])
    hid_hi, _ = put("hid_hi", [P, FA, T], F32R, at=at_r)
    hid_lo, _ = put("hid_lo", [P, FA, T], F32R, at=at_r + FA * T * 4)
    ada0, _ = put("ada0", [P, KD, D], at=at_r)
    c_cols = small[:, 440:440 + 2 * KD]
    KB = 1024
    dn, _ = put("dn", [P, 4, DNH, T], at=at_r)
    df, _ = put("df", [P, 3 * DFH, T], at=at_r + 32 * KB)
    df_v, _ = put("df_v", [P, NT, DFH, P], at=at_r + 56 * KB)
    df_o, _ = put("df_o", [P, NT, DFH, P], at=at_r + 64 * KB)
    k_tok, _ = put("k_tok", [P, NT, DNH, P], at=at_r + 32 * KB)
    v_tok, _ = put("v_tok", [P, NT, DNH, P], at=at_r + 40 * KB)
    dn_sq, _ = put("dn_sq", [P, 2, DNH, T], at=at_r + 48 * KB)
    gram_t, delta_t, sys_t, cut_t, inv_n, inv_t, xbuf, v_new, state, k_stage = ([None, None] for _ in range(10))
    spots = [at_r + 48 * KB + 2 * KB * i for i in range(8)] + [at_h + 2 * KB * i for i in range(12)]
    for d in range(2):
        for buf, name in ((delta_t, "decay_t"), (gram_t, "qk_t"), (sys_t, "sys_t"), (cut_t, "cut_t"),
                          (inv_n, "inv"), (inv_t, "inv_t"), (xbuf, "xbuf"), (v_new, "v_new"),
                          (state, "state"), (k_stage, "k_stage")):
            buf[d], _ = put(f"{name}{d}", [P, DNH, P], at=spots.pop(0))
    levels, _ = put("levels", [P, 2 * LEVELS * P], at=at_r + 64 * KB)
    dn_o, _ = put("dn_o", [P, NT, DNH, P], at=at_r + 16 * KB)
    y_dn, _ = put("y_dn", [P, DNH, T], at=at_r)
    o_sq, _ = put("o_sq", [P, NT * DNH, P], at=at_r + 8 * KB)
    df_sq, _ = put("df_sq", [P, NT * DFH, P], at=at_r)
    y_df, _ = put("y_df", [P, DFH, T], at=at_h + 24 * KB)
    rq, _ = put("rq", [P, RH, SEQ], at=at_r)
    rk, _ = put("rk", [P, RH, T], at=at_r + 8 * KB)
    rv, _ = put("rv", [P, NT, 2 * D], at=at_r + 24 * KB)
    rg, _ = put("rg", [P, 16, SEQ], at=at_r + 56 * KB)
    ry_hi, _ = put("ry_hi", [P, 16, SEQ], F32R, at=at_r + 56 * KB)
    ry_lo, _ = put("ry_lo", [P, 16, SEQ], F32R, at=at_r + 8 * KB)
    rc, _ = put("rc", [P, 12 * SEQ], at=at_ada)
    r_decay = [put(f"r_decay{i}", [P, 4 * SEQ], at=at_h + 4 * KB * i)[0] for i in range(2)]
    r_back = [put(f"r_back{i}", [P, 4 * SEQ], at=at_h + (8 + 4 * i) * KB)[0] for i in range(2)]
    r_probs = [put(f"r_probs{i}", [P, 4 * SEQ], at=at_h + (16 + 4 * i) * KB)[0] for i in range(2)]
    r_kst = [put(f"r_kst{i}", [P, T], at=at_h + (24 + 2 * i) * KB)[0] for i in range(2)]
    r_square, _ = put("r_square", [P, 2 * SEQ], at=at_h + 28 * KB)

    ps = nc.alloc_psum_tensor("ps", [P, 8, 512], F32)
    NRM = 4

    def c_(i):
        return const[:, i * P:(i + 1) * P]

    ident, ones = c_(C_ID), c_(C_ONE)

    def over(ap, n):
        return ap.unsqueeze(1).to_broadcast([P, n, ap.shape[1]])

    def spread(ap, n):
        return ap.unsqueeze(2).to_broadcast([P, ap.shape[1], n])

    runs = []

    def run(name, n, elems, source):
        s0 = sum(r[2] for r in runs)
        runs.append((name, s0, n, elems, source))

    def ffn_runs(j):
        def up(f0):
            return lambda r: a["w_up"][j, bass.ds(f0 + r, 1)].rearrange("a p n -> (a p) n")

        def down(f0, nf):
            return lambda r: a["w_down"][j, bass.ds(r, 1), :, f0 * P:(f0 + nf) * P].rearrange("a p n -> (a p) n")

        run(f"up{j}a", FA, 2048, up(0))
        run(f"down{j}a", KD, FA * P, down(0, FA))
        run(f"up{j}b", FB, 2048, up(FA))
        run(f"down{j}b", KD, FB * P, down(FA, FB))

    def tiles(key, t0):
        return lambda r: a[key][bass.ds(t0 + r, 1)].rearrange("a p n -> (a p) n")

    ffn_runs(0)
    run("diff", 6, 2048, tiles("w_ab", 0))
    run("ab", 1, D, lambda r: a["w_ab16"])
    run("conv", 6, 2048, tiles("w_ab", 6))
    run("z", 2, 2048, tiles("w_ab", 12))
    run("about", KD, D, tiles("w_ab_out", 0))
    ffn_runs(1)
    ffn_runs(2)
    run("retq", 4, 2048, tiles("w_ret", 0))
    run("retk", 4, 2048, tiles("w_ret", 4))
    run("retv", 8, 2048, tiles("w_ret", 8))
    run("retg", 8, 2048, tiles("w_ret", 16))
    run("retout", KD, 2048, tiles("w_ret_out", 0))
    ffn_runs(3)
    R = {r[0]: r for r in runs}
    STEPS = sum(r[2] for r in runs)
    ELEMS = [r[3] for r in runs for _ in range(r[2])]

    def walk(eng, name, body, tallies=(), skip=0):
        _, s0, n, _, _ = R[name]
        looped = (n - 2 - skip) // 2
        for r in range(skip):
            body(s0 + r, (s0 + r) % 2, r, ELEMS[s0 + r + 2])
        if looped >= 2:
            with eng.Fori(0, looped) as i:
                for t, k in tallies:
                    t.enter(i, k)
                for b in range(2):
                    r = skip + 2 * i + b
                    body(s0 + r, (s0 + skip + b) % 2, r, ELEMS[s0 + skip + b])
                for t, k in tallies:
                    t.leave(looped)
            first = skip + 2 * looped
        else:
            first = skip
        for r in range(first, n):
            s = s0 + r
            body(s, s % 2, r, ELEMS[s + 2] if s + 2 < STEPS else 0)

    raw_ready = [sem(f"raw_ready{i}") for i in range(2)]
    hi_ready = sem("hi_ready")
    lo_ready = sem("lo_ready")
    step_done = sem("step_done")
    acc_free = sem("acc_free")
    silu_done = sem("silu_done")
    hidden_hi = sem("hidden_hi")
    hidden_lo = sem("hidden_lo")
    sq_ready = sem("sq_ready")
    sq_added = sem("sq_added")
    ssq_done = sem("ssq_done")
    root_done = sem("root_done")
    inverse_done = sem("inverse_done")
    rstd_done = sem("rstd_done")
    mod_ready = sem("mod_ready")
    normed = sem("normed")
    shifted = sem("shifted")
    h_hi_done = sem("h_hi_done")
    h_lo_done = sem("h_lo_done")
    ada_ready = [sem(f"ada_ready{i}") for i in range(2)]
    ada_dot = sem("ada_dot")
    loaded = sem("loaded")
    c_silu = sem("c_silu")

    norms = ["n00", "n01", "n02", "n10", "n11", "n12", "fin"]
    chunks_before = {n: KD * i for i, n in enumerate(norms)}
    ups_before = {}
    count = 0
    for j in range(4):
        for part, nf in (("a", FA), ("b", FB)):
            ups_before[f"up{j}{part}"] = count
            count += nf

    RESIDENT = 9
    ADA_SHIFT = KD
    ADA_START = 2 * KD
    c_loaded, x_loaded = sem("c_loaded"), sem("x_loaded")
    ada0_ready, ada0_done = [sem(f"ada0_ready{k}") for k in range(KD)], sem("ada0_done")

    def sp_program(sp):
        sp.dma_start(c_cols, a["c_cols"]).then_inc(c_loaded, 16)
        sp.dma_start(silu_c[:, 0, :], a["c_ctx"].partition_broadcast(P)).then_inc(c_loaded, 16)
        sp.dma_start(silu_c[:, 1, :], a["c"][0, :].partition_broadcast(P)).then_inc(c_loaded, 16)
        sp.dma_start(x[:], a["xT"]).then_inc(x_loaded, 16)
        sp.dma_start(const[:], a["const"]).then_inc(x_loaded, 16)
        for k in range(KD):
            sp.dma_start(ada0[:, k, :], a["ada0"][k]).then_inc(ada0_ready[k], 16)
        for dst, key in ((mbias[:], "mbias"), (norm_g[:], "norm_g"), (conv_w[:], "conv_w"),
                         (vecs[:, 0:1], "dn_norm"), (vecs[:, 1:2], "subln")):
            sp.dma_start(dst, a[key]).then_inc(loaded, 16)
        sp.dma_start(gate_in[:, 0, :], a["a_log"][0, :].partition_broadcast(P)).then_inc(loaded, 16)
        sp.dma_start(gate_in[:, 1, :], a["dt_bias"][0, :].partition_broadcast(P)).then_inc(loaded, 16)
        sp.dma_start(small[:, 0:16], a["ret_decay"][0, :].partition_broadcast(P)).then_inc(loaded, 16)
        sp.dma_start(small[:, 64:320], a["lam"][0, :].partition_broadcast(P)).then_inc(loaded, 16)

        for name, s0, n, elems, source in runs:
            def load(s, slot, r, wait=True):
                if wait:
                    sp.wait_ge(lo_ready, s - 1)
                src = source(r)
                sp.dma_start(w_raw[slot][:, 0:elems], src).then_inc(raw_ready[slot], 16)

            first = 0
            if s0 == 0:
                load(0, 0, 0, wait=False)
                load(1, 1, 1, wait=False)
                first = 2
            m = (n - first) // 2
            if m >= 2:
                with sp.Fori(0, m) as i:
                    for b in range(2):
                        load(s0 + first + 2 * i + b, (s0 + first + b) % 2, first + 2 * i + b)
                first += 2 * m
            for r in range(first, n):
                load(s0 + r, (s0 + r) % 2, r)
        for half in range(2):
            chunks = slice(half * KD // 2, (half + 1) * KD // 2)
            sp.wait_ge(sem("out_ready"), half + 1)
            sp.dma_start(a["out"][:, chunks], x[:, chunks, LAT]).then_inc(sem("out_stored"), 16)
        sp.wait_ge(sem("out_stored"), 32)

    ADA_BEFORE_DN = ADA_START + 60 + 2

    def pool_program(pool):
        def tile(t, slot, wait=True):
            if wait:
                pool.wait_ge(ada_dot, 2 * t - 2)
            index = t if isinstance(t, int) and t < ADA_SHIFT else t - ADA_START + ADA_SHIFT
            pool.dma_start(ada_w[:, slot, :], a["ada"][bass.ds(index, 1)].rearrange("a p n -> (a p) n")) \
                .then_inc(ada_ready[slot], 16)

        for t in range(ADA_SHIFT):
            tile(t, t % 2, wait=t >= 2)
        for t in range(2):
            pool.wait_ge(ada_dot, 2 * (ADA_SHIFT - 1 + t))
            tile(ADA_START + t, t, wait=False)
        with pool.Fori(0, (ADA_BEFORE_DN - ADA_START - 2) // 2) as i:
            for b in range(2):
                tile(ADA_START + 2 + 2 * i + b, b)
        pool_deltanet(pool)
        with pool.Fori(0, (NADA - ADA_BEFORE_DN) // 2) as i:
            for b in range(2):
                tile(ADA_BEFORE_DN + 2 * i + b, b)
        pool_retention(pool)

    def split_hi(act, s, slot, elems):
        act.wait_ge(raw_ready[slot], 8 * (s - slot) + 16)
        if not (isinstance(s, int) and s < 2):
            act.wait_ge(step_done, s - 1)
        act.activation(w_hi[slot][:, 0:elems], w_raw[slot][:, 0:elems], ACT.Copy).then_inc(hi_ready, 1)

    def act_up(act, name, cols):
        n = cols.stop - cols.start

        def body(s, slot, r, ahead):
            act.wait_ge(step_done, s + 1)
            act.activation(sil[:, slot, 0:n], ps[:, 2 * slot, cols], ACT.Silu).then_inc(silu_done, 1)
            if ahead:
                split_hi(act, s + 2, slot, ahead)
            act.wait_ge(acc_free, s + 3)
            act.activation(hid_hi[:, bass.ds(r, 1), cols].rearrange("p a n -> p (a n)"), prod[:, slot, 0:n],
                           ACT.Copy).then_inc(hidden_hi, 1)
        walk(act, name, body)

    def act_plain(act, name):
        def body(s, slot, r, ahead):
            if ahead:
                split_hi(act, s + 2, slot, ahead)
        walk(act, name, body)

    def adds_before(norm):
        return 1 + (KD - 2) * (norms.index(norm) - 1)

    def sums_before(norm):
        return 0 if norm == "n00" else KD + norms.index(norm) - 1

    def act_square(act, norm, r, slot, cols):
        n = cols.stop - cols.start
        if norm == "n00":
            if r >= 2:
                act.wait_ge(ssq_done, r - 1)
        elif not (isinstance(r, int) and r < 2):
            act.wait_ge(sq_added, adds_before(norm) + r - 2)
        out = sil[:, 0, 0:n] if norm != "n00" and isinstance(r, int) and r == 0 else prod[:, slot, 0:n]
        act.activation(out, x[:, bass.ds(r, 1), cols].rearrange("p a n -> p (a n)"),
                       ACT.Square).then_inc(sq_ready, 1)

    warm_root, _ = put("warm_root", [P, 1])
    warmed = sem("warmed")

    def act_down_norm(act, name, norm, cols):
        s0 = R[name][1]

        def body(s, slot, r, ahead):
            if isinstance(r, int) and r == KD - 1:
                act.activation(warm_root[:], vecs[:, 2:3], ACT.Sqrt).then_inc(warmed, 1)
            if ahead:
                split_hi(act, s + 2, slot, ahead)
            act.wait_ge(acc_free, s + 3)
            act_square(act, norm, r, slot, cols)
        walk(act, name, body, skip=2)

    def act_root(act, norm, t0, scale):
        k = norms.index(norm)
        act.wait_ge(ssq_done, sums_before(norm) + (KD if norm == "n00" else 1))
        act.activation(norm_columns(norm, t0, 0), ps[:, NRM, t0:NT], ACT.Sqrt, bias=vecs[:, 2:3],
                       scale=scale).then_inc(root_done, 1)

    def act_modulate(act, norm):
        k, base_c = norms.index(norm), chunks_before[norm]

        def one(c, b):
            act.wait_ge(normed, base_c + c + 1)
            if not (isinstance(c, int) and base_c + c < 2):
                act.wait_ge(h_lo_done, base_c + c - 1)
            for st, cols in live(norm):
                last = act.activation(sil[:, b, cols], prod[:, b, cols], ACT.Identity,
                                      bias=mod[:, k, 1, st, bass.ds(c, 1)], scale=mod[:, k, 0, st, bass.ds(c, 1)])
            last.then_inc(shifted, 1)
            act.wait_ge(shifted, base_c + c + 1)
            cols = streams_of(norm)
            act.activation(h_hi[:, bass.ds(c, 1), cols].rearrange("p a n -> p (a n)"), sil[:, b, cols],
                           ACT.Copy).then_inc(h_hi_done, 1)
        one(0, 0)
        one(1, 1)
        with act.Fori(0, (KD - 2) // 2) as i:
            for b in range(2):
                one(2 * i + 2 + b, b)

    def streams_of(norm):
        return slice(live(norm)[0][1].start, T)

    def live(norm):
        return ((1, LAT),) if norm in ("n12", "fin") else ((0, CTX), (1, LAT))

    ALL = slice(0, T)

    def scalar_program(act):
        act.wait_ge(c_loaded, 48)
        act.activation(c_cols, c_cols, ACT.Silu).then_inc(c_silu, 1)
        act.activation(silu_c[:], silu_c[:], ACT.Silu).then_inc(c_silu, 1)
        act.wait_ge(sem("eps_set"), 1)
        act.wait_ge(x_loaded, 32)
        for r in range(KD):
            act_square(act, "n00", r, r % 2, ALL)
        act_root(act, "n00", 0, 1.0 / D)
        act.wait_ge(loaded, 16 * RESIDENT)
        split_hi(act, 0, 0, ELEMS[0])
        split_hi(act, 1, 1, ELEMS[1])
        act_modulate(act, "n00")
        act_up(act, "up0a", ALL)
        act_plain(act, "down0a")
        act_up(act, "up0b", ALL)
        act_down_norm(act, "down0b", "n01", ALL)
        act_root(act, "n01", 0, 1.0 / D)
        act_modulate(act, "n01")
        act_ab(act)
        act_down_norm(act, "about", "n02", ALL)
        act_root(act, "n02", 0, 1.0 / D)
        act_modulate(act, "n02")
        act_up(act, "up1a", ALL)
        act_plain(act, "down1a")
        act_up(act, "up1b", ALL)
        act_down_norm(act, "down1b", "n10", ALL)
        act_root(act, "n10", 0, 1.0 / D)
        act_modulate(act, "n10")
        act_up(act, "up2a", ALL)
        act_plain(act, "down2a")
        act_up(act, "up2b", ALL)
        act_down_norm(act, "down2b", "n11", ALL)
        act_root(act, "n11", 0, 1.0 / D)
        act_modulate(act, "n11")
        act_ret(act)
        act_down_norm(act, "retout", "n12", LAT)
        act_root(act, "n12", 2, 1.0 / D)
        act_modulate(act, "n12")
        act_up(act, "up3a", LAT)
        act_plain(act, "down3a")
        act_up(act, "up3b", LAT)
        act_down_norm(act, "down3b", "fin", LAT)
        act_root(act, "fin", 2, 1.0 / D)

    order_v = Tally(sem("vector_order"))

    def split_lo(dve, s, slot, elems):
        dve.wait_ge(hi_ready, s + 1)
        dve.tensor_tensor(w_lo[slot][:, 0:elems], w_raw[slot][:, 0:elems], w_hi[slot][:, 0:elems].bitcast(F32),
                          ALU.subtract).then_inc(lo_ready, 1)

    def ada_tile(dve, t, slot):
        dve.wait_ge(ada_ready[slot], 8 * ((t if isinstance(t, int) and t < ADA_SHIFT else t - ADA_START + ADA_SHIFT) - slot) + 16)
        for st in range(2):
            if not (isinstance(t, int) and t == 0 and st == 0):
                dve.wait_ge(ada_dot, 2 * t + st)
            dve.scalar_tensor_tensor(out=ada_product[:], in0=ada_w[:, slot, :], scalar=1.0, in1=silu_c[:, st, :],
                                     op0=ALU.mult, op1=ALU.mult, accum_out=mcol[:, st, bass.ds(t, 1)]) \
               .then_inc(ada_dot, 1)

    ada_next = [0]

    def dve_up(dve, name, cols, ada):
        u0, t0 = ups_before[name], ada_next[0]
        n = cols.stop - cols.start

        def body(s, slot, r, ahead):
            dve.wait_ge(silu_done, u0 + r + 1)
            if not (isinstance(r, int) and u0 + r < 2):
                dve.wait_ge(hidden_lo, u0 + r - 1)
            dve.tensor_tensor(prod[:, slot, 0:n], sil[:, slot, 0:n], ps[:, 2 * slot + 1, cols], ALU.mult) \
               .then_inc(acc_free, 1)
            if ahead:
                split_lo(dve, s + 2, slot, ahead)
            dve.wait_ge(hidden_hi, u0 + r + 1)
            dve.tensor_tensor(hid_lo[:, bass.ds(r, 1), cols].rearrange("p a n -> p (a n)"), prod[:, slot, 0:n],
                              hid_hi[:, bass.ds(r, 1), cols].rearrange("p a n -> p (a n)").bitcast(F32),
                              ALU.subtract).then_inc(hidden_lo, 1)
            for q in range(ada):
                ada_tile(dve, t0 + ada * r + q, (t0 + q) % 2)
        walk(dve, name, body, skip=2)
        ada_next[0] += ada * R[name][2]

    def dve_down(dve, name, norm_gate, streams, ada, norm=None):
        k, t0 = norms.index(norm_gate), ada_next[0]
        total = streams[-1][1].stop - streams[0][1].start

        def body(s, slot, r, ahead):
            if norm and not (isinstance(r, int) and r < 2):
                dve.wait_ge(sq_ready, chunks_before[norm] + r)
                dve.wait_ge(sq_added, adds_before(norm) + r - 2)
                dve.tensor_tensor(sil[:, 0, 0:total], sil[:, 0, 0:total], prod[:, 1 - slot, 0:total], ALU.add) \
                   .then_inc(sq_added, 1)
            dve.wait_ge(step_done, s + 1)
            for st, cols in streams:
                xc = x[:, bass.ds(r, 1), cols].rearrange("p a n -> p (a n)")
                last = dve.scalar_tensor_tensor(out=xc, in0=ps[:, 2 * slot, cols],
                                                scalar=mod[:, k, 2, st, bass.ds(r, 1)], in1=xc,
                                                op0=ALU.mult, op1=ALU.add)
            last.then_inc(acc_free, 1)
            if ahead:
                split_lo(dve, s + 2, slot, ahead)
            if ada and not (ada == 2 and isinstance(r, int) and r == KD - 1):
                ada_tile(dve, t0 + r, (t0 + slot + R[name][1]) % 2)
        walk(dve, name, body, skip=2 if norm else 0)
        ada_next[0] += R[name][2] if ada else 0

    def dve_left_tile(dve):
        ada_tile(dve, ada_next[0] - 1, (ada_next[0] - 1) % 2)

    def dve_mod(dve, norm):
        k = norms.index(norm)
        t = 3 * KD * k

        def bias(m):
            return over(mbias[:, t + m * KD:t + (m + 1) * KD], 2)

        dve.wait_ge(ada_dot, 2 * (t + 3 * KD)) if norm != "n00" else None
        order_v.inc(dve.tensor_tensor(mod_tmp[:], mcol[:, :, t + KD:t + 2 * KD], bias(1), ALU.add))
        order_v.wait_by(dve)
        order_v.inc(dve.scalar_tensor_tensor(out=mod[:, k, 0], in0=mod_tmp[:], scalar=1.0,
                                             in1=over(norm_g[:, k, :], 2), op0=ALU.add, op1=ALU.mult))
        dve.tensor_tensor(mod[:, k, 1], mcol[:, :, t:t + KD], bias(0), ALU.add).then_inc(mod_ready, 1)
        order_v.wait_by(dve)

    def dve_gate(dve, norm):
        k = norms.index(norm)
        t = 3 * KD * k + 2 * KD
        dve.wait_ge(ada_dot, 2 * (t + KD))
        order_v.inc(dve.tensor_tensor(mod_tmp[:], mcol[:, :, t:t + KD], over(mbias[:, t:t + KD], 2), ALU.add))
        order_v.wait_by(dve)
        order_v.inc(dve.tensor_scalar(mod[:, k, 2], mod_tmp[:], 1.0 if k % 3 == 1 else 0.5, None, ALU.mult))
        order_v.wait_by(dve)

    def norm_columns(norm, t0, at):
        first = 320 + 16 * norms.index(norm) + at
        return small[:, first + t0:first + NT]

    def dve_inverse(dve, norm, t0):
        dve.wait_ge(root_done, norms.index(norm) + 1)
        dve.reciprocal(norm_columns(norm, t0, 8), norm_columns(norm, t0, 0)).then_inc(inverse_done, 1)

    def dve_modulate(dve, norm):
        base_c, cols = chunks_before[norm], streams_of(norm)
        dve.wait_ge(rstd_done, norms.index(norm) + 1)
        dve.wait_ge(mod_ready, norms.index(norm) + 1)

        def flat(ap, c):
            return ap[:, bass.ds(c, 1), cols].rearrange("p a n -> p (a n)")

        def normalise(c, b):
            if not (isinstance(c, int) and base_c + c < 2):
                dve.wait_ge(shifted, base_c + c - 1)
            dve.tensor_tensor(prod[:, b, cols], flat(x, c), ps[:, NRM, cols], ALU.mult).then_inc(normed, 1)

        def lo_part(c, b):
            dve.wait_ge(h_hi_done, base_c + c + 1)
            dve.tensor_tensor(flat(h_lo, c), sil[:, b, cols], flat(h_hi, c).bitcast(F32), ALU.subtract) \
               .then_inc(h_lo_done, 1)

        normalise(0, 0)
        normalise(1, 1)
        with dve.Fori(0, (KD - 2) // 2) as i:
            for b in range(2):
                lo_part(2 * i + b, b)
                normalise(2 * i + 2 + b, b)
        lo_part(KD - 2, 0)
        lo_part(KD - 1, 1)
        dve.wait_ge(h_lo_done, base_c + KD)

    BOTH = ((0, CTX), (1, LAT))
    ONLY = ((1, LAT),)

    def vector_program(dve):
        dve.memset(vecs[:, 2:3], EPS).then_inc(sem("eps_set"), 1)
        dve.memset(vecs[:, 3:4], 0.0).then_inc(sq_added, 1)
        for slot in range(2):
            dve.memset(sil[:, slot], 0.0).then_inc(acc_free, 1)
        dve.wait_ge(c_silu, 2)
        for t in range(ADA_SHIFT):
            ada_tile(dve, t, t % 2)
        dve.wait_ge(x_loaded, 32)
        dve_inverse(dve, "n00", 0)
        split_lo(dve, 0, 0, ELEMS[0])
        split_lo(dve, 1, 1, ELEMS[1])
        dve.wait_ge(loaded, 16 * RESIDENT)
        order_v.inc(dve.tensor_scalar(vecs[:, 1:2], vecs[:, 1:2], 1.0 - LAMBDA_INIT, None, ALU.mult))
        dve.wait_ge(ada0_done, 1)
        dve.tensor_copy(mcol[:, :, ADA_SHIFT:ADA_START],
                        ps[:, 5, 0:2 * KD].rearrange("p (n s) -> p s n", s=2)).then_inc(ada_dot, 2 * KD)
        ada_next[0] = ADA_START
        dve.wait_ge(ada_dot, 2 * ADA_START)
        dve_mod(dve, "n00")
        dve_modulate(dve, "n00")
        dve_up(dve, "up0a", ALL, 2)
        dve_gate(dve, "n00")
        dve_down(dve, "down0a", "n00", BOTH, 1)
        dve_up(dve, "up0b", ALL, 2)
        dve_down(dve, "down0b", "n00", BOTH, 2, norm="n01")
        dve_mod(dve, "n01")
        dve_inverse(dve, "n01", 0)
        dve_modulate(dve, "n01")
        dve_left_tile(dve)
        dve_ab(dve)
        dve_gate(dve, "n01")
        dve_down(dve, "about", "n01", BOTH, 0, norm="n02")
        dve_mod(dve, "n02")
        dve_inverse(dve, "n02", 0)
        dve_modulate(dve, "n02")
        dve_gate(dve, "n02")
        dve_up(dve, "up1a", ALL, 2)
        dve_down(dve, "down1a", "n02", BOTH, 1)
        dve_up(dve, "up1b", ALL, 2)
        dve_down(dve, "down1b", "n02", BOTH, 2, norm="n10")
        dve_mod(dve, "n10")
        dve_inverse(dve, "n10", 0)
        dve_modulate(dve, "n10")
        dve_left_tile(dve)
        dve_gate(dve, "n10")
        dve_up(dve, "up2a", ALL, 0)
        dve_down(dve, "down2a", "n10", BOTH, 1)
        dve_up(dve, "up2b", ALL, 0)
        dve_down(dve, "down2b", "n10", BOTH, 0, norm="n11")
        dve_mod(dve, "n11")
        dve_inverse(dve, "n11", 0)
        dve_modulate(dve, "n11")
        dve_ret(dve)
        dve_gate(dve, "n11")
        dve_down(dve, "retout", "n11", ONLY, 0, norm="n12")
        dve_mod(dve, "n12")
        dve_inverse(dve, "n12", 2)
        dve_modulate(dve, "n12")
        dve_gate(dve, "n12")
        dve_up(dve, "up3a", LAT, 0)
        dve_down(dve, "down3a", "n12", ONLY, 0)
        dve_up(dve, "up3b", LAT, 0)
        dve_down(dve, "down3b", "n12", ONLY, 0, norm="fin")
        dve_inverse(dve, "fin", 2)
        dve.wait_ge(rstd_done, len(norms))
        for c in range(KD):
            last = dve.scalar_tensor_tensor(out=x[:, c, LAT], in0=x[:, c, LAT], scalar=norm_g[:, 6, c:c + 1],
                                            in1=ps[:, NRM, LAT], op0=ALU.mult, op1=ALU.mult)
            if c % (KD // 2) == KD // 2 - 1:
                last.then_inc(sem("out_ready"), 1)

    def products(pe, out, slot, off, nk, rhs_hi, rhs_lo, first=True, last=True):
        for k in range(nk):
            hi = w_hi[slot][:, off + k * P:off + (k + 1) * P]
            lo = w_lo[slot][:, off + k * P:off + (k + 1) * P]
            pe.matmul(out, lo, rhs_hi(k), start=first and k == 0, stop=False)
            pe.matmul(out, hi, rhs_lo(k), start=False, stop=False)
            mm = pe.matmul(out, hi, rhs_hi(k), start=False, stop=last and k == nk - 1)
        return mm

    def pe_ready(pe, s):
        pe.wait_ge(lo_ready, s + 1)
        pe.wait_ge(acc_free, s + 1)

    def pair_products(pe, s, slot, cols, norm=None):
        pe_ready(pe, s)
        for k in range(KD if norm else 0):
            pe.wait_ge(h_lo_done, chunks_before[norm] + k + 1)
            for u in range(2):
                mm = products(pe, ps[:, 2 * slot + u, cols], slot, u * D + k * P, 1, lambda _: h_hi[:, k, cols],
                              lambda _: h_lo[:, k, cols], k == 0, k == KD - 1)
        for u in range(0 if norm else 2):
            mm = products(pe, ps[:, 2 * slot + u, cols], slot, u * D, KD,
                          lambda k: h_hi[:, k, cols], lambda k: h_lo[:, k, cols])
        mm.then_inc(step_done, 1)

    def pe_pairs(pe, name, cols, norm=None):
        def body(s, slot, r, ahead):
            pair_products(pe, s, slot, cols, norm if isinstance(r, int) and r == 0 else None)
        walk(pe, name, body, skip=2)

    def pe_ssq(pe, norm, r, squares, t0):
        for t in range(t0, NT):
            mm = pe.matmul(ps[:, NRM, t:t + 1], squares[:, (t - t0) * P:(t - t0 + 1) * P], ones[:, 0:1],
                           start=r == 0 and t == t0, stop=r == KD - 1, skip_group_check=True)
        return mm

    def pe_down(pe, name, nk, hi, lo, cols, norm=None, up=None, t0=0, ready=None):
        s0 = R[name][1]

        def body(s, slot, r, ahead):
            pe_ready(pe, s)
            if up and isinstance(r, int) and r == 0:
                pe.wait_ge(hidden_lo, up - 1)
            for k in range(nk):
                if up and isinstance(r, int) and r == 0 and k == nk - 1:
                    pe.wait_ge(hidden_lo, up)
                if ready and isinstance(r, int) and r == 0:
                    ready(k)
                whi = w_hi[slot][:, k * P:(k + 1) * P]
                wlo = w_lo[slot][:, k * P:(k + 1) * P]
                pe.matmul(ps[:, 2 * slot, cols], wlo, hi(k), start=k == 0, stop=False)
                pe.matmul(ps[:, 2 * slot, cols], whi, lo(k), start=False, stop=False)
                mm = pe.matmul(ps[:, 2 * slot, cols], whi, hi(k), start=False, stop=k == nk - 1)
            mm.then_inc(step_done, 1)
        walk(pe, name, body, skip=2)
        if norm:
            pe.wait_ge(sq_added, adds_before(norm) + KD - 2)
            pe_ssq(pe, norm, 0, sil[:, 0], t0)
            pe.wait_ge(sq_ready, chunks_before[norm] + KD)
            pe_ssq(pe, norm, KD - 1, prod[:, (s0 + KD - 1) % 2], t0).then_inc(ssq_done, 1)

    def pe_rstd(pe, norm, t0):
        pe.wait_ge(inverse_done, norms.index(norm) + 1)
        inverse = norm_columns(norm, 0, 8)
        for t in range(t0, NT):
            mm = pe.matmul(ps[:, NRM, t * P:(t + 1) * P], inverse[:, t:t + 1].to_broadcast([P, P]), ident,
                           start=True, stop=True)
        mm.then_inc(rstd_done, 1)

    def pe_ffn(pe, j, cols, of, norm, t0):
        for part, nf in (("a", FA), ("b", FB)):
            name = f"up{j}{part}"
            pe_pairs(pe, name, cols, norm=of if part == "a" else None)
            pe_down(pe, f"down{j}{part}", nf, lambda k: hid_hi[:, k, cols], lambda k: hid_lo[:, k, cols], cols,
                    norm=norm if part == "b" else None, up=ups_before[name] + nf, t0=t0)

    def tensor_program(pe):
        pe.wait_ge(x_loaded, 32)
        for r in range(KD):
            pe.wait_ge(sq_ready, r + 1)
            pe_ssq(pe, "n00", r, prod[:, r % 2], 0).then_inc(ssq_done, 1)
        pe.wait_ge(c_silu, 1)
        for k in range(KD):
            pe.wait_ge(ada0_ready[k], 16)
            for n in range(KD):
                mm = pe.matmul(ps[:, 5, 2 * n:2 * n + 2], ada0[:, k, n * P:(n + 1) * P],
                               c_cols[:, 2 * k:2 * k + 2], start=k == 0 and n == 0, stop=k == KD - 1,
                               skip_group_check=True)
        mm.then_inc(ada0_done, 1)
        pe_rstd(pe, "n00", 0)
        pe_ffn(pe, 0, ALL, "n00", "n01", 0)
        pe_rstd(pe, "n01", 0)
        pe_ab(pe)

        def about_ready(k):
            if k == DFH:
                pe_merge(pe)
            pe.wait_ge(y_lo_done, k + 1)
        pe_down(pe, "about", KD, lambda k: h_hi[:, k, :], lambda k: h_lo[:, k, :], ALL, norm="n02",
                ready=about_ready)
        pe_rstd(pe, "n02", 0)
        pe_ffn(pe, 1, ALL, "n02", "n10", 0)
        pe_rstd(pe, "n10", 0)
        pe_ffn(pe, 2, ALL, "n10", "n11", 0)
        pe_rstd(pe, "n11", 0)
        pe_ret(pe)
        pe_down(pe, "retout", 16, lambda k: ry_hi[:, k, :], lambda k: ry_lo[:, k, :], LAT, norm="n12", t0=2,
                ready=lambda k: pe.wait_ge(r_lo, k // 2 + 1))
        pe_rstd(pe, "n12", 2)
        pe_ffn(pe, 3, LAT, "n12", "fin", 2)
        pe_rstd(pe, "fin", 2)

    dnf = dn[:].rearrange("p a h t -> p (a h) t")
    S_AB = R["ab"][1]
    S_Z_END = R["about"][1]
    ab_turned, ab_placed = sem("ab_turned"), sem("ab_placed")
    gates, _ = put("gates", [P, 12, 32])
    ab_tok, G_Y, G_ABS, G_EXP, G_S, G_S2, G_POLY, G_OUT = (gates[:, n, :] for n in range(8))
    log_decay, beta, g_tmp = gates[:, 8, :], gates[:, 9, :], gates[:, 10, :]
    ab_raw, _ = put("ab_raw", [P, NT, 16])
    qk_inv = small[:, 460:492].rearrange("p (w t h) -> p w t h", w=2, t=NT)
    qk_root = small[:, 16:48].rearrange("p (w t h) -> p w t h", w=2, t=NT)
    dsm, _ = put("dsm", [P, 2, 6, 4])
    la_stage, _ = put("la_stage", [P, 2, 4])
    attn_s, _ = put("attn_s", [P, 6])
    attn_n, _ = put("attn_n", [P, 2, 12])
    at_probs = [put(f"at_probs{i}", [P, 2, T], at=at_r + 4 * KB * i)[0] for i in range(2)]
    at_mixed = [put(f"at_mixed{i}", [P, T], at=at_r + (8 + 2 * i) * KB)[0] for i in range(2)]
    at_turned = [put(f"at_turned{i}", [P, T], at=at_r + (12 + 2 * i) * KB)[0] for i in range(2)]

    abs_ready, exp_ready = sem("abs_ready"), sem("exp_ready")

    def dve_softplus(dve, y, out, n, use):
        ab, ex, s, s2, p = (g[:, 0:n] for g in (G_ABS, G_EXP, G_S, G_S2, G_POLY))
        order_v.inc(dve.tensor_scalar(ab, y, -1.0, None, ALU.mult))
        order_v.wait_by(dve)
        dve.tensor_tensor(ab, ab, y, ALU.max).then_inc(abs_ready, 1)
        dve.wait_ge(exp_ready, use)
        order_v.inc(dve.tensor_scalar(s, ex, 2.0, None, ALU.add))
        order_v.wait_by(dve)
        order_v.inc(dve.reciprocal(s2, s))
        order_v.wait_by(dve)
        order_v.inc(dve.tensor_tensor(s, ex, s2, ALU.mult))
        order_v.wait_by(dve)
        order_v.inc(dve.tensor_tensor(s2, s, s, ALU.mult))
        order_v.wait_by(dve)
        order_v.inc(dve.tensor_scalar(p, s2, 1.0 / 17.0, None, ALU.mult))
        for term in range(7, 0, -1):
            order_v.wait_by(dve)
            order_v.inc(dve.scalar_tensor_tensor(out=p, in0=p, scalar=1.0 / (2 * term + 1), in1=s2,
                                                 op0=ALU.add, op1=ALU.mult))
        order_v.wait_by(dve)
        order_v.inc(dve.scalar_tensor_tensor(out=p, in0=p, scalar=1.0, in1=s, op0=ALU.add, op1=ALU.mult))
        order_v.inc(dve.tensor_scalar(ab, y, 0.0, None, ALU.max))
        order_v.wait_by(dve)
        order_v.inc(dve.scalar_tensor_tensor(out=out, in0=p, scalar=2.0, in1=ab, op0=ALU.mult, op1=ALU.add))
        order_v.wait_by(dve)

    def act_softplus(act, n, use):
        act.wait_ge(abs_ready, use)
        act.activation(G_EXP[:, 0:n], G_ABS[:, 0:n], ACT.Exp, scale=-1.0).then_inc(exp_ready, 1)

    rot_done, rope_done = sem("rot_done"), sem("rope_done")
    dv_turned, dv_done = sem("dv_turned"), sem("dv_done")
    lam_sum, lam_exp = sem("lam_sum"), sem("lam_exp")
    scores_done, max_done, probs_done = sem("scores_done"), sem("max_done"), sem("probs_done")
    mixed_done, turned_done, pt_done = sem("mixed_done"), sem("turned_done"), sem("pt_done")
    pv_done, attn_out = sem("pv_done"), sem("attn_out")
    ATTN = [(h, qt, SEQ if qt < 2 else T) for h in range(DFH) for qt in range(NT)]
    S_DIFF_END = R["conv"][1]
    DV_BANKS = (4, 5, 6, 4)

    def pe_diff(pe):
        pe.wait_ge(acc_free, S_DIFF_END + 2)
        pe.wait_ge(rope_done, 4)
        for t in range(NT):
            if t == 3:
                pe_turn_ab16(pe)
                pe.wait_ge(dv_done, 1)
            for h in range(DFH):
                mm = pe.transpose(ps[:, DV_BANKS[t], h * P:(h + 1) * P], df[:, 8 + h, t * P:(t + 1) * P], ident)
            mm.then_inc(dv_turned, 1)
        for n in range(len(ATTN) + 2):
            if n < len(ATTN):
                h, qt, nk = ATTN[n]
                if n >= 2:
                    pe.wait_ge(probs_done, n - 1)
                for m in range(2):
                    rows = slice(64 * m, 64 * m + 64)
                    mm = pe.matmul(ps[:, 2 * (n % 2) + m, 0:nk], df[rows, h, qt * P:(qt + 1) * P],
                                   df[rows, 4 + h, 0:nk], start=True, stop=True)
                mm.then_inc(scores_done, 1)
            if n >= 2:
                pe_weigh_values(pe, n - 2)
            if n == 1:
                pe.wait_ge(dv_done, NT)
                pe.wait_ge(ab_placed, 1)
            if 1 <= n <= len(ATTN):
                pe_turn_probs(pe, n - 1)
        pe.wait_ge(attn_out, len(ATTN))

    def pe_rotate_diff(pe, j):
        pe.wait_ge(acc_free, R["diff"][1] + j + 3)
        if j >= 2:
            pe.wait_ge(rope_done, j - 1)
        pe.matmul(ps[:, 5 + j % 2, :], c_(C_ROTD), df[:, 2 * j:2 * j + 2, LAT], start=True, stop=True) \
          .then_inc(rot_done, 1)

    def pe_turn_probs(pe, n):
        nk = ATTN[n][2]
        pe.wait_ge(mixed_done, n + 1)
        if n >= 2:
            pe.wait_ge(pt_done, n - 1)
        for kt in range(nk // P):
            mm = pe.transpose(ps[:, 5 + n % 2, kt * P:(kt + 1) * P], at_mixed[n % 2][:, kt * P:(kt + 1) * P], ident)
        mm.then_inc(turned_done, 1)

    def pe_weigh_values(pe, n):
        h, qt, nk = ATTN[n]
        pe.wait_ge(pt_done, n + 1)
        if n >= 2:
            pe.wait_ge(attn_out, n - 1)
        for kt in range(nk // P):
            mm = pe.matmul(ps[:, (4, 7)[n % 2], 0:P], at_turned[n % 2][:, kt * P:(kt + 1) * P], df_v[:, kt, h, :],
                           start=kt == 0, stop=kt == nk // P - 1)
        mm.then_inc(pv_done, 1)

    def act_diff(act):
        act.wait_ge(lam_sum, 1)
        act.activation(attn_s[:, 2:4], attn_s[:, 0:2], ACT.Exp).then_inc(lam_exp, 1)
        for t in range(NT):
            act.wait_ge(dv_turned, t + 1)
            act.activation(df_v[:, t].rearrange("p h d -> p (h d)"), ps[:, DV_BANKS[t], :], ACT.Copy) \
               .then_inc(dv_done, 1)
        for n in range(len(ATTN) + 2):
            if n < len(ATTN):
                nk, st = ATTN[n][2], attn_n[:, n % 2]
                act.wait_ge(max_done, n + 1)
                if n >= 2:
                    act.wait_ge(mixed_done, n - 1)
                for m in range(2):
                    last = act.activation(at_probs[n % 2][:, m, 0:nk], ps[:, 2 * (n % 2) + m, 0:nk], ACT.Exp,
                                          bias=st[:, 2 + m:3 + m], scale=0.125, accum_out=st[:, 4 + m:5 + m])
                last.then_inc(probs_done, 1)
            if 1 <= n <= len(ATTN):
                nk = ATTN[n - 1][2]
                act.wait_ge(turned_done, n)
                if n >= 3:
                    act.wait_ge(pv_done, n - 2)
                act.activation(at_turned[(n - 1) % 2][:, 0:nk], ps[:, 5 + (n - 1) % 2, 0:nk], ACT.Copy) \
                   .then_inc(pt_done, 1)
            if n >= 2:
                h, qt, nk = ATTN[n - 2]
                act.wait_ge(pv_done, n - 1)
                act.activation(df_o[:, qt, h, :], ps[:, (4, 7)[n % 2], 0:P], ACT.Copy).then_inc(attn_out, 1)

    def dve_rope_diff(dve, j):
        lat = df[:, 2 * j:2 * j + 2, LAT]
        dve.wait_ge(rot_done, j + 1)
        if j:
            dve.wait_ge(rope_done, j)
        p2 = prod[:, j % 2, :].rearrange("p (a t) -> p a t", a=2)
        rot = ps[:, 5 + j % 2, :].rearrange("p (a t) -> p a t", a=2)
        dve.tensor_tensor(p2, rot, over(const[:, C_SIND:C_SIND + SEQ], 2), ALU.mult)
        order_v.inc(dve.tensor_tensor(lat, lat, over(const[:, C_COSD:C_COSD + SEQ], 2), ALU.mult))
        order_v.wait_by(dve)
        dve.tensor_tensor(lat, lat, p2, ALU.add).then_inc(rope_done, 1)

    def dve_lambda(dve):
        lam = small[:, 64:320]
        for m in range(2):
            last = dve.tensor_tensor(sil[:, 0, m * 64:(m + 1) * 64],
                                     lam[:, m * 128:m * 128 + 64], lam[:, m * 128 + 64:m * 128 + 128], ALU.mult)
        order_v.inc(last)
        order_v.wait_by(dve)
        dve.tensor_reduce(attn_s[:, 0:2], sil[:, 0, 0:128].rearrange("p (m d) -> p m d", m=2), AX.X, ALU.add) \
           .then_inc(lam_sum, 1)

    def dve_diff(dve):
        dve_place_ab16(dve)
        dve.wait_ge(rope_done, 4)
        dve.wait_ge(lam_exp, 1)
        order_v.inc(dve.tensor_tensor(attn_s[:, 4:5], attn_s[:, 3:4], attn_s[:, 2:3], ALU.subtract))
        order_v.wait_by(dve)
        order_v.inc(dve.tensor_scalar(attn_s[:, 5:6], attn_s[:, 4:5], LAMBDA_INIT, None, ALU.subtract))
        order_v.wait_by(dve)
        for n in range(len(ATTN) + 1):
            if n >= 1:
                nk, st, probs, mixed = ATTN[n - 1][2], attn_n[:, (n - 1) % 2], at_probs[(n - 1) % 2], at_mixed[(n - 1) % 2]
                dve.wait_ge(probs_done, n)
                order_v.inc(dve.reciprocal(st[:, 6:8], st[:, 4:6]))
                order_v.wait_by(dve)
                if n >= 3:
                    dve.wait_ge(turned_done, n - 2)
                order_v.inc(dve.tensor_tensor(st[:, 8:9], st[:, 7:8], attn_s[:, 5:6], ALU.mult))
                order_v.inc(dve.tensor_scalar(mixed[:, 0:nk], probs[:, 0, 0:nk], st[:, 6:7], None, ALU.mult))
                order_v.wait_by(dve)
                dve.scalar_tensor_tensor(out=mixed[:, 0:nk], in0=probs[:, 1, 0:nk], scalar=st[:, 8:9],
                                         in1=mixed[:, 0:nk], op0=ALU.mult, op1=ALU.add).then_inc(mixed_done, 1)
            if n < len(ATTN):
                nk, st = ATTN[n][2], attn_n[:, n % 2]
                dve.wait_ge(scores_done, n + 1)
                order_v.inc(dve.tensor_reduce(st[:, 0:2], ps[:, 2 * (n % 2):2 * (n % 2) + 2, 0:nk], AX.X, ALU.max))
                order_v.wait_by(dve)
                dve.tensor_scalar(st[:, 2:4], st[:, 0:2], -0.125, None, ALU.mult).then_inc(max_done, 1)

    conv_center, conv_out = sem("conv_center"), sem("conv_out")
    gate_exp, gates_ready = sem("gate_exp"), sem("gates_ready")
    qk_squared, qk_summed, qk_rooted = sem("qk_squared"), sem("qk_summed"), sem("qk_rooted")
    qk_inverse = sem("qk_inverse")
    k_turned, v_turned_dn = sem("k_turned"), sem("dn_v_turned")
    k_tok_done, v_tok_done = sem("k_tok_done"), sem("v_tok_done")
    k_back, k_feat_done = sem("k_back"), sem("k_feat_done")
    levels_ready = sem("levels_ready")

    def act_conv(act):
        def body(s, slot, r, ahead):
            act.wait_ge(step_done, s + 1)
            if not (isinstance(r, int) and r == 0):
                act.wait_ge(conv_out, r)
            for u in range(2):
                act.activation(prod[:, u, :], ps[:, 2 * slot + u, :], ACT.Copy,
                               scale=conv_w[:, bass.ds(2 * r + u, 1), 1:2].rearrange("p a b -> p (a b)")) \
                   .then_inc(conv_center, 1)
            if ahead:
                split_hi(act, s + 2, slot, ahead)
            act.wait_ge(acc_free, s + 3)
            act.activation(dnf[:, bass.ds(2 * r, 2), :], prod[:], ACT.Silu).then_inc(conv_out, 1)
        walk(act, "conv", body, skip=2)
        act.wait_ge(conv_out, 6)
        act.activation(dn_sq[:], dn[:, 0:2], ACT.Square).then_inc(qk_squared, 1)

        def z_body(s, slot, r, ahead):
            split_hi(act, s + 2, slot, ahead)
            if r == 0:
                act.wait_ge(acc_free, s + 3)
                act_silu_z(act, 0)
                act.wait_ge(qk_summed, 1)
                act.activation(qk_root[:].rearrange("p w t h -> p (w t h)"), ps[:, NRM, 0:32], ACT.Sqrt,
                               bias=vecs[:, 2:3]).then_inc(qk_rooted, 1)
        walk(act, "z", z_body)

    def act_silu_z(act, r):
        act.activation(dnf[:, 12 + 2 * r:14 + 2 * r, :], prod[:], ACT.Silu).then_inc(conv_out, 1)

    def dve_conv(dve):
        def body(s, slot, r, ahead):
            dve.wait_ge(conv_center, 2 * r + 2)
            for side, (dst, src, tap) in enumerate(((slice(1, SEQ), slice(0, SEQ - 1), 0), (slice(0, SEQ - 1), slice(1, SEQ), 2))):
                for u in range(2):
                    out = prod[:, u, :].rearrange("p (a t) -> p a t", a=2)[:, :, dst]
                    tap_w = conv_w[:, bass.ds(2 * r + u, 1), tap:tap + 1].rearrange("p a b -> p (a b)")
                    last = dve.scalar_tensor_tensor(
                        out=out, in0=ps[:, 2 * slot + u, :].rearrange("p (a t) -> p a t", a=2)[:, :, src],
                        scalar=tap_w, in1=out, op0=ALU.mult, op1=ALU.add)
                if side == 0:
                    order_v.inc(last)
                    order_v.wait_by(dve)
            last.then_inc(acc_free, 1)
            if ahead:
                split_lo(dve, s + 2, slot, ahead)
        walk(dve, "conv", body, tallies=((order_v, 2),))

        def z_body(s, slot, r, ahead):
            dve.wait_ge(step_done, s + 1)
            dve.wait_ge(conv_out, 6 + r)
            dve.tensor_copy(prod[:], ps[:, 2 * slot:2 * slot + 2, :]).then_inc(acc_free, 1)
            split_lo(dve, s + 2, slot, ahead)
            if r == 0:
                dve.wait_ge(qk_rooted, 1)
                dve.reciprocal(qk_inv[:], qk_root[:]).then_inc(qk_inverse, 1)
                dve.wait_ge(qk_inverse, 1)
                order_v.inc(dve.tensor_scalar(qk_inv[:, 0], qk_inv[:, 0], P ** -0.5, None, ALU.mult))
                order_v.wait_by(dve)
        walk(dve, "z", z_body)

    def pe_ab16(pe):
        pe_ready(pe, S_AB)
        products(pe, ps[:, 2 * (S_AB % 2), :], S_AB % 2, 0, KD, lambda k: h_hi[:, k, :], lambda k: h_lo[:, k, :]) \
            .then_inc(step_done, 1)

    def pe_turn_ab16(pe):
        pe.wait_ge(acc_free, S_AB + 3)
        for t in range(NT):
            mm = pe.transpose(ps[:, 7, t * P:(t + 1) * P], sil[:, 1, t * P:(t + 1) * P], ident)
        mm.then_inc(ab_turned, 1)

    def dve_ab16(dve):
        dve.wait_ge(step_done, S_AB + 1)
        dve.tensor_copy(sil[:, 1], ps[:, 2 * (S_AB % 2), :]).then_inc(acc_free, 1)
        split_lo(dve, S_AB + 2, S_AB % 2, ELEMS[S_AB + 2])

    def dve_place_ab16(dve):
        dve.wait_ge(ab_turned, 1)
        dve.tensor_copy(ab_raw[:], ps[:, 7, :].rearrange("p (t n) -> p t n", t=NT)[:, :, 0:16]).then_inc(ab_placed, 1)

    def act_gate_exps(act):
        act_softplus(act, 32, 1)
        act.wait_ge(ab_placed, 1)
        act.activation(ab_tok, gate_in[:, 0, :], ACT.Exp)
        act.activation(g_tmp.rearrange("p (t n) -> p t n", t=NT), ab_raw[:, :, 8:16], ACT.Exp, scale=-1.0) \
           .then_inc(gate_exp, 1)

    def dve_gates(dve):
        dve.wait_ge(ab_placed, 1)
        y = G_Y.rearrange("p (t n) -> p t n", t=NT)
        order_v.inc(dve.tensor_tensor(y, ab_raw[:, :, 0:8], gate_in[:, 1, :].rearrange("p (t n) -> p t n", t=NT), ALU.add))
        order_v.wait_by(dve)
        dve_softplus(dve, G_Y, G_OUT, 32, 1)
        dve.wait_ge(gate_exp, 1)
        dve.scalar_tensor_tensor(out=log_decay, in0=G_OUT, scalar=-1.0, in1=ab_tok, op0=ALU.mult, op1=ALU.mult)
        order_v.inc(dve.tensor_scalar(g_tmp, g_tmp, 1.0, None, ALU.add))
        order_v.wait_by(dve)
        dve.reciprocal(beta, g_tmp).then_inc(gates_ready, 1)

    df_squared, df_summed, df_rooted, df_scaled = (sem(f"df_{n}") for n in ("squared", "summed", "rooted", "scaled"))
    df_turned, df_placed = sem("df_turned"), sem("df_placed")
    df_stat = [small[:, 64 + 16 * n:80 + 16 * n] for n in range(3)]
    df_heads = df_o[:].rearrange("p t h d -> p (t h) d")

    def act_df_norm(act):
        act.wait_ge(attn_out, len(ATTN))
        act.wait_ge(mixed_done, len(ATTN))
        act.activation(df_sq[:], df_heads, ACT.Square).then_inc(df_squared, 1)
        act.wait_ge(df_summed, 1)
        act.activation(df_stat[1], df_stat[0], ACT.Sqrt, bias=vecs[:, 2:3], scale=1.0 / P).then_inc(df_rooted, 1)

    def dve_df_norm(dve):
        dve.wait_ge(df_squared, 1)
        dve.tensor_reduce(df_stat[0], df_sq[:], AX.X, ALU.add).then_inc(df_summed, 1)
        dve.wait_ge(df_rooted, 1)
        order_v.inc(dve.reciprocal(df_stat[2], df_stat[1]))
        order_v.wait_by(dve)
        dve.tensor_tensor(df_heads, df_heads, spread(df_stat[2], P), ALU.mult).then_inc(df_scaled, 1)

    def pe_turn_df(pe):
        pe.wait_ge(df_scaled, 1)
        for t in range(NT):
            if t >= 2:
                pe.wait_ge(df_placed, t - 1)
            else:
                pe.wait_ge(qk_rooted, 1)
            for h in range(DFH):
                mm = pe.transpose(ps[:, (7, 4)[t % 2], h * P:(h + 1) * P], df_o[:, t, h, :], ident)
            mm.then_inc(df_turned, 1)

    def act_turn_df(act):
        for t in range(NT):
            act.wait_ge(df_turned, t + 1)
            act.activation(y_df[:, :, t * P:(t + 1) * P], ps[:, (7, 4)[t % 2], :].rearrange("p (h d) -> p h d", h=4),
                           ACT.Copy, scale=vecs[:, 1:2]).then_inc(df_placed, 1)

    def pe_qk_sums(pe):
        pe.wait_ge(qk_squared, 1)
        for w in range(2):
            for t in range(NT):
                for h in range(DNH):
                    col = 16 * w + 4 * t + h
                    mm = pe.matmul(ps[:, NRM, col:col + 1], dn_sq[:, w, h, t * P:(t + 1) * P], ones[:, 0:1],
                                   start=col == 0, stop=True, skip_group_check=True)
        mm.then_inc(qk_summed, 1)

    def pe_turn_kv(pe):
        pe.wait_ge(acc_free, S_Z_END + 2)
        pe.wait_ge(qk_inverse, 1)
        for t in range(NT):
            tt = slice(t * P, (t + 1) * P)
            if t >= 2:
                pe.wait_ge(k_tok_done, t - 1)
                pe.wait_ge(v_tok_done, t - 1)
            for h in range(DNH):
                mm = pe.transpose(ps[:, t % 2, h * P:(h + 1) * P], dn[:, 1, h, tt], ident)
            mm.then_inc(k_turned, 1)
            for h in range(DNH):
                mm = pe.transpose(ps[:, 2 + t % 2, h * P:(h + 1) * P], dn[:, 2, h, tt], ident)
            mm.then_inc(v_turned_dn, 1)
            if t:
                pe_turn_back(pe, t - 1)
        pe_turn_back(pe, NT - 1)

    def pe_turn_back(pe, t):
        pe.wait_ge(k_tok_done, t + 1)
        if t >= 2:
            pe.wait_ge(k_feat_done, t - 1)
        for h in range(DNH):
            mm = pe.transpose(ps[:, 5 + t % 2, h * P:(h + 1) * P], k_tok[:, t, h, :], ident)
        mm.then_inc(k_back, 1)

    def act_turn_kv(act):
        act_turn_df(act)
        act.dma_start(levels[:], a["levels"]).then_inc(levels_ready, 16)
        for t in range(NT + 1):
            if t < NT:
                act.wait_ge(v_turned_dn, t + 1)
                act.activation(v_tok[:, t].rearrange("p h d -> p (h d)"), ps[:, 2 + t % 2, :], ACT.Copy) \
                   .then_inc(v_tok_done, 1)
            if t:
                act.wait_ge(k_back, t)
                act.activation(dn[:, 1, :, (t - 1) * P:t * P],
                               ps[:, 6 - t % 2, :].rearrange("p (h d) -> p h d", h=4), ACT.Copy).then_inc(k_feat_done, 1)
        act.wait_ge(acc_free, S_Z_END + 2)
        act_silu_z(act, 1)

    def dve_turn_kv(dve):
        for t in range(NT):
            dve.wait_ge(k_turned, t + 1)
            dve.tensor_tensor(k_tok[:, t], ps[:, t % 2, :].rearrange("p (h d) -> p h d", h=4),
                              spread(qk_inv[:, 1, t, :], P), ALU.mult).then_inc(k_tok_done, 1)
        for d in range(2):
            dve.memset(state[d][:], 0.0).then_inc(dn_dve[d], 1)

    inverse = [f"{n}{l}" for l in range(1, LEVELS) for n in ("X", "TU")]
    PE_ST = stages(["G", "KK", "QK", "X0"] + inverse + ["W", "V", "O", "S"])
    ACT_ST = stages(["GC", "EG", "EL", "EC", "DEC", "DC"] + [f"X{l}" for l in range(1, LEVELS)] + ["WN"])
    dve_stages = (["CUT", "DSUB", "SYS", "M0", "U0", "T0", "M1"]
                  + [f"{n}{l + 1 if n == 'M' else l}" for l in range(1, LEVELS - 1) for n in ("M", "T", "U")]
                  + ["KEG", "QE", "KDEC", "U6", "VN", "OUT", "ST"])
    dve_stages.insert(dve_stages.index("U1") + 1, "QKM")
    DVE_COUNT = len(dve_stages)
    DVE_ST = stages(["START"] + dve_stages)
    dn_pe = [sem(f"dn_products{d}") for d in range(2)]
    dn_act = [sem(f"dn_scalar{d}") for d in range(2)]
    dn_dve = [sem(f"dn_vector{d}") for d in range(2)]
    staged = [sem(f"dn_staged{d}") for d in range(2)]
    CUTS, TRIS = (C_CUTF, C_CUTB), (C_TRIF, C_TRIB)
    LAST = (P - 1, 0)

    def need(eng, which, table, d, it, stage):
        eng.wait_ge(which[d], it * (DVE_COUNT if table is DVE_ST else len(table)) + table[stage])

    def chunk(d, stream, b):
        return 2 * stream + (b if d == 0 else 1 - b)

    def heads(buf):
        return buf[:].rearrange("p h d -> p (h d)")

    def joined(ap, l, side):
        return ap.rearrange("p (n s b) -> p n s b", s=2, b=1 << l)[:, :, side, :]

    def bank(n, d):
        return ps[:, 2 * n + d, :]

    def bank4(n, d):
        return bank(n, d).rearrange("p (h d) -> p h d", h=4)

    def pool_deltanet(pool):
        pool.wait_ge(k_feat_done, NT)
        pool.wait_ge(gates_ready, 1)
        for stream in range(2):
            for b in range(2):
                it = 2 * stream + b
                for d in range(2):
                    tt = chunk(d, stream, b)
                    if it:
                        need(pool, dn_pe, PE_ST, d, it - 1, "QK")
                    pool.tensor_copy(k_stage[d][:], dn[:, 1, :, bass.ds(tt * P, P)]).then_inc(staged[d], 1)
                    pool.tensor_copy(la_stage[:, d, :], log_decay[:, bass.ds(tt * 8 + 4 * d, 4)]).then_inc(staged[d], 1)

    def pe_deltanet(pe):
        pe.wait_ge(qk_inverse, 1)
        pe.wait_ge(k_feat_done, NT)
        with pe.Fori(0, 2) as stream:
            for b in range(2):
                it = 2 * stream + b
                for d in range(2):
                    pe.wait_ge(staged[d], 2 * it + 2)
                    for h in range(DNH):
                        pe.matmul(bank(0, d)[:, h * P:(h + 1) * P], la_stage[:, d, h:h + 1].to_broadcast([P, P]),
                                  c_(TRIS[d]), start=True, stop=True)
                    pe.matmul(bank(1, d)[:, 0:4], c_(TRIS[d]), la_stage[:, d, :], start=True, stop=True) \
                      .then_inc(dn_pe[d], 1)
                for d in range(2):
                    need(pe, dn_dve, DVE_ST, d, it, "START")
                    for h in range(DNH):
                        mm = pe.matmul(bank(2, d)[:, h * P:(h + 1) * P], k_stage[d][:, h, :], k_stage[d][:, h, :],
                                       start=True, stop=True)
                    mm.then_inc(dn_pe[d], 1)
                    for h in range(DNH):
                        mm = pe.matmul(bank(3, d)[:, h * P:(h + 1) * P], k_stage[d][:, h, :],
                                       dn[:, 0, h, bass.ds(chunk(d, stream, b) * P, P)], start=True, stop=True)
                    mm.then_inc(dn_pe[d], 1)
                for l in range(LEVELS):
                    for d in range(2):
                        need(pe, dn_dve, DVE_ST, d, it, "M0" if l == 0 else "M1" if l == 1 else f"U{l - 1}")
                        for h in range(DNH):
                            out = bank(0, d)[:, h * P:(h + 1) * P]
                            if l == 0:
                                mm = pe.transpose(out, cut_t[d][:, h, :], ident)
                            else:
                                mm = pe.matmul(out, cut_t[d][:, h, :], inv_n[d][:, h, :], start=True, stop=True)
                        mm.then_inc(dn_pe[d], 1)
                    for d in range(2):
                        if l == 0:
                            continue
                        need(pe, dn_act, ACT_ST, d, it, f"X{l}")
                        for h in range(DNH):
                            if l < LEVELS - 1:
                                pe.matmul(joined(bank4(1, d)[:, h], l, d), inv_t[d][:, h, :],
                                          joined(xbuf[d][:, h], l, d), start=True, stop=True)
                            mm = pe.matmul(joined(bank4(2, d)[:, h], l, 1 - d), xbuf[d][:, h, :],
                                           joined(inv_t[d][:, h], l, 1 - d), start=True, stop=True)
                        mm.then_inc(dn_pe[d], 1)
                for d in range(2):
                    need(pe, dn_dve, DVE_ST, d, it, "U6")
                    for h in range(DNH):
                        mm = pe.matmul(bank(0, d)[:, h * P:(h + 1) * P], inv_n[d][:, h, :], inv_t[d][:, h, :],
                                       start=True, stop=True)
                    mm.then_inc(dn_pe[d], 1)
                for d in range(2):
                    tt = chunk(d, stream, b)
                    need(pe, dn_act, ACT_ST, d, it, "WN")
                    for h in range(DNH):
                        out = bank(1, d)[:, h * P:(h + 1) * P]
                        pe.matmul(out, inv_t[d][:, h, :], v_tok[:, bass.ds(tt, 1), h, :].rearrange("p a d -> p (a d)"),
                                  start=True, stop=False)
                        mm = pe.matmul(out, xbuf[d][:, h, :], state[d][:, h, :], start=False, stop=True)
                    mm.then_inc(dn_pe[d], 1)
                for d in range(2):
                    need(pe, dn_dve, DVE_ST, d, it, "VN")
                    for h in range(DNH):
                        out = bank(2, d)[:, h * P:(h + 1) * P]
                        pe.matmul(out, cut_t[d][:, h, :], state[d][:, h, :], start=True, stop=False)
                        mm = pe.matmul(out, gram_t[d][:, h, :], v_new[d][:, h, :], start=False, stop=True)
                    mm.then_inc(dn_pe[d], 1)
                    for h in range(DNH):
                        mm = pe.matmul(bank(3, d)[:, h * P:(h + 1) * P], sys_t[d][:, h, :], v_new[d][:, h, :],
                                       start=True, stop=True)
                    mm.then_inc(dn_pe[d], 1)

    def act_deltanet(act):
        with act.Fori(0, 2) as stream:
            for b in range(2):
                it = 2 * stream + b
                for d in range(2):
                    s = dsm[:, d]
                    need(act, dn_pe, PE_ST, d, it, "G")
                    need(act, dn_dve, DVE_ST, d, it, "START")
                    act.activation(s[:, 0], bank(1, d)[:, 0:4], ACT.Copy).then_inc(dn_act[d], 1)
                    act.activation(heads(v_new[d]), bank(0, d), ACT.Exp).then_inc(dn_act[d], 1)
                    act.activation(s[:, 4], bank4(0, d)[:, :, LAST[d]], ACT.Exp).then_inc(dn_act[d], 1)
                    need(act, dn_act, ACT_ST, d, it, "GC")
                    act.activation(s[:, 1], s[:, 0], ACT.Exp).then_inc(dn_act[d], 1)
                for d in range(2):
                    s = dsm[:, d]
                    need(act, dn_dve, DVE_ST, d, it, "CUT")
                    act.activation(heads(delta_t[d]), heads(delta_t[d]), ACT.Exp).then_inc(dn_act[d], 1)
                    need(act, dn_dve, DVE_ST, d, it, "DSUB")
                    act.activation(s[:, 3], s[:, 2], ACT.Exp).then_inc(dn_act[d], 1)
                for l in range(1, LEVELS):
                    for d in range(2):
                        need(act, dn_pe, PE_ST, d, it, f"X{l}")
                        act.activation(heads(xbuf[d]), bank(0, d), ACT.Copy).then_inc(dn_act[d], 1)
                for d in range(2):
                    need(act, dn_pe, PE_ST, d, it, "W")
                    act.activation(heads(xbuf[d]), bank(0, d), ACT.Copy, scale=-1.0).then_inc(dn_act[d], 1)

    def dve_deltanet(dve):
        dve.wait_ge(levels_ready, 16)
        with dve.Fori(0, 2) as stream:
            for b in range(2):
                it = 2 * stream + b

                def beta_of(d, h):
                    return beta[:, bass.ds(chunk(d, stream, b) * 8 + 4 * d + h, 1)]

                for d in range(2):
                    s = dsm[:, d]
                    need(dve, dn_act, ACT_ST, d, it, "EL")
                    for h in range(DNH):
                        last = dve.scalar_tensor_tensor(out=delta_t[d][:, h, :], in0=bank4(0, d)[:, h, :],
                                                        scalar=s[:, 0, h:h + 1], in1=c_(CUTS[d]),
                                                        op0=ALU.subtract, op1=ALU.min)
                    last.then_inc(dn_dve[d], 1)
                    dve.tensor_tensor(s[:, 2], bank4(0, d)[:, :, LAST[d]], s[:, 0], ALU.subtract).then_inc(dn_dve[d], 1)
                for d in range(2):
                    need(dve, dn_act, ACT_ST, d, it, "DEC")
                    need(dve, dn_pe, PE_ST, d, it, "KK")
                    for h in range(DNH):
                        last = dve.scalar_tensor_tensor(out=sys_t[d][:, h, :], in0=bank4(2, d)[:, h, :],
                                                        scalar=beta_of(d, h), in1=delta_t[d][:, h, :],
                                                        op0=ALU.mult, op1=ALU.mult)
                    last.then_inc(dn_dve[d], 1)
                    need(dve, dn_dve, DVE_ST, d, it, "SYS")
                    dve_mask(dve, d, 0)
                    need(dve, dn_dve, DVE_ST, d, it, "M0")
                    dve.tensor_tensor(inv_t[d][:], over(ident, 4), cut_t[d][:], ALU.subtract).then_inc(dn_dve[d], 1)
                    need(dve, dn_pe, PE_ST, d, it, "X0")
                    dve.tensor_tensor(inv_n[d][:], over(ident, 4), bank4(0, d), ALU.subtract).then_inc(dn_dve[d], 1)
                    need(dve, dn_dve, DVE_ST, d, it, "U0")
                    dve_mask(dve, d, 1)
                for l in range(1, LEVELS - 1):
                    for d in range(2):
                        need(dve, dn_pe, PE_ST, d, it, f"X{l}")
                        dve_mask(dve, d, l + 1)
                    for d in range(2):
                        need(dve, dn_pe, PE_ST, d, it, f"TU{l}")
                        n, t = joined(heads(inv_n[d]), l, d), joined(heads(inv_t[d]), l, 1 - d)
                        dve.tensor_tensor(n, n, joined(bank(1, d), l, d), ALU.subtract).then_inc(dn_dve[d], 1)
                        dve.tensor_tensor(t, t, joined(bank(2, d), l, 1 - d), ALU.subtract).then_inc(dn_dve[d], 1)
                        if l == 1:
                            need(dve, dn_pe, PE_ST, d, it, "QK")
                            dve.tensor_tensor(heads(gram_t[d]), bank(3, d), heads(delta_t[d]), ALU.mult) \
                               .then_inc(dn_dve[d], 1)
                for d in range(2):
                    s, tt = dsm[:, d], chunk(d, stream, b)
                    kt = k_tok[:, bass.ds(tt, 1)].rearrange("p a h d -> p (a h) d")
                    need(dve, dn_pe, PE_ST, d, it, "X6")
                    need(dve, dn_act, ACT_ST, d, it, "DC")
                    dve.tensor_tensor(inv_n[d][:], kt, spread(s[:, 1], P), ALU.mult).then_inc(dn_dve[d], 1)
                    dve.tensor_tensor(cut_t[d][:], dn[:, 0, :, bass.ds(tt * P, P)], v_new[d][:], ALU.mult) \
                       .then_inc(dn_dve[d], 1)
                    dve.tensor_tensor(sys_t[d][:], kt, spread(s[:, 3], P), ALU.mult).then_inc(dn_dve[d], 1)
                    need(dve, dn_pe, PE_ST, d, it, "TU6")
                    t = joined(heads(inv_t[d]), LEVELS - 1, 1 - d)
                    dve.tensor_tensor(t, t, joined(bank(2, d), LEVELS - 1, 1 - d), ALU.subtract).then_inc(dn_dve[d], 1)
                for d in range(2):
                    tt = chunk(d, stream, b)
                    need(dve, dn_pe, PE_ST, d, it, "V")
                    dve.tensor_tensor(v_new[d][:], bank4(1, d), spread(beta[:, bass.ds(tt * 8 + 4 * d, 4)], P),
                                      ALU.mult).then_inc(dn_dve[d], 1)
                for d in range(2):
                    tt = chunk(d, stream, b)
                    o = dn_o[:, bass.ds(tt, 1)].rearrange("p a h d -> p (a h) d")
                    need(dve, dn_pe, PE_ST, d, it, "O")
                    if b == 0:
                        dve.tensor_copy(o, bank4(2, d)).then_inc(dn_dve[d], 1)
                    else:
                        need(dve, dn_dve, DVE_ST, 1 - d, it - 1, "OUT")
                        dve.tensor_tensor(o, o, bank4(2, d), ALU.add).then_inc(dn_dve[d], 1)
                    need(dve, dn_pe, PE_ST, d, it, "S")
                    for h in range(DNH):
                        last = dve.scalar_tensor_tensor(out=state[d][:, h, :], in0=state[d][:, h, :],
                                                        scalar=dsm[:, d, 4, h:h + 1], in1=bank4(3, d)[:, h, :],
                                                        op0=ALU.mult, op1=ALU.add)
                    last.then_inc(dn_dve[d], 1)

    def dve_mask(dve, d, l):
        m = levels[:, (d * LEVELS + l) * P:(d * LEVELS + l + 1) * P]
        dve.tensor_tensor(cut_t[d][:], sys_t[d][:], over(m, 4), ALU.mult).then_inc(dn_dve[d], 1)

    o_squared, o_summed, o_rooted, o_scaled = (sem(f"dn_out_{n}") for n in ("squared", "summed", "rooted", "scaled"))
    o_turned, o_gated = sem("dn_out_turned"), sem("dn_out_gated")
    y_hi_done, y_lo_done = sem("y_hi_done"), sem("y_lo_done")
    o_heads = dn_o[:].rearrange("p t h d -> p (t h) d")
    o_stat = [small[:, 112 + 16 * n:128 + 16 * n] for n in range(3)]
    q_scale = qk_inv[:, 0].rearrange("p t h -> p (t h)")

    def deltanet_done(eng):
        for d in range(2):
            eng.wait_ge(dn_dve[d], 4 * DVE_COUNT + 1)

    def y_chunk(c):
        return y_df[:, c, :] if c < DFH else y_dn[:, c - DFH, :]

    def act_merge(act):
        act.activation(warm_root[:], vecs[:, 2:3], ACT.Sqrt).then_inc(warmed, 1)
        deltanet_done(act)

        def split(c):
            act.activation(h_hi[:, c, :], y_chunk(c), ACT.Copy).then_inc(y_hi_done, 1)
        for half in range(2):
            hh = slice(8 * half, 8 * half + 8)
            act.activation(o_sq[:, hh], o_heads[:, hh], ACT.Square).then_inc(o_squared, 1)
            split(half)
        act.wait_ge(o_summed, 2)
        act.activation(o_stat[1], o_stat[0], ACT.Sqrt, bias=vecs[:, 2:3], scale=1.0 / P).then_inc(o_rooted, 1)
        split(2)
        split(3)
        act.wait_ge(o_gated, NT)
        for c in range(DFH, KD):
            split(c)

    def dve_merge(dve):
        deltanet_done(dve)

        def split(c):
            dve.wait_ge(y_hi_done, c + 1)
            dve.tensor_tensor(h_lo[:, c, :], y_chunk(c), h_hi[:, c, :].bitcast(F32), ALU.subtract).then_inc(y_lo_done, 1)

        order_v.inc(dve.tensor_tensor(o_stat[2], q_scale, q_scale, ALU.mult))
        for half in range(2):
            hh = slice(8 * half, 8 * half + 8)
            dve.wait_ge(o_squared, half + 1)
            order_v.inc(dve.tensor_reduce(o_stat[0][:, hh], o_sq[:, hh], AX.X, ALU.add))
            order_v.wait_by(dve)
            dve.tensor_tensor(o_stat[0][:, hh], o_stat[0][:, hh], o_stat[2][:, hh], ALU.mult).then_inc(o_summed, 1)
            split(half)
        dve.wait_ge(o_rooted, 1)
        order_v.inc(dve.reciprocal(o_stat[2], o_stat[1]))
        order_v.wait_by(dve)
        order_v.inc(dve.tensor_tensor(o_stat[2], o_stat[2], q_scale, ALU.mult))
        order_v.wait_by(dve)
        for half in range(2):
            hh = slice(8 * half, 8 * half + 8)
            dve.tensor_tensor(o_heads[:, hh], o_heads[:, hh], spread(o_stat[2][:, hh], P), ALU.mult).then_inc(o_scaled, 1)
        split(2)
        split(3)
        for t in range(NT):
            dve.wait_ge(o_turned, t + 1)
            dve.scalar_tensor_tensor(out=y_dn[:, :, t * P:(t + 1) * P],
                                     in0=ps[:, 4 + t, :].rearrange("p (h d) -> p h d", h=4),
                                     scalar=vecs[:, 0:1], in1=dn[:, 3, :, t * P:(t + 1) * P],
                                     op0=ALU.mult, op1=ALU.mult).then_inc(o_gated, 1)
        dve.wait_ge(o_gated, NT)
        for c in range(DFH, KD):
            split(c)

    def pe_merge(pe):
        for t in range(NT):
            pe.wait_ge(o_scaled, t // 2 + 1)
            for h in range(DNH):
                mm = pe.transpose(ps[:, 4 + t, h * P:(h + 1) * P], dn_o[:, t, h, :], ident)
            mm.then_inc(o_turned, 1)

    def pe_ab(pe):
        def diff_body(s, slot, r):
            pair_products(pe, s, slot, ALL, "n01" if r == 0 else None)
            if r >= 4:
                pe_rotate_diff(pe, 2 * r - 8)
                pe_rotate_diff(pe, 2 * r - 7)
        for r in range(R["diff"][2]):
            diff_body(R["diff"][1] + r, (R["diff"][1] + r) % 2, r)
        pe_ab16(pe)
        pe_diff(pe)
        pe_pairs(pe, "conv", ALL)

        def z_body(s, slot, r, ahead):
            pair_products(pe, s, slot, ALL)
            if r == 0:
                pe_qk_sums(pe)
        walk(pe, "z", z_body)
        pe_turn_df(pe)
        pe_turn_kv(pe)
        pe_deltanet(pe)

    def act_ab(act):
        act_plain(act, "diff")
        act_plain(act, "ab")
        act_diff(act)
        act_gate_exps(act)
        act_df_norm(act)
        act_conv(act)
        act_turn_kv(act)
        act_deltanet(act)
        act_merge(act)

    def dve_ab(dve):
        def body(s, slot, r, ahead):
            dve.wait_ge(step_done, s + 1)
            dve.tensor_copy(df[:, bass.ds(2 * r, 2), :], ps[:, 2 * slot:2 * slot + 2, :]).then_inc(acc_free, 1)
            if ahead:
                split_lo(dve, s + 2, slot, ahead)
            if isinstance(r, int) and r >= 4:
                dve_rope_diff(dve, 2 * r - 8)
                dve_rope_diff(dve, 2 * r - 7)
        walk(dve, "diff", body)
        dve_lambda(dve)
        dve_ab16(dve)
        dve_diff(dve)
        dve_gates(dve)
        dve_df_norm(dve)
        dve_conv(dve)
        dve_turn_kv(dve)
        dve_deltanet(dve)
        dve_merge(dve)

    rcopied, rrot, rroped = sem("ret_copied"), sem("ret_rotated"), sem("ret_roped")
    v_turned, v_placed = sem("ret_v_turned"), sem("ret_v_placed")
    g_placed = sem("ret_g_placed")
    tables_ready, decays_ready = sem("tables_ready"), sem("decays_ready")
    lg, _ = put("lg", [P, 32])
    rs, _ = put("rs", [P, 2, 6])
    r_staged, r_exps, r_decayed = sem("ret_staged"), sem("ret_exps"), sem("ret_decayed")
    r_scores, r_weighed, r_mixed = sem("ret_scores"), sem("ret_weighed"), sem("ret_mixed")
    r_squared, r_rooted, r_inverse, r_scaled = (sem(f"ret_{n}") for n in ("squared", "rooted", "inverse", "scaled"))
    r_turned, r_gated, r_hi, r_lo = (sem(f"ret_{n}") for n in ("turned", "gated", "hi", "lo"))
    r_halves = sem("ret_halves")
    LEAD, LAG = 1, 2

    def head_slots(eng, body):
        def straight(h):
            body(h, h % 2, lambda g: 0 <= h + g < RH)
        for h in range(-LEAD, LAG):
            straight(h)
        with eng.Fori(0, (RH - LEAD - LAG) // 2) as i:
            for b in range(2):
                body(2 * i + LAG + b, b, lambda g: True)
        for h in range(LAG + (RH - LEAD - LAG) // 2 * 2, RH + LAG):
            straight(h)

    sil2 = [sil[:, i, :].rearrange("p (a t) -> p a t", a=2) for i in range(2)]
    prod2 = [prod[:, i, :].rearrange("p (a t) -> p a t", a=2) for i in range(2)]
    S_RG = R["retg"][1]
    COS_R, SIN_R = rc[:, 10 * SEQ:11 * SEQ], rc[:, 11 * SEQ:12 * SEQ]

    def pool_retention(pool):
        pool.wait_ge(ada_dot, 2 * NADA)
        pool.dma_start(rc[:], a["ret_tables"]).then_inc(tables_ready, 16)
        pool.wait_ge(rroped, 8)
        pool.wait_ge(step_done, S_RG + 8)
        with pool.Fori(0, RH // 2) as i:
            for b in range(2):
                pool.tensor_copy(r_kst[b][:], rk[:, bass.ds(2 * i + b, 1), :].rearrange("p a t -> p (a t)")) \
                    .then_inc(r_staged, 1)
            pool.wait_ge(r_scores, 2 * i + 2)

    def pe_rotate(pe, s, slot, r):
        pe.wait_ge(acc_free, s + 3)
        pe.matmul(ps[:, 5 + slot, :], c_(C_ROTR), sil[:, slot, :], start=True, stop=True).then_inc(rrot, 1)

    def pe_ret(pe):
        def lagged(name, cols, follow):
            s0, n = R[name][1], R[name][2]

            def body(s, slot, r, ahead):
                pair_products(pe, s, slot, cols, "n11" if name == "retq" and isinstance(r, int) and r == 0 else None)
                if not (isinstance(r, int) and r == 0):
                    follow(s - 1, 1 - slot, r - 1)
            walk(pe, name, body, skip=2)
            follow(s0 + n - 1, (s0 + n - 1) % 2, n - 1)

        lagged("retq", LAT, lambda s, slot, r: pe_rotate(pe, s, slot, r))
        lagged("retk", ALL, lambda s, slot, r: pe_rotate(pe, s, slot, r))

        def turn_v(s, slot, r):
            pe.wait_ge(acc_free, s + 3)
            if not (isinstance(r, int) and r == 0):
                pe.wait_ge(v_placed, r)
            else:
                pe.wait_ge(rroped, 8)
            for u in range(2):
                for t in range(NT):
                    mm = pe.transpose(ps[:, 5 + t // 2, (t % 2) * 256 + u * P:(t % 2) * 256 + (u + 1) * P],
                                      sil[:, u, t * P:(t + 1) * P], ident)
            mm.then_inc(v_turned, 1)
        lagged("retv", ALL, turn_v)
        pe_pairs(pe, "retg", LAT)
        pe.wait_ge(acc_free, S_RG + 8 + 2)

        def body(h, b, has):
            if has(1):
                pe.wait_ge(r_staged, h + 2)
                if has(-1):
                    pe.wait_ge(r_weighed, h)
                for kt in range(NT):
                    mm = pe.matmul(ps[:, 2 * (1 - b) + kt // 2, (kt % 2) * 256:(kt % 2 + 1) * 256],
                                   r_kst[1 - b][:, kt * P:(kt + 1) * P],
                                   rq[:, bass.ds(h + 1, 1), :].rearrange("p a t -> p (a t)"), start=True, stop=True)
                mm.then_inc(r_scores, 1)
            if has(0):
                pe.wait_ge(r_weighed, h + 1)
                if has(-2):
                    pe.wait_ge(r_scaled, h - 1)
                for qt in range(2):
                    for kt in range(NT):
                        mm = pe.matmul(ps[:, 4 + b, qt * 256:(qt + 1) * 256],
                                       r_probs[b][:, kt * 256 + qt * P:kt * 256 + (qt + 1) * P],
                                       rv[:, kt, bass.ds(h * 256, 256)], start=kt == 0, stop=kt == NT - 1)
                mm.then_inc(r_mixed, 1)
            if has(-1):
                pe.wait_ge(r_scaled, h)
                for f in range(2):
                    for qt in range(2):
                        mm = pe.transpose(ps[:, 7 - b, f * 256 + qt * P:f * 256 + (qt + 1) * P],
                                          prod[:, 1 - b, qt * 256 + f * P:qt * 256 + (f + 1) * P], ident)
                mm.then_inc(r_turned, 1)
        head_slots(pe, body)

    def act_ret(act):
        act_plain(act, "retq")
        act_plain(act, "retk")
        act_softplus(act, 16, 2)

        def v_body(s, slot, r, ahead):
            if ahead:
                split_hi(act, s + 2, slot, ahead)
            if not (isinstance(r, int) and r == 0):
                place_v(r - 1)

        def place_v(r):
            act.wait_ge(v_turned, r + 1)
            act.activation(rv[:, :, bass.ds(r * 256, 256)],
                           ps[:, 5:7, :].rearrange("p b (t n) -> p (b t) n", t=2), ACT.Copy).then_inc(v_placed, 1)
        walk(act, "retv", v_body, skip=2)
        place_v(7)

        def g_body(s, slot, r, ahead):
            if ahead:
                split_hi(act, s + 2, slot, ahead)
            act.wait_ge(acc_free, s + 3)
            act.activation(rg[:, bass.ds(2 * r, 2), :], sil2[0 if slot == S_RG % 2 else 1], ACT.Silu) \
               .then_inc(g_placed, 1)
        walk(act, "retg", g_body)
        act.wait_ge(decays_ready, 1)
        act.wait_ge(tables_ready, 16)

        def body(h, b, has):
            if has(1):
                if has(-1):
                    act.wait_ge(r_weighed, h)
                lf, lb = lg[:, bass.ds(h + 1, 1)], lg[:, bass.ds(9 + h, 1)]
                dec, back = r_decay[1 - b], r_back[1 - b]
                act.activation(dec[:, 512:1024], rc[:, 0:512], ACT.Exp, scale=lf)
                act.activation(back[:, 512:1024], rc[:, 0:512], ACT.Exp, scale=lb).then_inc(r_exps, 1)
                act.activation(dec[:, 0:512], rc[:, 1536:2048], ACT.Exp, scale=lf)
                act.activation(back[:, 0:512], rc[:, 2048:2560], ACT.Exp, scale=lb).then_inc(r_exps, 1)
            if has(-2):
                act.wait_ge(r_gated, h - 1)
                act.activation(ry_hi[:, bass.ds(2 * h - 4, 2), :], sil2[b], ACT.Copy).then_inc(r_hi, 1)
            if has(0):
                act.wait_ge(r_mixed, h + 1)
                if has(-1):
                    act.wait_ge(r_squared, h)
                if has(-2):
                    act.wait_ge(r_inverse, h - 1)
                for qt in range(2):
                    last = act.activation(r_square[:, qt * 256:(qt + 1) * 256], ps[:, 4 + b, qt * 256:(qt + 1) * 256],
                                          ACT.Square, accum_out=rs[:, b, qt:qt + 1])
                last.then_inc(r_squared, 1)
                act.wait_ge(r_squared, h + 1)
                act.activation(rs[:, b, 2:4], rs[:, b, 0:2], ACT.Sqrt, bias=vecs[:, 2:3], scale=1.0 / 256) \
                   .then_inc(r_rooted, 1)
        head_slots(act, body)

    def dve_ret(dve):
        def rope(r, slot, out, total):
            dve.wait_ge(rrot, total + r + 1)
            dve.tensor_tensor(prod2[slot], ps[:, 5 + slot, :].rearrange("p (a t) -> p a t", a=2), over(SIN_R, 2), ALU.mult)
            order_v.inc(dve.tensor_tensor(out, sil2[slot], over(COS_R, 2), ALU.mult))
            order_v.wait_by(dve)
            dve.tensor_tensor(out, out, prod2[slot], ALU.add).then_inc(rroped, 1)

        def q_out(r):
            return rq[:, bass.ds(2 * r, 2), :]

        def k_out(r):
            return rk[:, bass.ds(2 * r, 2), LAT]

        dve.wait_ge(tables_ready, 16)
        for name, out, total in (("retq", q_out, 0), ("retk", k_out, 4)):
            s0, n = R[name][1], R[name][2]

            def body(s, slot, r, ahead):
                dve.wait_ge(step_done, s + 1)
                if name == "retk":
                    dve.tensor_copy(rk[:, bass.ds(2 * r, 2), CTX], ps[:, 2 * slot:2 * slot + 2, CTX])
                dve.tensor_copy(sil2[slot], ps[:, 2 * slot:2 * slot + 2, LAT]).then_inc(acc_free, 1)
                if ahead:
                    split_lo(dve, s + 2, slot, ahead)
                if r >= 1:
                    rope(r - 1, 1 - slot, out(r - 1), total)
            for r in range(n):
                s = s0 + r
                body(s, s % 2, r, ELEMS[s + 2])
            rope(n - 1, (s0 + n - 1) % 2, out(n - 1), total)

        order_v.inc(dve.tensor_scalar(G_Y[:, 0:16], small[:, 0:16], -1.0, None, ALU.mult))
        order_v.wait_by(dve)
        dve_softplus(dve, G_Y[:, 0:16], lg[:, 16:32], 16, 2)
        dve.tensor_scalar(lg[:, 0:16], lg[:, 16:32], -1.0, None, ALU.mult).then_inc(decays_ready, 1)

        def v_body(s, slot, r, ahead):
            dve.wait_ge(step_done, s + 1)
            if not (isinstance(r, int) and r == 0):
                dve.wait_ge(v_turned, r)
            else:
                dve.wait_ge(rroped, 8)
            dve.tensor_copy(sil[:], ps[:, 2 * slot:2 * slot + 2, :]).then_inc(acc_free, 1)
            if ahead:
                split_lo(dve, s + 2, slot, ahead)
        walk(dve, "retv", v_body, skip=2)

        def g_body(s, slot, r, ahead):
            dve.wait_ge(step_done, s + 1)
            if isinstance(r, int) and r == 0:
                dve.wait_ge(v_turned, 8)
            if not (isinstance(r, int) and r < 2):
                dve.wait_ge(g_placed, r - 1)
            dve.tensor_copy(sil2[0 if slot == S_RG % 2 else 1], ps[:, 2 * slot:2 * slot + 2, LAT]).then_inc(acc_free, 1)
            if ahead:
                split_lo(dve, s + 2, slot, ahead)
        walk(dve, "retg", g_body, skip=2)

        def body(h, b, has):
            if has(-1):
                r = rs[:, 1 - b]
                dve.wait_ge(r_rooted, h)
                dve.reciprocal(r[:, 4:6], r[:, 2:4]).then_inc(r_inverse, 1)
                dve.wait_ge(r_inverse, h)
                for qt in range(2):
                    last = dve.tensor_scalar(prod[:, 1 - b, qt * 256:(qt + 1) * 256],
                                             ps[:, 5 - b, qt * 256:(qt + 1) * 256], r[:, 4 + qt:5 + qt], None, ALU.mult)
                last.then_inc(r_scaled, 1)
            if has(-2):
                dve.wait_ge(r_turned, h - 1)
                dve.tensor_tensor(sil2[b], ps[:, 6 + b, :].rearrange("p (a t) -> p a t", a=2),
                                  rg[:, bass.ds(2 * h - 4, 2), :], ALU.mult).then_inc(r_gated, 1)
            if has(1):
                dec, back = r_decay[1 - b], r_back[1 - b]
                dve.wait_ge(r_exps, 2 * h + 3)
                dve.tensor_tensor(dec[:, 512:1024], dec[:, 512:1024], rc[:, 512:1024], ALU.mult)
                dve.tensor_tensor(back[:, 512:1024], back[:, 512:1024], rc[:, 1024:1536], ALU.mult) \
                   .then_inc(r_halves, 1)
                dve.wait_ge(r_exps, 2 * h + 4)
                dve.wait_ge(r_halves, h + 2)
                dve.tensor_tensor(dec[:], dec[:], back[:], ALU.add).then_inc(r_decayed, 1)
                dve.wait_ge(r_decayed, h + 2)
                dve.wait_ge(r_scores, h + 2)
                if has(-1):
                    dve.wait_ge(r_mixed, h)
                dve.scalar_tensor_tensor(out=r_probs[1 - b][:],
                                         in0=ps[:, 2 - 2 * b:4 - 2 * b, :].rearrange("p b t -> p (b t)"),
                                         scalar=P ** -0.5, in1=dec[:], op0=ALU.mult, op1=ALU.mult) \
                   .then_inc(r_weighed, 1)
            if has(-2):
                dve.wait_ge(r_hi, h - 1)
                dve.tensor_tensor(ry_lo[:, bass.ds(2 * h - 4, 2), :], sil2[b],
                                  ry_hi[:, bass.ds(2 * h - 4, 2), :].bitcast(F32), ALU.subtract).then_inc(r_lo, 1)
        head_slots(dve, body)

    with nc.Block() as block:
        @block.sync
        def _(sp):
            sp_program(sp)

        @block.gpsimd
        def _(pool):
            pool_program(pool)

        @block.scalar
        def _(act):
            scalar_program(act)

        @block.vector
        def _(dve):
            vector_program(dve)

        @block.tensor
        def _(pe):
            tensor_program(pe)


def lay_out(x, c, ctx, c_ctx, ada_w, ada_b, norm_w, final_norm_w, ffn_w_in, ffn_w_out, ab_w_in, ab_conv_w,
            dn_A_log, dn_dt_bias, dn_norm_w, diff_lambda, diff_subln_w, ab_w_out, ret_w_in, ret_decay_logit,
            ret_w_out):
    def columns(w, n):
        k = w.shape[0] // P
        return w.reshape(k, P, n, P).transpose(2, 1, 0, 3).reshape(n, P, k * P)

    def pairs(w, n):
        return columns(w, n).reshape(n // 2, 2, P, -1).transpose(0, 2, 1, 3).reshape(n // 2, P, -1)

    const, levels, ret = constants()
    tokens = np.concatenate([ctx[0], x[0]], axis=0)
    w = ab_w_in[0]
    return {
        "xT": tokens.T.reshape(KD, P, T).transpose(1, 0, 2),
        "c": c, "c_ctx": c_ctx,
        "ada": np.delete(ada_w.transpose(0, 2, 1).reshape(NADA, P, D), slice(KD, 2 * KD), axis=0),
        "ada0": ada_w[0, :, D:2 * D].reshape(KD, P, D),
        "c_cols": np.stack([c_ctx.reshape(KD, P), c.reshape(KD, P)], axis=-1).transpose(1, 0, 2).reshape(P, 2 * KD),
        "mbias": ada_b.reshape(NADA, P).T,
        "norm_g": np.concatenate([norm_w.reshape(6, D), final_norm_w[None]]).reshape(7, KD, P).transpose(2, 0, 1),
        "w_up": ffn_w_in.reshape(4, KD, P, 2, NF, P).transpose(0, 4, 2, 3, 1, 5).reshape(4, NF, P, 2 * D),
        "w_down": ffn_w_out.reshape(4, NF, P, KD, P).transpose(0, 3, 2, 1, 4).reshape(4, KD, P, FF),
        "w_ab": np.concatenate([pairs(w[:, 2064:3600], 12), pairs(w[:, 0:2048], 16)]),
        "w_ab16": columns(np.pad(w[:, 2048:2064], ((0, 0), (0, P - 16))), 1)[0],
        "w_ab_out": columns(np.concatenate([ab_w_out[0][512:], ab_w_out[0][:512]]), KD),
        "w_ret": pairs(ret_w_in[0], 48),
        "w_ret_out": columns(ret_w_out[0], KD),
        "conv_w": ab_conv_w[0].reshape(3, 12, P).transpose(2, 1, 0),
        "dn_norm": dn_norm_w.reshape(P, 1), "subln": diff_subln_w.reshape(P, 1),
        "a_log": np.tile(dn_A_log.reshape(1, 8), (1, NT)), "dt_bias": np.tile(dn_dt_bias.reshape(1, 8), (1, NT)),
        "ret_decay": ret_decay_logit.reshape(1, 16), "lam": diff_lambda.reshape(1, 256),
        "const": const, "levels": levels, "ret_tables": ret,
    }


def kernel(**inputs):
    from concourse import bacc
    from concourse.bass_utils import run_bass_kernel_spmd

    arrays = {k: np.ascontiguousarray(v) for k, v in lay_out(**{k: np.asarray(v) for k, v in inputs.items()}).items()}
    nc = bacc.Bacc("TRN2", target_bir_lowering=False, num_devices=1)
    aps = {}
    for name, v in arrays.items():
        aps[name] = nc.dram_tensor(f"in_{name}", v.shape, mybir.dt.from_np(v.dtype), kind="ExternalInput").ap()
    aps["out"] = nc.dram_tensor("out_y", (P, KD, SEQ), F32, kind="ExternalOutput").ap()
    build(nc, aps)
    r = run_bass_kernel_spmd(nc, [{f"in_{k}": v for k, v in arrays.items()}], core_ids=[0])
    got = r.results[0]["out_y"]
    return got.transpose(2, 1, 0).reshape(1, SEQ, D)
```
